# Optimizing a Trainium2 kernel written in Bass

```python
import math
import jax, jax.numpy as jnp
from jax import lax
import numpy as np

D_MODEL = 1024
BATCH = 1
SEQ = 256
DEPTH = 2

N_MIXERS = 4
EPS = 1e-6
Q_BLOCK = 128
CHUNK = 128

MLA_HEADS = 8
MLA_NOPE = 128
MLA_ROPE = 64
MLA_V = 128
MLA_Q_LORA = 384
MLA_KV_LORA = 256
ROPE_THETA = 10000.0

DIFF_HEADS = 8
DIFF_HD = D_MODEL // (2 * DIFF_HEADS)

MLSTM_HEADS = 8
MLSTM_QK = D_MODEL // 2 // MLSTM_HEADS
MLSTM_V = D_MODEL // MLSTM_HEADS

RET_HEADS = D_MODEL // 256
RET_QK = 256
RET_V = 2 * D_MODEL // RET_HEADS

FFN_HIDDEN = 2816
CONV_W = 3


def n_of(kind):
    return len(range(kind, DEPTH, N_MIXERS))

def rms_norm(x, g):
    xf = x.astype(jnp.float32)
    y = xf * lax.rsqrt(jnp.mean(xf * xf, -1, keepdims=True) + EPS)
    return (y * g.astype(jnp.float32)).astype(x.dtype)

def head_group_norm(x, g):
    xf = x.astype(jnp.float32)
    mu = jnp.mean(xf, -1, keepdims=True)
    xc = xf - mu
    y = xc * lax.rsqrt(jnp.mean(xc * xc, -1, keepdims=True) + EPS)
    return (y * g.astype(jnp.float32)).astype(x.dtype)

def query_blocks(t):
    b, s = t.shape[:2]
    return jnp.moveaxis(t.reshape(b, s // Q_BLOCK, Q_BLOCK, *t.shape[2:]), 1, 0)

def merge_blocks(t):
    t = jnp.moveaxis(t, 0, 1)
    return t.reshape(t.shape[0], -1, *t.shape[3:])

def rope_cos_sin(s, dim):
    inv = ROPE_THETA ** (-jnp.arange(0, dim, 2, dtype=jnp.float32) / dim)
    ang = jnp.arange(s, dtype=jnp.float32)[:, None] * inv[None, :]
    return jnp.cos(ang), jnp.sin(ang)

def apply_rope(x, cos, sin):
    half = x.shape[-1] // 2
    x1, x2 = x[..., :half], x[..., half:]
    cos = cos.astype(x.dtype)
    sin = sin.astype(x.dtype)
    return jnp.concatenate([x1 * cos - x2 * sin, x1 * sin + x2 * cos], -1)

def to_chunks(t):
    b, s = t.shape[:2]
    t = t.reshape(b, s // CHUNK, CHUNK, *t.shape[2:])
    return jnp.moveaxis(jnp.moveaxis(t, 1, 0), 3, 2)

def from_chunks(t):
    t = jnp.moveaxis(jnp.moveaxis(t, 2, 3), 0, 1)
    return t.reshape(t.shape[0], -1, *t.shape[3:])

def mla_mixer(x, w_dq, q_norm_g, w_uq, w_dkv, kv_norm_g, w_ukv, w_o):
    b, s, _ = x.shape
    H = MLA_HEADS
    cq = rms_norm(x @ w_dq, q_norm_g)
    q = (cq @ w_uq).reshape(b, s, H, MLA_NOPE + MLA_ROPE)
    ckv_kr = x @ w_dkv
    ckv = rms_norm(ckv_kr[..., :MLA_KV_LORA], kv_norm_g)
    kv = (ckv @ w_ukv).reshape(b, s, H, MLA_NOPE + MLA_V)
    k_nope, v = kv[..., :MLA_NOPE], kv[..., MLA_NOPE:]
    cos, sin = rope_cos_sin(s, MLA_ROPE)
    q_nope = q[..., :MLA_NOPE]
    q_rope = apply_rope(q[..., MLA_NOPE:], cos[:, None, :], sin[:, None, :])
    k_rope = apply_rope(ckv_kr[..., MLA_KV_LORA:], cos, sin)
    scale = (MLA_NOPE + MLA_ROPE) ** -0.5

    def block(args):
        qn, qr = args
        sc = (jnp.einsum('bqhd,bkhd->bhqk', qn, k_nope).astype(jnp.float32)
              + jnp.einsum('bqhr,bkr->bhqk', qr, k_rope).astype(jnp.float32)) * scale
        p = jax.nn.softmax(sc, -1).astype(v.dtype)
        return jnp.einsum('bhqk,bkhd->bqhd', p, v)

    o = merge_blocks(lax.map(block, (query_blocks(q_nope), query_blocks(q_rope))))
    return o.reshape(b, s, H * MLA_V) @ w_o

def diff_mixer(x, w_qkv, lam_p, subln_g, w_o, layer_idx):
    b, s, _ = x.shape
    H, d = DIFF_HEADS, DIFF_HD
    qkv = x @ w_qkv
    q = qkv[..., :2 * H * d].reshape(b, s, H, 2, d)
    k = qkv[..., 2 * H * d:4 * H * d].reshape(b, s, H, 2, d)
    v = qkv[..., 4 * H * d:].reshape(b, s, H, 2 * d)
    lam_init = 0.8 - 0.6 * math.exp(-0.3 * layer_idx)
    lp = lam_p.astype(jnp.float32)
    lam = jnp.exp(jnp.sum(lp[0] * lp[1])) - jnp.exp(jnp.sum(lp[2] * lp[3])) + lam_init
    slopes = 2.0 ** (-8.0 * jnp.arange(1, H + 1, dtype=jnp.float32) / H)
    pos = jnp.arange(s, dtype=jnp.int32)
    scale = d ** -0.5

    def block(args):
        qb, qpos = args
        sc = jnp.einsum('bqhjd,bkhjd->bhjqk', qb, k).astype(jnp.float32) * scale
        dist = jnp.abs(qpos[:, None] - pos[None, :]).astype(jnp.float32)
        sc = sc - slopes[None, :, None, None, None] * dist[None, None, None]
        p = jax.nn.softmax(sc, -1)
        a = (p[:, :, 0] - lam * p[:, :, 1]).astype(v.dtype)
        return jnp.einsum('bhqk,bkhd->bqhd', a, v)

    o = merge_blocks(lax.map(block, (query_blocks(q), pos.reshape(-1, Q_BLOCK))))
    o = rms_norm(o, subln_g) * (1.0 - lam_init)
    return o.reshape(b, s, H * 2 * d) @ w_o

def mlstm_chunkwise(q, k, v, i_pre, log_f):
    b, s, H, dk = q.shape
    dv = v.shape[-1]
    f32 = jnp.float32
    xs = (to_chunks(q.astype(f32)), to_chunks(k.astype(f32)), to_chunks(v.astype(f32)),
          to_chunks(i_pre), to_chunks(log_f))
    tri = jnp.tril(jnp.ones((CHUNK, CHUNK), bool))

    def step(carry, inp):
        C, n, m = carry
        qc, kc, vc, ic, fc = inp
        bcum = jnp.cumsum(fc, -1)
        dmat = jnp.where(tri, bcum[..., :, None] - bcum[..., None, :] + ic[..., None, :], -jnp.inf)
        m_inter = bcum + m[..., None]
        m_t = jnp.maximum(jnp.max(dmat, -1), m_inter)
        w_intra = jnp.exp(dmat - m_t[..., None])
        w_inter = jnp.exp(m_inter - m_t)
        sqk = jnp.einsum('bhtd,bhsd->bhts', qc, kc) * w_intra
        num = (w_inter[..., None] * jnp.einsum('bhtd,bhde->bhte', qc, C)
               + jnp.einsum('bhts,bhse->bhte', sqk, vc))
        den = w_inter * jnp.einsum('bhtd,bhd->bht', qc, n) + jnp.sum(sqk, -1)
        h = num / jnp.maximum(jnp.abs(den), jnp.exp(-m_t))[..., None]
        b_last = bcum[..., -1]
        g_s = b_last[..., None] - bcum + ic
        m_new = jnp.maximum(b_last + m, jnp.max(g_s, -1))
        w_s = jnp.exp(g_s - m_new[..., None])
        decay = jnp.exp(b_last + m - m_new)
        C_new = decay[..., None, None] * C + jnp.einsum('bhs,bhsd,bhse->bhde', w_s, kc, vc)
        n_new = decay[..., None] * n + jnp.einsum('bhs,bhsd->bhd', w_s, kc)
        return (C_new, n_new, m_new), h

    init = (jnp.zeros((b, H, dk, dv), f32), jnp.zeros((b, H, dk), f32), jnp.zeros((b, H), f32))
    _, hs = lax.scan(step, init, xs)
    return from_chunks(hs).astype(v.dtype)

def mlstm_mixer(x, w_in, b_gates, norm_g, w_out):
    b, s, _ = x.shape
    H, dk, dv = MLSTM_HEADS, MLSTM_QK, MLSTM_V
    proj = x @ w_in
    o1, o2, o3, o4 = H * dk, 2 * H * dk, 2 * H * dk + H * dv, 2 * H * dk + 2 * H * dv
    q = proj[..., :o1].reshape(b, s, H, dk)
    k = proj[..., o1:o2].reshape(b, s, H, dk) * (dk ** -0.5)
    v = proj[..., o2:o3].reshape(b, s, H, dv)
    o_gate = jax.nn.sigmoid(proj[..., o3:o4])
    g = (proj[..., o4:] + b_gates).astype(jnp.float32).reshape(b, s, 4, H)
    h_f = mlstm_chunkwise(q, k, v, g[:, :, 0], jax.nn.log_sigmoid(g[:, :, 1]))
    fl = lambda t: jnp.flip(t, 1)
    h_b = fl(mlstm_chunkwise(fl(q), fl(k), fl(v), fl(g[:, :, 2]), jax.nn.log_sigmoid(fl(g[:, :, 3]))))
    h = head_group_norm(h_f + h_b, norm_g.reshape(H, dv))
    return (h.reshape(b, s, H * dv) * o_gate) @ w_out

def retention_chunkwise(q, k, v, log_gamma):
    b, s, H, dk = q.shape
    dv = v.shape[-1]
    f32 = jnp.float32
    idx = jnp.arange(CHUNK, dtype=f32)
    rel = idx[:, None] - idx[None, :]
    dmask = jnp.exp(jnp.maximum(rel, 0.0)[None] * log_gamma[:, None, None]) * (rel >= 0)[None]
    xi = jnp.exp((idx[None] + 1.0) * log_gamma[:, None])
    zeta = jnp.exp((CHUNK - 1.0 - idx[None]) * log_gamma[:, None])
    g_chunk = jnp.exp(CHUNK * log_gamma)
    xs = (to_chunks(q.astype(f32)), to_chunks(k.astype(f32)), to_chunks(v.astype(f32)))

    def step(R, inp):
        qc, kc, vc = inp
        inner = jnp.einsum('bhts,bhse->bhte', jnp.einsum('bhtd,bhsd->bhts', qc, kc) * dmask, vc)
        cross = jnp.einsum('bhtd,bhde->bhte', qc, R) * xi[None, :, :, None]
        R_new = g_chunk[None, :, None, None] * R + jnp.einsum('bhsd,bhse->bhde', kc * zeta[None, :, :, None], vc)
        return R_new, inner + cross

    _, ys = lax.scan(step, jnp.zeros((b, H, dk, dv), f32), xs)
    return from_chunks(ys).astype(v.dtype)

def retention_mixer(x, w_in, decay_logit, norm_g, w_o):
    b, s, _ = x.shape
    H, dk, dv = RET_HEADS, RET_QK, RET_V
    proj = x @ w_in
    o1, o2, o3 = H * dk, 2 * H * dk, 2 * H * dk + H * dv
    q = proj[..., :o1].reshape(b, s, H, dk)
    k = proj[..., o1:o2].reshape(b, s, H, dk) * (dk ** -0.5)
    v = proj[..., o2:o3].reshape(b, s, H, dv)
    gate = proj[..., o3:]
    lg = jax.nn.log_sigmoid(decay_logit.astype(jnp.float32))
    fl = lambda t: jnp.flip(t, 1)
    y = retention_chunkwise(q, k, v, lg[0]) + fl(retention_chunkwise(fl(q), fl(k), fl(v), lg[1]))
    y = head_group_norm(y, norm_g.reshape(H, dv)).reshape(b, s, H * dv)
    return (jax.nn.silu(gate) * y) @ w_o

def conv_ffn(x, w_up, conv_w, conv_b, w_down):
    u = x @ w_up
    s = u.shape[1]
    half = CONV_W // 2
    up = jnp.pad(u, ((0, 0), (half, half), (0, 0)))
    c = conv_b
    for j in range(CONV_W):
        c = c + conv_w[j] * up[:, j:j + s]
    g, val = c[..., :FFN_HIDDEN], c[..., FFN_HIDDEN:]
    return (jax.nn.gelu(g) * val) @ w_down

def first_inputs(seed: int = 0) -> dict:
    key = jax.random.key(seed)
    ks = iter(jax.random.split(key, 40))
    D = D_MODEL
    nA, nB, nC, nD = n_of(0), n_of(1), n_of(2), n_of(3)

    def w(shape, fan_in):
        return jax.random.normal(next(ks), shape, jnp.float32) * (fan_in ** -0.5)

    def gain(shape):
        return 1.0 + 0.02 * jax.random.normal(next(ks), shape, jnp.float32)

    inp = {}
    inp['x'] = jax.random.normal(next(ks), (BATCH, SEQ, D), jnp.float32)
    inp['norm_g'] = gain((DEPTH, 4, D))
    inp['ffn_w_up'] = w((DEPTH, D, 2 * FFN_HIDDEN), D)
    inp['ffn_conv_w'] = w((DEPTH, CONV_W, 2 * FFN_HIDDEN), CONV_W)
    inp['ffn_conv_b'] = 0.01 * jax.random.normal(next(ks), (DEPTH, 2 * FFN_HIDDEN), jnp.float32)
    inp['ffn_w_down'] = w((DEPTH, FFN_HIDDEN, D), FFN_HIDDEN)
    inp['mla_w_dq'] = w((nA, D, MLA_Q_LORA), D)
    inp['mla_q_norm_g'] = gain((nA, MLA_Q_LORA))
    inp['mla_w_uq'] = w((nA, MLA_Q_LORA, MLA_HEADS * (MLA_NOPE + MLA_ROPE)), MLA_Q_LORA)
    inp['mla_w_dkv'] = w((nA, D, MLA_KV_LORA + MLA_ROPE), D)
    inp['mla_kv_norm_g'] = gain((nA, MLA_KV_LORA))
    inp['mla_w_ukv'] = w((nA, MLA_KV_LORA, MLA_HEADS * (MLA_NOPE + MLA_V)), MLA_KV_LORA)
    inp['mla_w_o'] = w((nA, MLA_HEADS * MLA_V, D), MLA_HEADS * MLA_V)
    inp['diff_w_qkv'] = w((nB, D, 3 * D), D)
    inp['diff_lambda'] = 0.1 * jax.random.normal(next(ks), (nB, 4, DIFF_HD), jnp.float32)
    inp['diff_subln_g'] = gain((nB, 2 * DIFF_HD))
    inp['diff_w_o'] = w((nB, D, D), D)
    H = MLSTM_HEADS
    inp['mlstm_w_in'] = w((nC, D, 2 * H * MLSTM_QK + 2 * H * MLSTM_V + 4 * H), D)
    i_bias = 0.1 * jax.random.normal(next(ks), (nC, 2, H), jnp.float32)
    f_bias = jnp.linspace(3.0, 6.0, H, dtype=jnp.float32)[None, None] + 0.1 * jax.random.normal(next(ks), (nC, 2, H), jnp.float32)
    inp['mlstm_b_gates'] = jnp.stack([i_bias[:, 0], f_bias[:, 0], i_bias[:, 1], f_bias[:, 1]], 1).reshape(nC, 4 * H)
    inp['mlstm_norm_g'] = gain((nC, H * MLSTM_V))
    inp['mlstm_w_out'] = w((nC, H * MLSTM_V, D), H * MLSTM_V)
    Hr = RET_HEADS
    inp['ret_w_in'] = w((nD, D, 2 * Hr * RET_QK + 2 * Hr * RET_V), D)
    eps_h = 2.0 ** (-5.0 - np.arange(Hr, dtype=np.float32))
    base_logit = jnp.asarray(np.log((1.0 - eps_h) / eps_h), jnp.float32)
    inp['ret_decay_logit'] = base_logit[None, None] + 0.1 * jax.random.normal(next(ks), (nD, 2, Hr), jnp.float32)
    inp['ret_norm_g'] = gain((nD, Hr * RET_V))
    inp['ret_w_o'] = w((nD, Hr * RET_V, D), Hr * RET_V)
    return inp

def first_block(x, norm_g, ffn_w_up, ffn_conv_w, ffn_conv_b, ffn_w_down,
              mla_w_dq, mla_q_norm_g, mla_w_uq, mla_w_dkv, mla_kv_norm_g, mla_w_ukv, mla_w_o,
              diff_w_qkv, diff_lambda, diff_subln_g, diff_w_o,
              mlstm_w_in, mlstm_b_gates, mlstm_norm_g, mlstm_w_out,
              ret_w_in, ret_decay_logit, ret_norm_g, ret_w_o):
    h = x
    for i in range(DEPTH):
        kind, j = i % N_MIXERS, i // N_MIXERS
        a = rms_norm(h, norm_g[i, 0])
        if kind == 0:
            a = mla_mixer(a, mla_w_dq[j], mla_q_norm_g[j], mla_w_uq[j], mla_w_dkv[j],
                          mla_kv_norm_g[j], mla_w_ukv[j], mla_w_o[j])
        elif kind == 1:
            a = diff_mixer(a, diff_w_qkv[j], diff_lambda[j], diff_subln_g[j], diff_w_o[j], i)
        elif kind == 2:
            a = mlstm_mixer(a, mlstm_w_in[j], mlstm_b_gates[j], mlstm_norm_g[j], mlstm_w_out[j])
        else:
            a = retention_mixer(a, ret_w_in[j], ret_decay_logit[j], ret_norm_g[j], ret_w_o[j])
        h = h + rms_norm(a, norm_g[i, 1])
        f = conv_ffn(rms_norm(h, norm_g[i, 2]), ffn_w_up[i], ffn_conv_w[i], ffn_conv_b[i], ffn_w_down[i])
        h = h + rms_norm(f, norm_g[i, 3])
    return h


DEPTH_2 = 1

ATT_HEADS = 8
ATT_HEAD_DIM = 128
ATT_WIDTH = ATT_HEADS * ATT_HEAD_DIM
MOBA_BLOCK = 256
MOBA_TOPK = 3
Q_CHUNK = 128
ROPE_THETA_2 = 500000.0
ROPE_DIM = ATT_HEAD_DIM // 4

GDN_HEADS = 8
GDN_KDIM = 128
GDN_VDIM = 128
GDN_KWIDTH = GDN_HEADS * GDN_KDIM
GDN_VWIDTH = GDN_HEADS * GDN_VDIM
CONV_WIDTH = 4
GDN_CHUNK = 64

NEG = -1e30

IN_SPLITS = [ATT_WIDTH, ATT_WIDTH, ATT_WIDTH, ATT_WIDTH,
             GDN_KWIDTH, GDN_KWIDTH, GDN_VWIDTH, GDN_VWIDTH,
             GDN_HEADS, GDN_HEADS,
             D_MODEL, D_MODEL]
IN_COLS = int(sum(IN_SPLITS))
IN_OFFSETS = [int(o) for o in np.cumsum(IN_SPLITS)[:-1]]


def rmsnorm(x, w):
    xf = x.astype(jnp.float32)
    y = xf * lax.rsqrt(jnp.mean(xf * xf, axis=-1, keepdims=True) + EPS)
    return (y * w.astype(jnp.float32)).astype(x.dtype)

def l2norm(x):
    return x * lax.rsqrt(jnp.sum(x * x, axis=-1, keepdims=True) + EPS)

def partial_rope(x, pos):
    half = ROPE_DIM // 2
    inv_freq = jnp.power(ROPE_THETA_2, -jnp.arange(half, dtype=jnp.float32) * (2.0 / ROPE_DIM))
    ang = pos.astype(jnp.float32)[:, None] * inv_freq[None, :]
    cos, sin = jnp.cos(ang), jnp.sin(ang)
    xr = x[..., :ROPE_DIM].astype(jnp.float32)
    x1, x2 = xr[..., :half], xr[..., half:]
    rot = jnp.concatenate([x1 * cos - x2 * sin, x2 * cos + x1 * sin], axis=-1).astype(x.dtype)
    return jnp.concatenate([rot, x[..., ROPE_DIM:]], axis=-1)

def moba_attention(q, k, v):
    bsz, nh, s, dh = q.shape
    nb = -(-s // MOBA_BLOCK)
    pad = nb * MOBA_BLOCK - s
    nc = s // Q_CHUNK
    kk = min(MOBA_TOPK, nb)
    scale = dh ** -0.5
    padw = ((0, 0), (0, 0), (0, pad), (0, 0))
    kblk = jnp.pad(k, padw).reshape(bsz, nh, nb, MOBA_BLOCK, dh)
    vblk = jnp.pad(v, padw).reshape(bsz, nh, nb, MOBA_BLOCK, dh)
    kmean = jnp.mean(kblk.astype(jnp.float32), axis=3)
    qch = q.reshape(bsz, nh, nc, Q_CHUNK, dh)
    head_idx = jnp.arange(nh)[:, None, None]

    def per_batch(args):
        q_b, k_b, v_b, km_b = args

        def per_chunk(c):
            q_c = lax.dynamic_index_in_dim(q_b, c, axis=1, keepdims=False)
            q_pos = c * Q_CHUNK + jnp.arange(Q_CHUNK)
            blk = (c * Q_CHUNK) // MOBA_BLOCK
            gate = jnp.einsum('hqd,hnd->hqn', q_c.astype(jnp.float32), km_b)
            gate = jnp.where((jnp.arange(nb) < blk)[None, None, :], gate, -jnp.inf)
            _, idx = lax.top_k(gate, kk)
            sel_valid = jnp.arange(kk) < blk
            k_sel = k_b[head_idx, idx]
            v_sel = v_b[head_idx, idx]
            s_sel = jnp.einsum('hqd,hqjld->hqjl', q_c, k_sel).astype(jnp.float32) * scale
            s_sel = jnp.where(sel_valid[None, None, :, None], s_sel, NEG)
            k_own = lax.dynamic_index_in_dim(k_b, blk, axis=1, keepdims=False)
            v_own = lax.dynamic_index_in_dim(v_b, blk, axis=1, keepdims=False)
            s_own = jnp.einsum('hqd,hld->hql', q_c, k_own).astype(jnp.float32) * scale
            k_pos = blk * MOBA_BLOCK + jnp.arange(MOBA_BLOCK)
            s_own = jnp.where(k_pos[None, None, :] <= q_pos[None, :, None], s_own, NEG)
            scores = jnp.concatenate([s_sel.reshape(nh, Q_CHUNK, kk * MOBA_BLOCK), s_own], axis=-1)
            p = jax.nn.softmax(scores, axis=-1).astype(v_b.dtype)
            p_sel = p[..., :kk * MOBA_BLOCK].reshape(nh, Q_CHUNK, kk, MOBA_BLOCK)
            p_own = p[..., kk * MOBA_BLOCK:]
            return (jnp.einsum('hqjl,hqjld->hqd', p_sel, v_sel)
                    + jnp.einsum('hql,hld->hqd', p_own, v_own))

        return lax.map(per_chunk, jnp.arange(nc))

    out = lax.map(per_batch, (qch, kblk, vblk, kmean))
    return out.transpose(0, 1, 3, 2, 4).reshape(bsz, s, nh * dh)

def causal_dwconv(x, w):
    width = w.shape[0]
    return lax.conv_general_dilated(x, w[:, None, :], window_strides=(1,), padding=[(width - 1, 0)],
                                    dimension_numbers=('NWC', 'WIO', 'NWC'),
                                    feature_group_count=x.shape[-1])

def gated_deltanet(q, k, v, g, beta):
    bsz, s, nh, dk = q.shape
    dv = v.shape[-1]
    c = GDN_CHUNK
    n = s // c
    q = l2norm(q) * (dk ** -0.5)
    k = l2norm(k)

    def chunks(t):
        return t.reshape(bsz, n, c, nh, -1).transpose(0, 3, 1, 2, 4)

    qc, kc, vc = chunks(q), chunks(k), chunks(v)
    gc = g.reshape(bsz, n, c, nh).transpose(0, 3, 1, 2)
    bc = beta.reshape(bsz, n, c, nh).transpose(0, 3, 1, 2)
    G = jnp.cumsum(gc, axis=-1)
    causal = jnp.tril(jnp.ones((c, c), dtype=bool))
    strict = jnp.tril(jnp.ones((c, c), dtype=bool), k=-1)
    diff = G[..., :, None] - G[..., None, :]
    decay = jnp.where(causal, jnp.exp(jnp.where(causal, diff, 0.0)), 0.0)
    k_beta = kc * bc[..., None]
    m = jnp.where(strict, jnp.einsum('bhnid,bhnjd->bhnij', k_beta, kc) * decay, 0.0)
    a_mat = m + jnp.eye(c, dtype=m.dtype)
    rhs = jnp.concatenate([vc * bc[..., None], k_beta * jnp.exp(G)[..., None]], axis=-1)
    sol = lax.linalg.triangular_solve(a_mat, rhs, left_side=True, lower=True, unit_diagonal=True)
    u, w = sol[..., :dv], sol[..., dv:]
    qk = jnp.where(causal, jnp.einsum('bhnid,bhnjd->bhnij', qc, kc) * decay, 0.0)
    q_dec = qc * jnp.exp(G)[..., None]
    k_dec = kc * jnp.exp(G[..., -1:] - G)[..., None]
    g_last = jnp.exp(G[..., -1])

    def step(state, xs):
        u_i, w_i, q_i, qk_i, k_i, gl_i = xs
        v_new = u_i - jnp.einsum('bhcd,bhde->bhce', w_i, state)
        o_i = jnp.einsum('bhcd,bhde->bhce', q_i, state) + jnp.einsum('bhij,bhje->bhie', qk_i, v_new)
        state = state * gl_i[..., None, None] + jnp.einsum('bhcd,bhce->bhde', k_i, v_new)
        return state, o_i

    xs = tuple(jnp.moveaxis(t, 2, 0) for t in (u, w, q_dec, qk, k_dec, g_last))
    state0 = jnp.zeros((bsz, nh, dk, dv), dtype=jnp.float32)
    _, o = lax.scan(step, state0, xs)
    return o.transpose(1, 0, 3, 2, 4).reshape(bsz, s, nh, dv)

def hybrid_layer(x, pre_norm_w, w_in, conv_w, a_log, dt_bias, gdn_norm_w,
                 w_branch_a, w_branch_b, w_out, post_norm_w):
    bsz, s, _ = x.shape
    f32 = jnp.float32
    h = rmsnorm(x, pre_norm_w)
    proj = jnp.einsum('bsd,de->bse', h, w_in)
    (q_a, k_a, v_a, z_a, q_b, k_b, v_b, z_b,
     beta_logit, decay_logit, gate_a, gate_b) = jnp.split(proj, IN_OFFSETS, axis=-1)

    pos = jnp.arange(s)

    def heads(t):
        return t.reshape(bsz, s, ATT_HEADS, ATT_HEAD_DIM).transpose(0, 2, 1, 3)

    o_a = moba_attention(partial_rope(heads(q_a), pos), partial_rope(heads(k_a), pos), heads(v_a))
    y_a = jnp.einsum('bse,ed->bsd', o_a * jax.nn.silu(z_a), w_branch_a)

    qkv = jax.nn.silu(causal_dwconv(jnp.concatenate([q_b, k_b, v_b], axis=-1), conv_w))
    q_b, k_b, v_b = jnp.split(qkv, [GDN_KWIDTH, 2 * GDN_KWIDTH], axis=-1)
    g = -jnp.exp(a_log.astype(f32)) * jax.nn.softplus(decay_logit.astype(f32) + dt_bias.astype(f32))
    beta = jax.nn.sigmoid(beta_logit.astype(f32))
    o_b = gated_deltanet(q_b.reshape(bsz, s, GDN_HEADS, GDN_KDIM).astype(f32),
                         k_b.reshape(bsz, s, GDN_HEADS, GDN_KDIM).astype(f32),
                         v_b.reshape(bsz, s, GDN_HEADS, GDN_VDIM).astype(f32), g, beta)
    o_b = rmsnorm(o_b, gdn_norm_w).reshape(bsz, s, GDN_VWIDTH).astype(x.dtype)
    y_b = jnp.einsum('bse,ed->bsd', o_b * jax.nn.silu(z_b), w_branch_b)

    merged = jax.nn.sigmoid(gate_a) * y_a + jax.nn.sigmoid(gate_b) * y_b
    out = jnp.einsum('bsd,de->bse', merged, w_out)
    return x + rmsnorm(out, post_norm_w)

def second_inputs(seed: int = 0) -> dict:
    key = jax.random.key(seed)
    ks = jax.random.split(key, 12)
    conv_ch = 2 * GDN_KWIDTH + GDN_VWIDTH
    x = jax.random.normal(ks[0], (BATCH, SEQ, D_MODEL), jnp.float32)
    pre_norm_w = 1.0 + 0.05 * jax.random.normal(ks[1], (DEPTH_2, D_MODEL), jnp.float32)
    w_in = jax.random.normal(ks[2], (DEPTH_2, D_MODEL, IN_COLS), jnp.float32) * D_MODEL ** -0.5
    conv_w = jax.random.normal(ks[3], (DEPTH_2, CONV_WIDTH, conv_ch), jnp.float32) * CONV_WIDTH ** -0.5
    a_log = jnp.log(jax.random.uniform(ks[4], (DEPTH_2, GDN_HEADS), jnp.float32, 1.0, 16.0))
    dt = jnp.exp(jax.random.uniform(ks[5], (DEPTH_2, GDN_HEADS), jnp.float32,
                                    float(np.log(1e-3)), float(np.log(1e-1))))
    dt_bias = dt + jnp.log(-jnp.expm1(-dt))
    gdn_norm_w = 1.0 + 0.05 * jax.random.normal(ks[6], (DEPTH_2, GDN_VDIM), jnp.float32)
    w_branch_a = jax.random.normal(ks[7], (DEPTH_2, ATT_WIDTH, D_MODEL), jnp.float32) * ATT_WIDTH ** -0.5
    w_branch_b = jax.random.normal(ks[8], (DEPTH_2, GDN_VWIDTH, D_MODEL), jnp.float32) * GDN_VWIDTH ** -0.5
    w_out = jax.random.normal(ks[9], (DEPTH_2, D_MODEL, D_MODEL), jnp.float32) * D_MODEL ** -0.5
    post_norm_w = 1.0 + 0.05 * jax.random.normal(ks[10], (DEPTH_2, D_MODEL), jnp.float32)
    return {"x": x, "pre_norm_w": pre_norm_w, "w_in": w_in, "conv_w": conv_w,
            "a_log": a_log, "dt_bias": dt_bias, "gdn_norm_w": gdn_norm_w,
            "w_branch_a": w_branch_a, "w_branch_b": w_branch_b, "w_out": w_out,
            "post_norm_w": post_norm_w}

def second_block(x, pre_norm_w, w_in, conv_w, a_log, dt_bias, gdn_norm_w,
              w_branch_a, w_branch_b, w_out, post_norm_w):
    for layer in range(DEPTH_2):
        x = hybrid_layer(x, pre_norm_w[layer], w_in[layer], conv_w[layer], a_log[layer],
                         dt_bias[layer], gdn_norm_w[layer], w_branch_a[layer],
                         w_branch_b[layer], w_out[layer], post_norm_w[layer])
    return x


def setup_inputs(seed=0):
    out = dict(first_inputs(seed))
    for name, value in second_inputs(seed + 1).items():
        if name != "x":
            out[name + "_2"] = value
    return out


def reference(
    x, norm_g, ffn_w_up, ffn_conv_w, ffn_conv_b, ffn_w_down, mla_w_dq, mla_q_norm_g, mla_w_uq,
    mla_w_dkv, mla_kv_norm_g, mla_w_ukv, mla_w_o, diff_w_qkv, diff_lambda, diff_subln_g,
    diff_w_o, mlstm_w_in, mlstm_b_gates, mlstm_norm_g, mlstm_w_out, ret_w_in, ret_decay_logit,
    ret_norm_g, ret_w_o, pre_norm_w_2, w_in_2, conv_w_2, a_log_2, dt_bias_2, gdn_norm_w_2,
    w_branch_a_2, w_branch_b_2, w_out_2, post_norm_w_2,
):
    x = first_block(
        x, norm_g, ffn_w_up, ffn_conv_w, ffn_conv_b, ffn_w_down, mla_w_dq, mla_q_norm_g,
        mla_w_uq, mla_w_dkv, mla_kv_norm_g, mla_w_ukv, mla_w_o, diff_w_qkv, diff_lambda,
        diff_subln_g, diff_w_o, mlstm_w_in, mlstm_b_gates, mlstm_norm_g, mlstm_w_out, ret_w_in,
        ret_decay_logit, ret_norm_g, ret_w_o,
    )
    return second_block(
        x, pre_norm_w_2, w_in_2, conv_w_2, a_log_2, dt_bias_2, gdn_norm_w_2, w_branch_a_2,
        w_branch_b_2, w_out_2, post_norm_w_2,
    )


_drawn_inputs = setup_inputs


def setup_inputs(seed=0):
    import zlib

    import numpy as np

    out = dict(_drawn_inputs(seed))
    spreads = {}
    factors = {'ffn_conv_b': 3.934, 'diff_subln_g': 4.383, 'gdn_norm_w_2': 3.041, 'post_norm_w_2': 2.798}
    for name, (base, spread) in spreads.items():
        noise = np.random.default_rng([zlib.crc32(name.encode()), seed]).standard_normal(out[name].shape)
        drawn = base * np.exp(spread * noise) if base else spread * noise
        out[name] = __import__('jax').numpy.asarray(drawn.astype(out[name].dtype))
    for name, factor in factors.items():
        out[name] = (out[name] * factor).astype(out[name].dtype)
    return out
```

```python
from contextlib import ExitStack
import math

import numpy as np

import concourse.bass as bass
from concourse import mybir

F32 = mybir.dt.float32
F32R = mybir.dt.float32r
ALU = mybir.AluOpType
ACT = mybir.ActivationFunctionType
AX = mybir.AxisListType

P = 128
TOK = 256
NT = TOK // P
D = 1024
KB = D // P
EPS = 1e-6
HEADS = 8
FFN = 2816
FFN_STEPS = FFN // (2 * P)
PAIRS = HEADS // 2

MLA_QL, MLA_KVL, MLA_ROPE, MLA_NOPE = 384, 256, 64, 128
MLA_QB, MLA_KVB = MLA_QL // P, MLA_KVL // P
MLA_SCALE = (MLA_NOPE + MLA_ROPE) ** -0.5
MLA_DOWN = MLA_QL + MLA_KVL + MLA_ROPE
DIFF_SCALE = 64 ** -0.5
LAM_INIT = 0.8 - 0.6 * math.exp(-0.3)
ATT_SCALE = P ** -0.5
ROT = 32
LEVELS = 6


class Phase:

    def __init__(self, name, widths, count, gpsimd_low=(), lagging=()):
        self.name, self.widths, self.count, self.gpsimd_low, self.lagging = name, widths, count, gpsimd_low, lagging
        self.base = {}


def phases():
    every = {k: 1024 for k in range(6)}
    four = {k: 1024 for k in range(4)}
    ph = dict(
        down_a=Phase("down_a", {k: MLA_DOWN for k in range(6)}, 1),
        down_b=Phase("down_b", {k: MLA_DOWN for k in range(2)}, 1),
        mla=Phase("mla", {0: MLA_QB * 192, 1: MLA_KVB * 256, 2: 1024}, HEADS, lagging=(2,)),
        ffn0=Phase("ffn0", every, FFN_STEPS, (3,), (5,)),
        diff=Phase("diff", four, HEADS, (1, 3), (3,)),
        ffn1=Phase("ffn1", every, FFN_STEPS, (3,), (5,)),
        gates=Phase("gates", {4: KB * 16}, 1),
        gdn=Phase("gdn", four, HEADS, (0, 1, 2, 3)),
        att=Phase("att", four, HEADS, (0, 2, 3)),
        out=Phase("out", {k: 1024 for k in range(5)}, HEADS, (1, 3), (4,)),
    )
    used = dict.fromkeys(range(6), 0)
    for p in ph.values():
        for k in p.widths:
            p.base[k] = used[k]
            used[k] += p.count
    ph["down_a"].after, ph["down_b"].after, ph["mla"].after = [ph["down_b"]], [ph["mla"]], [ph["ffn0"]]
    ph["ffn0"].after, ph["diff"].after, ph["ffn1"].after = [ph["diff"]], [ph["ffn1"]], [ph["gates"], ph["gdn"]]
    ph["gates"].after, ph["gdn"].after, ph["att"].after, ph["out"].after = [], [ph["att"]], [ph["out"]], []
    return ph


VEC = {}


def _vec(name, width):
    VEC[name] = (sum(w for _, w in VEC.values()), width)


for _n, _w in (("pre_gain", 5 * KB), ("q_gain", MLA_QB), ("kv_gain", MLA_KVB), ("sub_gain", 1),
               ("gdn_gain", 1), ("conv", HEADS * 12), ("ffn_conv", 2 * FFN_STEPS * 16),
               ("slope", HEADS), ("dt", 2 * HEADS), ("a_log", 2 * HEADS), ("lam", 256),
               ("norm_scale", 8), ("l2_factor", 8)):
    _vec(_n, _w)
NVEC = sum(w for _, w in VEC.values())

CONST = {}


def _const(name, width):
    CONST[name] = (sum(w for _, w in CONST.values()), width)


for _n, _w in (("ident", P), ("upper", P), ("strict_lower", P), ("level1", P), ("level1_t", P),
               ("levels", LEVELS * P), ("ones", P), ("causal", 3 * P), ("dist", NT * TOK),
               ("mla_cos", NT * MLA_ROPE), ("mla_sin", NT * MLA_ROPE),
               ("att_cos", NT * 2 * ROT), ("att_sin", NT * 2 * ROT)):
    _const(_n, _w)
NCONST = sum(w for _, w in CONST.values())


def constants():
    c = np.zeros((P, NCONST), np.float32)

    def put(name, a):
        o, w = CONST[name]
        c[:, o:o + w] = np.asarray(a, np.float32).reshape(P, w)

    r, k = np.arange(P)[:, None], np.arange(P)[None, :]
    put("ident", r == k)
    put("upper", r <= k)
    put("strict_lower", k < r)

    def level(s):
        return (r // (2 * s) == k // (2 * s)) & (r % (2 * s) >= s) & (k % (2 * s) < s)

    put("level1", level(1))
    put("level1_t", level(1).T)
    put("levels", np.stack([level(2 << n) for n in range(LEVELS)], 1))
    put("ones", np.ones((P, P)))
    tri = np.where(k <= r, 0.0, -1e30)
    put("causal", np.stack([tri, np.zeros((P, P)), tri], 1))
    pos = np.arange(TOK).reshape(NT, P).T
    put("dist", np.abs(pos[:, :, None] - np.arange(TOK)[None, None, :]))

    def rope(inv, repeat):
        ang = (np.arange(TOK, dtype=np.float32)[:, None] * inv[None, :]).astype(np.float32)
        co, si = np.cos(ang), np.sin(ang)
        both = np.concatenate([co, co], 1), np.concatenate([-si, si], 1)
        return [np.repeat(x.reshape(NT, P, -1).transpose(1, 0, 2)[:, :, None], repeat, 2) for x in both]

    inv = np.float32(10000.0) ** (-np.arange(0, MLA_ROPE, 2, dtype=np.float32) / np.float32(MLA_ROPE))
    co, si = rope(inv, 1)
    put("mla_cos", co)
    put("mla_sin", si)
    inv = np.power(np.float32(500000.0), -np.arange(ROT // 2, dtype=np.float32) * np.float32(2.0 / ROT))
    co, si = rope(inv, 2)
    put("att_cos", co)
    put("att_sin", si)
    return c


def lay_out(a):
    f = {k: np.asarray(v) for k, v in a.items()}
    out = {"x": f["x"][0], "const": constants()}

    v = np.zeros((P, NVEC), np.float32)

    def put(name, x):
        o, w = VEC[name]
        v[:, o:o + w] = np.asarray(x).reshape(P, w)

    def channels(x):
        return x.reshape(-1, P).T

    ng = f["norm_g"]
    put("pre_gain", np.concatenate([channels(g) for g in (ng[0, 0], ng[0, 2], ng[1, 0], ng[1, 2],
                                                          f["pre_norm_w_2"][0])], 1))
    put("q_gain", channels(f["mla_q_norm_g"][0]))
    put("kv_gain", channels(f["mla_kv_norm_g"][0]))
    put("sub_gain", channels(f["diff_subln_g"][0]))
    put("gdn_gain", channels(f["gdn_norm_w_2"][0]))
    put("conv", f["conv_w_2"][0].reshape(4, 3, HEADS, P).transpose(3, 2, 1, 0))
    taps = np.concatenate([f["ffn_conv_w"], f["ffn_conv_b"][:, None]], 1)
    put("ffn_conv", taps.reshape(2, 4, 2, FFN_STEPS, 2, P).transpose(5, 0, 3, 4, 2, 1))
    slopes = 2.0 ** (-8.0 * np.arange(1, HEADS + 1) / HEADS)
    put("slope", np.broadcast_to(-slopes / DIFF_SCALE, (P, HEADS)))
    put("dt", np.broadcast_to(np.repeat(f["dt_bias_2"][0], 2), (P, 16)))
    put("a_log", np.broadcast_to(np.repeat(f["a_log_2"][0], 2), (P, 16)))
    put("lam", np.broadcast_to(f["diff_lambda"][0].reshape(-1), (P, 256)))
    put("norm_scale", np.broadcast_to(np.array([1 / MLA_QL, 1 / MLA_QL, 1 / MLA_KVL, 1 / MLA_KVL, 0, 0, 0, 0]), (P, 8)))
    fac = np.array([0.5 * P ** -0.5, 0.5 * P ** -0.5, 0.5, 0.5] * 2)
    put("l2_factor", np.broadcast_to(fac, (P, 8)))
    out["vec"] = v
    out["post_gain"] = np.ascontiguousarray(np.broadcast_to(
        np.stack([ng[0, 1], ng[0, 3], ng[1, 1], ng[1, 3], f["post_norm_w_2"][0]])[:, None], (5, P, D)))

    def chunks(name, parts):
        for slot, x in parts.items():
            out[f"w_{name}_{slot}"] = np.ascontiguousarray(x).reshape(x.shape[0] * P, -1)

    down = np.concatenate([f["mla_w_dq"][0], f["mla_w_dkv"][0]], 1).reshape(KB, P, MLA_DOWN)
    chunks("down_a", {k: down[k:k + 1] for k in range(6)})
    chunks("down_b", {k: down[6 + k:7 + k] for k in range(2)})

    def rows(w):
        return w.reshape(-1, P, D)

    def heads(w, width):
        return w.reshape(-1, P, w.shape[1] // width, width).transpose(2, 1, 0, 3)

    chunks("mla", {0: heads(f["mla_w_uq"][0], 192), 1: heads(f["mla_w_ukv"][0], 256),
                   2: rows(f["mla_w_o"][0])})
    for layer in range(2):
        up = f["ffn_w_up"][layer].reshape(KB, P, 2, FFN_STEPS, 2, P)
        dn = f["ffn_w_down"][layer].reshape(FFN_STEPS, 2, P, D)
        parts = {2 * j + g: up[:, :, g, :, j].transpose(2, 1, 0, 3) for j in range(2) for g in range(2)}
        parts.update({4 + j: dn[:, j] for j in range(2)})
        chunks(f"ffn{layer}", parts)
    qkv = f["diff_w_qkv"][0]
    chunks("diff", {**{n: heads(qkv[:, n * D:n * D + D], P) for n in range(3)}, 3: rows(f["diff_w_o"][0])})
    w_in = f["w_in_2"][0]

    def part(n):
        return w_in[:, n * D:n * D + D]

    qk = np.stack([heads(part(0), P), heads(part(1), P)], 3)
    chunks("att", {0: qk[:, :, 0:4], 1: qk[:, :, 4:8], 2: heads(part(2), P), 3: heads(part(3), P)})
    chunks("gdn", {n: heads(part(4 + n), P) for n in range(4)})
    o = 8 * D
    chunks("gates", {4: w_in[:, o:o + 16].reshape(KB, P, 16).transpose(1, 0, 2)[None]})
    o += 16
    chunks("out", {0: heads(w_in[:, o:o + D], P), 1: heads(w_in[:, o + D:o + 2 * D], P),
                   2: heads(f["w_branch_a_2"][0], P), 3: heads(f["w_branch_b_2"][0], P),
                   4: rows(f["w_out_2"][0])})
    return out


def build(nc, dram, y_out):
    ph = phases()
    ctx = ExitStack()

    scope = [ctx]

    def sb(name, shape, dt=F32):
        return scope[-1].enter_context(nc.sbuf_tensor(name, shape, dt))

    def open_scope():
        scope.append(ExitStack())

    def close_scope():
        scope.pop().close()

    def sem(name):
        return ctx.enter_context(nc.semaphore(name))

    def sems(prefix, names):
        return {n: sem(f"{prefix}_{n}") for n in names.split()}

    raw = [sb(f"raw{k}", [P, 1024]) for k in range(5)]
    high = [sb(f"high{k}", [P, 1024], F32R) for k in range(5)]
    low = [sb(f"low{k}", [P, 1024], F32R) for k in range(5)]

    const = sb("const", [P, NCONST])
    vec = sb("vec", [P, NVEC])
    post_gain = sb("post_gain_sb", [P, D])
    hid = sb("hid", [P, NT, D])
    hn = sb("hn", [P, NT, D])
    junk = sb("junk", [P, 512])
    xh = sb("xh", [P, KB, TOK], F32R)
    xl = sb("xl", [P, KB, TOK], F32R)
    stat = sb("stat", [P, 16])
    mean = sb("mean", [P, 16])
    power = sb("power", [P, 8])

    v_sb = sb("v_sb", [P, NT, P])
    soft = sb("soft", [P, 16])
    o32 = sb("o32", [P, TOK])
    open_scope()
    raw.append(sb("raw5", [P, 1024]))
    high.append(sb("high5", [P, 1024], F32R))
    low.append(sb("low5", [P, 1024], F32R))

    acc = ctx.enter_context(nc.psum_tensor("acc", [P, 4, 512], F32))
    W = [ctx.enter_context(nc.psum_tensor(f"work{k}", [P, 512], F32)) for k in range(4)]

    def cst(name, shape=None, **dims):
        o, w = CONST[name]
        return const[:, o:o + w] if shape is None else const[:, o:o + w].rearrange(shape, **dims)

    def vcol(name, at=0, width=None):
        o, w = VEC[name]
        if isinstance(at, int):
            return vec[:, o + at:o + at + (width or w)]
        return vec[:, bass.ds(at + o, width)]

    ident = cst("ident")

    def spread(ap, n):
        return ap.unsqueeze(2).to_broadcast([P, ap.shape[1], n])

    def repeat(ap, n):
        return ap.unsqueeze(1).to_broadcast([P, n, ap.shape[1]])

    landed = [sem(f"landed{k}") for k in range(6)]
    high_done = [sem(f"high_done{k}") for k in range(6)]
    low_done = [sem(f"low_done{k}") for k in range(6)]
    used = [sem(f"used{k}") for k in range(6)]

    def load(sp, p, k, i):
        n, w = p.base[k] + i, p.widths[k]
        src = dram[f"w_{p.name}_{k}"]
        if not (isinstance(n, int) and n == 0):
            sp.wait_ge(low_done[k], n)
        at = slice(i * P, (i + 1) * P) if isinstance(i, int) else bass.ds(i * P, P)
        sp.dma_start(raw[k][:, 0:w], src[at, :]).then_inc(landed[k], 16)

    def split_high(act, p, k, i):
        n, w = p.base[k] + i, p.widths[k]
        if not (isinstance(n, int) and n == 0):
            act.wait_ge(used[k], n)
        act.wait_ge(landed[k], n * 16 + 16)
        act.activation(high[k][:, 0:w], raw[k][:, 0:w], ACT.Copy).then_inc(high_done[k], 1)

    def split_low(eng, is_gpsimd, p, k, i):
        n, w = p.base[k] + i, p.widths[k]
        if (k in p.gpsimd_low) != is_gpsimd:
            return
        eng.wait_ge(high_done[k], n + 1)
        eng.tensor_tensor(low[k][:, 0:w], raw[k][:, 0:w], high[k][:, 0:w], ALU.subtract).then_inc(low_done[k], 1)

    def refill(split, p, k, i):
        if not (isinstance(i, int) and i == p.count - 1):
            return split(p, k, i + 1)
        for q in p.after:
            if k in q.widths:
                split(q, k, 0)

    def first_of_next(split, p):
        for q in p.after:
            for k in q.widths:
                if k not in p.widths:
                    split(q, k, 0)

    def hi_of(act):
        return lambda p, k, i: split_high(act, p, k, i)

    def lo_of(eng, is_gpsimd=False):
        return lambda p, k, i: split_low(eng, is_gpsimd, p, k, i)

    def chunk_ready(pe, p, k, i):
        pe.wait_ge(low_done[k], p.base[k] + i + 1)

    def mm3(pe, out, lhs, rhs, start, stop):
        pe.matmul(out, lhs[0], rhs[0], start=start, stop=False)
        pe.matmul(out, lhs[0], rhs[1], start=False, stop=False)
        return pe.matmul(out, lhs[1], rhs[0], start=False, stop=stop)

    def both(h, l, *at):
        return h[at], l[at]

    def wslot(k, a, b):
        return high[k][:, a:b], low[k][:, a:b]

    def project_t(pe, out, k, width=P, offset=0, x=None, blocks=KB):
        x = x or (xh, xl)
        for b in range(blocks):
            o = b * width + offset
            last = mm3(pe, out, wslot(k, o, o + P), (x[0][:, b, :], x[1][:, b, :]), b == 0, b == blocks - 1)
        return last

    def rows_out(pe, k, oh, ol, start, stop):
        for t in range(NT):
            for half in range(2):
                c = half * 512
                last = mm3(pe, acc[:, 2 * t + half, :], (oh[:, t * P:(t + 1) * P], ol[:, t * P:(t + 1) * P]),
                           wslot(k, c, c + 512), start, stop)
        return last

    class Chain:

        def __init__(self, eng, s, per, i, seen=0):
            self.eng, self.s, self.per, self.at, self.k = eng, s, per, i * per + seen, 0

        def __call__(self, ins):
            ins.then_inc(self.s, 1)
            self.k += 1
            assert self.k <= self.per
            self.eng.wait_ge(self.s, self.at + self.k)

    def over(eng, count, body, peel_end=1):
        body(0)
        with eng.Fori(1, count - peel_end) as i:
            body(eng.snap(i))
        for i in range(count - peel_end, count):
            body(i)

    g = sems("g", "x tables")
    n_ = sems("n", "hid sq mean root hn turned xh xl")
    h = sems("h", "qkev s mx sm e p pt ptev vev pv oh ol rope roped turned turned_ev")
    DIFF_SEEN, ATT_SEEN = HEADS, 2 * HEADS
    q_ = sems("q", "sq mean root upd gain")

    def evac_split_act(act, items, banks, base, s, turned=None):
        for p, (src, gain, h, l, bank) in enumerate(items):
            if turned:
                act.wait_ge(*turned(bank))
            if p >= banks:
                act.wait_ge(s["xl"], base + p - banks + 1)
            act.activation(h, src, ACT.Copy, scale=gain).then_inc(s["xh"], 1)

    def evac_split_dve(dve, items, base, s):
        for p, (src, gain, h, l, bank) in enumerate(items):
            dve.wait_ge(s["xh"], base + p + 1)
            dve.scalar_tensor_tensor(l, src, gain, h, ALU.mult, ALU.subtract).then_inc(s["xl"], 1)

    def x_items(n):
        out = []
        for p in range(KB):
            b = 2 * (p % 4) + p // 4
            out.append((W[b // 2][:, (b % 2) * TOK:(b % 2 + 1) * TOK], vcol("pre_gain", n * KB + b, 1),
                        xh[:, b, :], xl[:, b, :], b // 2))
        return out

    def pre_pe(pe, n):
        pe.wait_ge(n_["hn"], 2 * n + 2)
        for b in range(KB):
            for t in range(NT):
                last = pe.transpose(W[b // 2][:, (b % 2) * TOK + t * P:(b % 2) * TOK + (t + 1) * P],
                                    hn[:, t, b * P:(b + 1) * P], ident)
            if b % 2:
                last.then_inc(n_["turned"], 1)

    def pre_act(act, n):
        for t in range(NT):
            if n:
                act.wait_ge(n_["hid"], 2 * (n - 1) + t + 1)
            elif t == 0:
                act.wait_ge(g["x"], 16)
            act.activation(hn[:, t, :], hid[:, t, :], ACT.Square, accum_out=stat[:, t:t + 1]).then_inc(n_["sq"], 1)
        evac_split_act(act, x_items(n), 4, KB * n, n_, lambda bank: (n_["turned"], 4 * n + bank + 1))

    def pre_dve(dve, n):
        for t in range(NT):
            dve.wait_ge(n_["sq"], 2 * n + t + 1)
            dve.tensor_scalar(mean[:, t:t + 1], stat[:, t:t + 1], 1.0 / D, EPS, ALU.mult, ALU.add).then_inc(n_["mean"], 1)
        for t in range(NT):
            dve.wait_ge(n_["root"], 2 * n + t + 1)
            dve.tensor_scalar(hn[:, t, :], hid[:, t, :], stat[:, 8 + t:9 + t], None, ALU.mult).then_inc(n_["hn"], 1)
        evac_split_dve(dve, x_items(n), KB * n, n_)

    def pre_pool(pool, n):
        for t in range(NT):
            pool.wait_ge(n_["mean"], 2 * n + t + 1)
            pool.tensor_tensor(stat[:, 8 + t:9 + t], mean[:, t:t + 1], power[:, 0:1], ALU.pow).then_inc(n_["root"], 1)

    def post_act(act, n, p, k):
        act.wait_ge(used[k], p.base[k] + p.count)
        for t in range(NT):
            act.activation(hn[:, t, :], acc[:, 2 * t:2 * t + 2, :].rearrange("p a b -> p (a b)"), ACT.Square,
                           accum_out=stat[:, 2 + t:3 + t]).then_inc(q_["sq"], 1)

    def post_dve(dve, n):
        dve.wait_ge(q_["gain"], 16 * (n + 1))
        for t in range(NT):
            dve.wait_ge(q_["sq"], 2 * n + t + 1)
            dve.tensor_scalar(mean[:, 2 + t:3 + t], stat[:, 2 + t:3 + t], 1.0 / D, EPS, ALU.mult, ALU.add).then_inc(q_["mean"], 1)
        for t in range(NT):
            dve.wait_ge(q_["root"], 2 * n + t + 1)
            dve.scalar_tensor_tensor(hn[:, t, :], acc[:, 2 * t:2 * t + 2, :].rearrange("p a b -> p (a b)"),
                                     stat[:, 10 + t:11 + t], post_gain[:], ALU.mult, ALU.mult).then_inc(q_["upd"], 1)
            dve.wait_ge(q_["upd"], 2 * n + t + 1)
            dve.tensor_tensor(hid[:, t, :], hid[:, t, :], hn[:, t, :], ALU.add).then_inc(n_["hid"], 1)

    def post_pool(pool, n):
        for t in range(NT):
            pool.wait_ge(q_["mean"], 2 * n + t + 1)
            pool.tensor_tensor(stat[:, 10 + t:11 + t], mean[:, 2 + t:3 + t], power[:, 0:1], ALU.pow).then_inc(q_["root"], 1)
        if n < 4:
            pool.wait_ge(q_["upd"], 2 * n + 2)
            pool.dma_start(post_gain[:], dram["post_gain"][n + 1]).then_inc(q_["gain"], 16)

    def start_sp(sp):
        sp.dma_start(hid[:], dram["x"].rearrange("(t p) d -> p t d", p=P)).then_inc(g["x"], 16)
        sp.dma_start(const[:], dram["const"]).then_inc(g["tables"], 16)
        sp.dma_start(vec[:], dram["vec"]).then_inc(g["tables"], 16)

    def start_pool(pool):
        pool.dma_start(post_gain[:], dram["post_gain"][0]).then_inc(q_["gain"], 16)

    m = sems("m", "sq mean root cn turned xh xl krev rope_k qk")
    cqh, cql = sb("cqh", [P, MLA_QB, TOK], F32R), sb("cql", [P, MLA_QB, TOK], F32R)
    ckh, ckl = sb("ckh", [P, MLA_KVB, TOK], F32R), sb("ckl", [P, MLA_KVB, TOK], F32R)
    rope_pad = sb("rope_pad", [P, NT, P])
    rope_a, rope_b = sb("rope_a", [P, NT, MLA_ROPE]), sb("rope_b", [P, NT, MLA_ROPE])
    kr_t = sb("kr_t", [P, TOK])
    qr_t = sb("qr_t", [P, TOK])
    q_sb, k_sb = sb("q_sb", [P, TOK]), sb("k_sb", [P, TOK])
    prob = sb("prob", [P, 4, TOK])
    prob_t = sb("prob_t", [P, NT, TOK])
    oh, ol = sb("oh", [P, TOK], F32R), sb("ol", [P, TOK], F32R)

    def down_pe(pe):
        for b in range(KB):
            p, k = (ph["down_a"], b) if b < 6 else (ph["down_b"], b - 6)
            chunk_ready(pe, p, k, 0)
            if b == 0:
                pe.wait_ge(n_["xl"], KB)
            for t in range(NT):
                x = (xh[:, b, t * P:(t + 1) * P], xl[:, b, t * P:(t + 1) * P])
                mm3(pe, acc[:, t, 0:MLA_QL], x, wslot(k, 0, MLA_QL), b == 0, b == KB - 1)
                last = mm3(pe, acc[:, 2 + t, 0:320], x, wslot(k, MLA_QL, MLA_DOWN), b == 0, b == KB - 1)
            last.then_inc(used[k], 1)
        pe.wait_ge(m["cn"], 4)
        pe.wait_ge(m["rope_k"], 3)
        for src, bank, half in ((0, 0, 0), (1, 0, 1), (2, 1, 0), (3, 1, 1), (4, 2, 0), (5, 2, 1)):
            for t in range(NT):
                a = latent[:, t, src * P:(src + 1) * P] if src < 5 else rope_pad[:, t, :]
                last = pe.transpose(W[bank][:, half * TOK + t * P:half * TOK + (t + 1) * P], a, ident)
            if half:
                last.then_inc(m["turned"], 1)

    latent = sb("latent", [P, NT, 5 * P])

    def latent_items():
        def item(src, bank, half):
            h, l, gain = ((cqh, cql, vcol("q_gain", src, 1)) if src < 3 else (ckh, ckl, vcol("kv_gain", src - 3, 1)))
            b = src if src < 3 else src - 3
            return W[bank][:, half * TOK:(half + 1) * TOK], gain, h[:, b, :], l[:, b, :], bank
        return [item(0, 0, 0), item(2, 1, 0), item(4, 2, 0), item(1, 0, 1), item(3, 1, 1)]

    def down_act(act):
        split = hi_of(act)
        for k in range(2):
            refill(split, ph["down_a"], k, 0)
        act.wait_ge(used[1], 2)
        for t in range(NT):
            act.activation(hn[:, t, 0:MLA_QL], acc[:, t, 0:MLA_QL], ACT.Square, accum_out=stat[:, 4 + t:5 + t]).then_inc(m["sq"], 1)
        for t in range(NT):
            act.activation(hn[:, t, MLA_QL:MLA_QL + MLA_KVL], acc[:, 2 + t, 0:MLA_KVL], ACT.Square,
                           accum_out=stat[:, 6 + t:7 + t]).then_inc(m["sq"], 1)
        for k in range(2):
            refill(split, ph["down_b"], k, 0)
        first_of_next(split, ph["down_b"])
        evac_split_act(act, latent_items(), 3, 0, m, lambda bank: (m["turned"], bank + 1))
        act.wait_ge(m["xl"], 3)
        act.activation(kr_t[:], W[2][:, TOK:2 * TOK], ACT.Copy).then_inc(m["krev"], 1)

    def rotate(dve, chain, out, src, cos, sin, half, a, b):
        dve.tensor_tensor(a[:], src, cos, ALU.mult)
        dve.tensor_tensor(b[:, :, 0:half], src[:, :, half:2 * half], sin[:, :, 0:half], ALU.mult)
        chain(dve.tensor_tensor(b[:, :, half:2 * half], src[:, :, 0:half], sin[:, :, half:2 * half], ALU.mult))
        return dve.tensor_tensor(out, a[:], b[:], ALU.add)

    mla_cos = cst("mla_cos", "p (t r) -> p t r", t=NT)
    mla_sin = cst("mla_sin", "p (t r) -> p t r", t=NT)

    def down_dve(dve):
        split = lo_of(dve)
        for k in range(2):
            refill(split, ph["down_a"], k, 0)
        dve.wait_ge(m["sq"], 4)
        dve.tensor_tensor(mean[:, 4:8], stat[:, 4:8], vcol("norm_scale", 0, 4), ALU.mult).then_inc(m["mean"], 1)
        dve.wait_ge(m["mean"], 1)
        dve.tensor_scalar(mean[:, 4:8], mean[:, 4:8], EPS, None, ALU.add).then_inc(m["mean"], 1)
        dve.memset(rope_pad[:], 0.0).then_inc(m["rope_k"], 1)
        dve.wait_ge(m["rope_k"], 1)
        kr = acc[:, 2:4, MLA_KVL:MLA_KVL + MLA_ROPE]

        def chain(ins):
            ins.then_inc(m["rope_k"], 1)
            dve.wait_ge(m["rope_k"], 2)

        rotate(dve, chain, rope_pad[:, :, 0:MLA_ROPE], kr, mla_cos, mla_sin, 32, rope_a, rope_b).then_inc(m["rope_k"], 1)
        dve.wait_ge(m["root"], 1)
        for t in range(NT):
            dve.tensor_scalar(latent[:, t, 0:MLA_QL], acc[:, t, 0:MLA_QL], stat[:, 12 + t:13 + t], None, ALU.mult).then_inc(m["cn"], 1)
            dve.tensor_scalar(latent[:, t, MLA_QL:5 * P], acc[:, 2 + t, 0:MLA_KVL], stat[:, 14 + t:15 + t], None,
                              ALU.mult).then_inc(m["cn"], 1)
        for k in range(2):
            refill(split, ph["down_b"], k, 0)
        first_of_next(split, ph["down_b"])
        evac_split_dve(dve, latent_items(), 0, m)

    def down_pool(pool):
        pool.wait_ge(m["mean"], 2)
        pool.tensor_tensor(stat[:, 12:16], mean[:, 4:8], power[:, 0:4], ALU.pow).then_inc(m["root"], 1)

    def mla_pe(pe):
        def queries_keys(j):
            chunk_ready(pe, ph["mla"], 0, j)
            chunk_ready(pe, ph["mla"], 1, j)
            if isinstance(j, int) and j == 0:
                pe.wait_ge(m["xl"], 5)
                pe.wait_ge(m["krev"], 1)
            else:
                pe.wait_ge(h["qkev"], j)
            project_t(pe, W[0][:, 0:TOK], 0, 192, 0, (cqh, cql), MLA_QB)
            project_t(pe, W[0][:, TOK:2 * TOK], 1, 256, 0, (ckh, ckl), MLA_KVB).then_inc(m["qk"], 1)

        def rotated_values(j):
            if not (isinstance(j, int) and j == 0):
                pe.wait_ge(h["vev"], j)
            for t in range(NT):
                for b in range(MLA_QB):
                    last = mm3(pe, W[1][:, t * 64:t * 64 + 64], (cqh[:, b, t * P:(t + 1) * P], cql[:, b, t * P:(t + 1) * P]),
                               wslot(0, b * 192 + P, b * 192 + 192), b == 0, b == MLA_QB - 1)
            last.then_inc(used[0], 1)
            for t in range(NT):
                for b in range(MLA_KVB):
                    last = mm3(pe, W[1][:, P + t * P:P + (t + 1) * P],
                               (ckh[:, b, t * P:(t + 1) * P], ckl[:, b, t * P:(t + 1) * P]),
                               wslot(1, b * 256 + P, b * 256 + 256), b == 0, b == MLA_KVB - 1)
            last.then_inc(used[1], 1)

        def turn_rotated(j):
            pe.wait_ge(h["roped"], j + 1)
            for t in range(NT):
                last = pe.transpose(W[3][:, t * P:(t + 1) * P], rope_pad[:, t, :], ident)
            last.then_inc(h["turned"], 1)

        def head(i):
            pe.wait_ge(h["qkev"], i + 1)
            pe.wait_ge(h["turned_ev"], i + 1)
            first = isinstance(i, int) and i == 0
            more = not (isinstance(i, int) and i == HEADS - 1)
            if not first:
                pe.wait_ge(h["ol"], i)
            for t in range(NT):
                out = W[2][:, t * TOK:(t + 1) * TOK]
                pe.matmul(out, q_sb[:, t * P:(t + 1) * P], k_sb[:], start=True, stop=False)
                last = pe.matmul(out, qr_t[:, t * P:(t + 1) * P], kr_t[:], start=False, stop=True)
            last.then_inc(h["s"], 1)
            if not first:
                chunk_ready(pe, ph["mla"], 2, i - 1)
                if isinstance(i, int) and i == 1:
                    rows_out(pe, 2, oh, ol, True, False).then_inc(used[2], 1)
                else:
                    rows_out(pe, 2, oh, ol, False, False).then_inc(used[2], 1)
            if more:
                queries_keys(i + 1)
            pe.wait_ge(h["p"], i + 1)
            for t in range(NT):
                for b in range(NT):
                    last = pe.transpose(W[3][:, b * TOK + t * P:b * TOK + (t + 1) * P], prob[:, t, b * P:(b + 1) * P], ident)
            last.then_inc(h["pt"], 1)
            if more:
                rotated_values(i + 1)
            pe.wait_ge(h["ptev"], i + 1)
            pe.wait_ge(h["vev"], i + 1)
            for b in range(NT):
                last = pe.matmul(W[2][:, 0:TOK], v_sb[:, b, :], prob_t[:, b, :], start=(b == 0), stop=(b == NT - 1))
            last.then_inc(h["pv"], 1)
            if more:
                turn_rotated(i + 1)

        queries_keys(0)
        rotated_values(0)
        turn_rotated(0)
        head(0)
        head(1)
        with pe.Fori(2, HEADS - 1) as r:
            head(pe.snap(r))
        head(HEADS - 1)
        chunk_ready(pe, ph["mla"], 2, HEADS - 1)
        pe.wait_ge(h["ol"], HEADS)
        rows_out(pe, 2, oh, ol, False, True).then_inc(used[2], 1)

    def mla_act(act):
        split = hi_of(act)

        def take_qk(j):
            act.wait_ge(m["qk"], j + 1)
            act.activation(q_sb[:], W[0][:, 0:TOK], ACT.Copy)
            act.activation(k_sb[:], W[0][:, TOK:2 * TOK], ACT.Copy).then_inc(h["qkev"], 1)

        def take_rotated(j):
            act.wait_ge(h["turned"], j + 1)
            act.activation(qr_t[:], W[3][:, 0:TOK], ACT.Copy).then_inc(h["turned_ev"], 1)

        def head(i):
            first = isinstance(i, int) and i == 0
            more = not (isinstance(i, int) and i == HEADS - 1)
            if not more:
                first_of_next(split, ph["mla"])
            act.wait_ge(h["mx"], i + 1)
            for t in range(NT):
                last = act.activation(prob[:, t, :], W[2][:, t * TOK:(t + 1) * TOK], ACT.Exp, bias=soft[:, 4 + t:5 + t],
                                      scale=MLA_SCALE, accum_out=soft[:, 8 + t:9 + t])
            last.then_inc(h["e"], 1)
            if more:
                take_qk(i + 1)
            if not first:
                refill(split, ph["mla"], 2, i - 1)
            act.wait_ge(h["pt"], i + 1)
            act.activation(prob_t[:], W[3][:].rearrange("p (b q) -> p b q", b=NT), ACT.Copy).then_inc(h["ptev"], 1)
            if more:
                refill(split, ph["mla"], 0, i + 1)
                refill(split, ph["mla"], 1, i + 1)
            act.wait_ge(h["pv"], i + 1)
            act.activation(oh[:], W[2][:, 0:TOK], ACT.Copy).then_inc(h["oh"], 1)
            if more:
                take_rotated(i + 1)

        take_qk(0)
        refill(split, ph["mla"], 0, 0)
        refill(split, ph["mla"], 1, 0)
        take_rotated(0)
        over(act, HEADS, head, 2)
        refill(split, ph["mla"], 2, HEADS - 1)

    def mla_dve(dve):
        split = lo_of(dve)

        def rotate_queries(j):
            dve.wait_ge(used[1], ph["mla"].base[1] + j + 1)
            rotate(dve, Chain(dve, h["rope"], 1, j), rope_pad[:, :, 0:MLA_ROPE],
                   W[1][:, 0:P].rearrange("p (t r) -> p t r", t=NT), mla_cos, mla_sin, 32, rope_a, rope_b).then_inc(h["roped"], 1)

        def take_values(j):
            if not (isinstance(j, int) and j == 0):
                dve.wait_ge(h["pv"], j)
            dve.tensor_copy(v_sb[:], W[1][:, P:3 * P].rearrange("p (t c) -> p t c", t=NT)).then_inc(h["vev"], 1)

        def head(i):
            first = isinstance(i, int) and i == 0
            more = not (isinstance(i, int) and i == HEADS - 1)
            if not more:
                first_of_next(split, ph["mla"])
            chain = Chain(dve, h["sm"], 2, i)
            dve.wait_ge(h["s"], i + 1)
            chain(dve.tensor_reduce(soft[:, 0:2], W[2][:].rearrange("p (t k) -> p t k", t=NT), AX.X, ALU.max))
            dve.tensor_scalar(soft[:, 4:6], soft[:, 0:2], -MLA_SCALE, None, ALU.mult).then_inc(h["mx"], 1)
            dve.wait_ge(h["e"], i + 1)
            chain(dve.reciprocal(soft[:, 12:14], soft[:, 8:10]))
            for t in range(NT):
                last = dve.tensor_scalar(prob[:, t, :], prob[:, t, :], soft[:, 12 + t:13 + t], None, ALU.mult)
            last.then_inc(h["p"], 1)
            if not first:
                refill(split, ph["mla"], 2, i - 1)
            if more:
                rotate_queries(i + 1)
                take_values(i + 1)
                refill(split, ph["mla"], 0, i + 1)
                refill(split, ph["mla"], 1, i + 1)
            dve.wait_ge(h["oh"], i + 1)
            dve.tensor_tensor(ol[:], W[2][:, 0:TOK], oh[:], ALU.subtract).then_inc(h["ol"], 1)

        rotate_queries(0)
        take_values(0)
        refill(split, ph["mla"], 0, 0)
        refill(split, ph["mla"], 1, 0)
        over(dve, HEADS, head, 2)
        refill(split, ph["mla"], 2, HEADS - 1)

    f = [sems(f"f{j}", "g_mid v_mid g_tap v_tap gelu h32 hh hl") for j in range(2)]
    cg = [sb(f"cg{j}", [P, TOK]) for j in range(2)]
    cv = [sb(f"cv{j}", [P, TOK]) for j in range(2)]
    gelu = [sb(f"gelu{j}", [P, TOK]) for j in range(2)]
    h32 = [sb(f"h32_{j}", [P, TOK]) for j in range(2)]
    hh = [sb(f"hh{j}", [P, TOK], F32R) for j in range(2)]
    hl = [sb(f"hl{j}", [P, TOK], F32R) for j in range(2)]

    def ffn_pe(pe, layer):
        p = (ph["ffn0"], ph["ffn1"])[layer]
        done = layer * FFN_STEPS
        pe.wait_ge(n_["xl"], KB * (2 * layer + 2))

        def up(j, i):
            for gate, bank in ((1, 2 * j), (0, 2 * j + 1)):
                chunk_ready(pe, p, bank, i)
                if not (isinstance(i, int) and i + done == 0):
                    pe.wait_ge(f[j]["g_tap"] if gate else f[j]["v_tap"], 2 * (i + done))
                project_t(pe, W[bank][:, 0:TOK], bank).then_inc(used[bank], 1)

        def down(j, i, start=False, stop=False):
            chunk_ready(pe, p, 4 + j, i)
            pe.wait_ge(f[j]["hl"], i + done + 1)
            rows_out(pe, 4 + j, hh[j], hl[j], start, stop).then_inc(used[4 + j], 1)

        def step(i):
            up(0, i)
            if not (isinstance(i, int) and i == 0):
                down(1, i - 1)
            up(1, i)
            down(0, i, start=isinstance(i, int) and i == 0)

        over(pe, FFN_STEPS, step)
        down(1, FFN_STEPS - 1, stop=True)

    def ffn_taps(layer, i, j, value, tap, lo_, hi_=None):
        at = layer * FFN_STEPS * 16 + (2 * j + value) * 4 + tap
        return vcol("ffn_conv", i * 16 + at, 1)

    def ffn_act(act, layer):
        p = (ph["ffn0"], ph["ffn1"])[layer]
        done = layer * FFN_STEPS
        split = hi_of(act)

        def block(j, i, between):
            for value in range(2):
                bank, s = 2 * j + value, f[j]
                act.wait_ge(used[bank], p.base[bank] + i + 1)
                if value and not (isinstance(i, int) and i + done == 0):
                    act.wait_ge(s["h32"], i + done)
                act.activation((cg, cv)[value][j][:], W[bank][:, 0:TOK], ACT.Identity,
                               scale=ffn_taps(layer, i, j, value, 1, 0),
                               bias=ffn_taps(layer, i, j, value, 3, 0)).then_inc((s["g_mid"], s["v_mid"])[value], 1)
                refill(split, p, bank, i)
            act.wait_ge(f[j]["g_tap"], 2 * (i + done) + 2)
            act.activation(gelu[j][:], cg[j][:], ACT.Gelu_apprx_tanh).then_inc(f[j]["gelu"], 1)
            between()
            act.wait_ge(f[j]["h32"], i + done + 1)
            if not (isinstance(i, int) and i + done == 0):
                act.wait_ge(used[4 + j], used_before(i, j))
            act.activation(hh[j][:], h32[j][:], ACT.Copy).then_inc(f[j]["hh"], 1)

        def used_before(i, j):
            return p.base[4 + j] + i

        def step(i):
            if isinstance(i, int) and i == FFN_STEPS - 1:
                first_of_next(split, p)
            block(0, i, lambda: None if isinstance(i, int) and i == 0 else refill(split, p, 5, i - 1))
            block(1, i, lambda: refill(split, p, 4, i))

        over(act, FFN_STEPS, step)
        refill(split, p, 5, FFN_STEPS - 1)

    def ffn_dve(dve, layer):
        p = (ph["ffn0"], ph["ffn1"])[layer]
        done = layer * FFN_STEPS
        split = lo_of(dve)

        def block(j, i):
            for value in range(2):
                bank, s = 2 * j + value, f[j]
                mid, tap, c = (s["g_mid"], s["v_mid"])[value], (s["g_tap"], s["v_tap"])[value], (cg, cv)[value][j]
                dve.wait_ge(mid, i + done + 1)
                dve.scalar_tensor_tensor(c[:, 1:TOK], W[bank][:, 0:TOK - 1], ffn_taps(layer, i, j, value, 0, 0),
                                         c[:, 1:TOK], ALU.mult, ALU.add).then_inc(tap, 1)
                dve.wait_ge(tap, 2 * (i + done) + 1)
                dve.scalar_tensor_tensor(c[:, 0:TOK - 1], W[bank][:, 1:TOK], ffn_taps(layer, i, j, value, 2, 0),
                                         c[:, 0:TOK - 1], ALU.mult, ALU.add).then_inc(tap, 1)
                refill(split, p, bank, i)

        def step(i):
            if isinstance(i, int) and i == FFN_STEPS - 1:
                first_of_next(split, p)
            block(0, i)
            if not (isinstance(i, int) and i == 0):
                refill(split, p, 5, i - 1)
            block(1, i)
            refill(split, p, 4, i)

        over(dve, FFN_STEPS, step)
        refill(split, p, 5, FFN_STEPS - 1)

    def ffn_pool(pool, layer):
        p = (ph["ffn0"], ph["ffn1"])[layer]
        done = layer * FFN_STEPS
        split = lo_of(pool, True)

        def hidden(j, i):
            s = f[j]
            pool.wait_ge(s["gelu"], i + done + 1)
            pool.wait_ge(s["v_tap"], 2 * (i + done) + 2)
            if not (isinstance(i, int) and i + done == 0):
                pool.wait_ge(s["hh"], i + done)
            pool.tensor_tensor(h32[j][:], gelu[j][:], cv[j][:], ALU.mult).then_inc(s["h32"], 1)
            pool.wait_ge(s["hh"], i + done + 1)
            pool.tensor_tensor(hl[j][:], h32[j][:], hh[j][:], ALU.subtract).then_inc(s["hl"], 1)

        def step(i):
            if isinstance(i, int) and i == FFN_STEPS - 1:
                first_of_next(split, p)
            refill(split, p, 0, i)
            refill(split, p, 1, i)
            hidden(0, i)
            if not (isinstance(i, int) and i == 0):
                refill(split, p, 5, i - 1)
            refill(split, p, 2, i)
            refill(split, p, 3, i)
            hidden(1, i)
            refill(split, p, 4, i)

        over(pool, FFN_STEPS, step)
        refill(split, p, 5, FFN_STEPS - 1)

    d = sems("d", "lam sq ms root on ot")
    qz = [sb(f"qz{j}", [P, TOK]) for j in range(2)]
    lam = sb("lam", [P, 8])
    lam_prod = sb("lam_prod", [P, 2, 64])
    sub = sb("sub", [P, 1])
    onorm = sb("onorm", [P, NT, P])

    def diff_setup_dve(dve):
        for j in range(2):
            dve.memset(qz[j][:], 0.0)
        dve.tensor_scalar(sub[:], vcol("sub_gain"), 1.0 - LAM_INIT, None, ALU.mult)
        lp = vcol("lam").rearrange("p (a b c) -> p a b c", a=2, b=2)
        dve.tensor_tensor(lam_prod[:], lp[:, :, 0, :], lp[:, :, 1, :], ALU.mult).then_inc(d["lam"], 1)
        dve.wait_ge(d["lam"], 1)
        dve.tensor_reduce(lam[:, 0:2], lam_prod[:], AX.X, ALU.add).then_inc(d["lam"], 1)
        dve.wait_ge(d["lam"], 3)
        dve.tensor_tensor(lam[:, 4:5], lam[:, 3:4], lam[:, 2:3], ALU.subtract).then_inc(d["lam"], 1)
        dve.wait_ge(d["lam"], 4)
        dve.tensor_scalar(lam[:, 5:6], lam[:, 4:5], -LAM_INIT, None, ALU.add).then_inc(d["lam"], 1)

    def diff_setup_act(act):
        act.wait_ge(d["lam"], 2)
        act.activation(lam[:, 2:4], lam[:, 0:2], ACT.Exp).then_inc(d["lam"], 1)

    def diff_pe(pe):
        pe.wait_ge(n_["xl"], KB * 3)

        def queries_keys(j):
            if not (isinstance(j, int) and j == 0):
                pe.wait_ge(h["qkev"], j + DIFF_SEEN)
            for k in range(2):
                chunk_ready(pe, ph["diff"], k, j)
                project_t(pe, W[0][:, k * TOK:(k + 1) * TOK], k).then_inc(used[k], 1)

        def values(j):
            chunk_ready(pe, ph["diff"], 2, j)
            for t in range(NT):
                for b in range(KB):
                    last = mm3(pe, W[1][:, t * P:(t + 1) * P], (xh[:, b, t * P:(t + 1) * P], xl[:, b, t * P:(t + 1) * P]),
                               wslot(2, b * P, (b + 1) * P), b == 0, b == KB - 1)
            last.then_inc(used[2], 1)

        def turn_result(i):
            pe.wait_ge(d["on"], i + 1)
            pe.wait_ge(h["vev"], (i + 2 if not (isinstance(i, int) and i == HEADS - 1) else HEADS) + DIFF_SEEN)
            for t in range(NT):
                last = pe.transpose(W[1][:, t * P:(t + 1) * P], onorm[:, t, :], ident)
            last.then_inc(d["ot"], 1)

        def add_output(i):
            chunk_ready(pe, ph["diff"], 3, i)
            pe.wait_ge(h["ol"], i + 1 + DIFF_SEEN)
            int_ = isinstance(i, int)
            rows_out(pe, 3, oh, ol, int_ and i == 0, int_ and i == HEADS - 1).then_inc(used[3], 1)

        def head(i):
            first = isinstance(i, int) and i == 0
            more = not (isinstance(i, int) and i == HEADS - 1)
            pe.wait_ge(h["qkev"], i + 1 + DIFF_SEEN)
            if not first:
                pe.wait_ge(h["ptev"], i + DIFF_SEEN)
                pe.wait_ge(d["on"], i)
            for j in range(2):
                for t in range(NT):
                    last = pe.matmul(W[2 + j][:, t * TOK:(t + 1) * TOK], qz[j][:, t * P:(t + 1) * P], k_sb[:],
                                     start=True, stop=True)
            last.then_inc(h["s"], 1)
            if not first:
                turn_result(i - 1)
            if more:
                queries_keys(i + 1)
            if not first:
                add_output(i - 1)
            pe.wait_ge(h["p"], i + 1 + DIFF_SEEN)
            for t in range(NT):
                for b in range(NT):
                    last = pe.transpose(W[2][:, b * TOK + t * P:b * TOK + (t + 1) * P], prob[:, t, b * P:(b + 1) * P], ident)
            last.then_inc(h["pt"], 1)
            if more:
                if not first:
                    pe.wait_ge(h["ol"], i + DIFF_SEEN)
                values(i + 1)
            pe.wait_ge(h["ptev"], i + 1 + DIFF_SEEN)
            pe.wait_ge(h["vev"], i + 1 + DIFF_SEEN)
            for t in range(NT):
                for b in range(NT):
                    last = pe.matmul(W[3][:, t * P:(t + 1) * P], prob_t[:, b, t * P:(t + 1) * P], v_sb[:, b, :],
                                     start=(b == 0), stop=(b == NT - 1))
            last.then_inc(h["pv"], 1)

        queries_keys(0)
        values(0)
        head(0)
        head(1)
        with pe.Fori(2, HEADS - 1) as r:
            head(pe.snap(r))
        head(HEADS - 1)
        turn_result(HEADS - 1)
        add_output(HEADS - 1)

    def diff_act(act):
        split = hi_of(act)

        def take_qk(j):
            act.wait_ge(used[1], ph["diff"].base[1] + j + 1)
            act.activation(qz[0][0:64, :], W[0][0:64, 0:TOK], ACT.Copy)
            act.activation(qz[1][64:P, :], W[0][64:P, 0:TOK], ACT.Copy)
            act.activation(k_sb[:], W[0][:, TOK:2 * TOK], ACT.Copy).then_inc(h["qkev"], 1)

        def result_high(i):
            act.wait_ge(d["ot"], i + 1)
            act.activation(oh[:], W[1][:, 0:TOK], ACT.Copy, scale=sub[:]).then_inc(h["oh"], 1)

        def head(i):
            first = isinstance(i, int) and i == 0
            more = not (isinstance(i, int) and i == HEADS - 1)
            if not more:
                first_of_next(split, ph["diff"])
            if not first:
                result_high(i - 1)
            act.wait_ge(h["mx"], i + 1 + DIFF_SEEN)
            for k in range(4):
                last = act.activation(prob[:, k, :], prob[:, k, :], ACT.Exp, bias=soft[:, 4 + k:5 + k],
                                      scale=DIFF_SCALE, accum_out=soft[:, 8 + k:9 + k])
            last.then_inc(h["e"], 1)
            if more:
                refill(split, ph["diff"], 0, i + 1)
                take_qk(i + 1)
                refill(split, ph["diff"], 1, i + 1)
            act.wait_ge(h["pt"], i + 1 + DIFF_SEEN)
            act.activation(prob_t[:], W[2][:].rearrange("p (b q) -> p b q", b=NT), ACT.Copy).then_inc(h["ptev"], 1)
            if not first:
                refill(split, ph["diff"], 3, i - 1)
            if more:
                refill(split, ph["diff"], 2, i + 1)
            act.wait_ge(h["pv"], i + 1 + DIFF_SEEN)
            for t in range(NT):
                last = act.activation(junk[:, t * P:(t + 1) * P], W[3][:, t * P:(t + 1) * P], ACT.Square, accum_out=stat[:, 4 + t:5 + t])
            last.then_inc(d["sq"], 1)

        act.wait_ge(d["lam"], 1)
        refill(split, ph["diff"], 0, 0)
        take_qk(0)
        refill(split, ph["diff"], 1, 0)
        refill(split, ph["diff"], 2, 0)
        over(act, HEADS, head, 2)
        result_high(HEADS - 1)
        refill(split, ph["diff"], 3, HEADS - 1)

    def diff_dve(dve):
        split = lo_of(dve)
        dist = cst("dist")

        def take_values(j):
            dve.wait_ge(used[2], ph["diff"].base[2] + j + 1)
            if not (isinstance(j, int) and j == 0):
                dve.wait_ge(h["pv"], j + DIFF_SEEN)
            dve.tensor_copy(v_sb[:], W[1][:, 0:TOK].rearrange("p (t c) -> p t c", t=NT)).then_inc(h["vev"], 1)

        def result_low(i):
            dve.wait_ge(h["oh"], i + 1 + DIFF_SEEN)
            dve.scalar_tensor_tensor(ol[:], W[1][:, 0:TOK], sub[:], oh[:], ALU.mult, ALU.subtract).then_inc(h["ol"], 1)

        def head(i):
            first = isinstance(i, int) and i == 0
            more = not (isinstance(i, int) and i == HEADS - 1)
            if not more:
                first_of_next(split, ph["diff"])
            chain = Chain(dve, h["sm"], 5, i, 2 * HEADS)
            dve.wait_ge(h["s"], i + 1 + DIFF_SEEN)
            for j in range(2):
                last = dve.scalar_tensor_tensor(prob[:, 2 * j:2 * j + 2, :].rearrange("p t k -> p (t k)"), dist,
                                                vcol("slope", i, 1), W[2 + j][:], ALU.mult, ALU.add)
            chain(last)
            chain(dve.tensor_reduce(soft[:, 0:4], prob[:], AX.X, ALU.max))
            dve.tensor_scalar(soft[:, 4:8], soft[:, 0:4], -DIFF_SCALE, None, ALU.mult).then_inc(h["mx"], 1)
            if not first:
                result_low(i - 1)
            dve.wait_ge(h["e"], i + 1 + DIFF_SEEN)
            chain(dve.reciprocal(soft[:, 12:16], soft[:, 8:12]))
            chain(dve.tensor_scalar(soft[:, 14:16], soft[:, 14:16], lam[:, 5:6], None, ALU.mult))
            for t in range(NT):
                last = dve.tensor_scalar(prob[:, t, :], prob[:, t, :], soft[:, 12 + t:13 + t], None, ALU.mult)
            chain(last)
            for t in range(NT):
                last = dve.scalar_tensor_tensor(prob[:, t, :], prob[:, 2 + t, :], soft[:, 14 + t:15 + t], prob[:, t, :],
                                                ALU.mult, ALU.add)
            last.then_inc(h["p"], 1)
            if more:
                refill(split, ph["diff"], 0, i + 1)
                refill(split, ph["diff"], 1, i + 1)
            if not first:
                refill(split, ph["diff"], 3, i - 1)
            if more:
                take_values(i + 1)
                refill(split, ph["diff"], 2, i + 1)
            dve.wait_ge(d["sq"], i + 1)
            dve.tensor_scalar(mean[:, 4:6], stat[:, 4:6], 1.0 / P, EPS, ALU.mult, ALU.add).then_inc(d["ms"], 1)
            dve.wait_ge(d["root"], i + 1)
            for t in range(NT):
                last = dve.tensor_scalar(onorm[:, t, :], W[3][:, t * P:(t + 1) * P], stat[:, 12 + t:13 + t], None, ALU.mult)
            last.then_inc(d["on"], 1)

        dve.wait_ge(d["lam"], 5)
        for k in (0, 1):
            refill(split, ph["diff"], k, 0)
        take_values(0)
        refill(split, ph["diff"], 2, 0)
        over(dve, HEADS, head, 2)
        result_low(HEADS - 1)
        refill(split, ph["diff"], 3, HEADS - 1)

    def diff_pool(pool):
        split = lo_of(pool, True)

        def head(i):
            first = isinstance(i, int) and i == 0
            more = not (isinstance(i, int) and i == HEADS - 1)
            if not more:
                first_of_next(split, ph["diff"])
            if more:
                refill(split, ph["diff"], 0, i + 1)
                refill(split, ph["diff"], 1, i + 1)
            if not first:
                refill(split, ph["diff"], 3, i - 1)
            if more:
                refill(split, ph["diff"], 2, i + 1)
            pool.wait_ge(d["ms"], i + 1)
            pool.tensor_tensor(stat[:, 12:14], mean[:, 4:6], power[:, 0:2], ALU.pow).then_inc(d["root"], 1)

        for k in (0, 1, 2):
            refill(split, ph["diff"], k, 0)
        over(pool, HEADS, head, 2)
        refill(split, ph["diff"], 3, HEADS - 1)

    close_scope()

    z_ = sems("z", "pe act dve")
    gate = {n: sb(f"gate_{n}", [P, HEADS, NT]) for n in
            "z neg abs e ln sp ea g cum eg th beta vbeta tot bg kdx kd".split()}
    cum_all = sb("cum_all", [P, 2 * HEADS, P])
    gdn_gain = sb("gdn_gain", [P, 1])
    obh, obl = sb("obh", [P, HEADS, TOK], F32R), sb("obl", [P, HEADS, TOK], F32R)

    def flat(t):
        return t[:].rearrange("p h t -> p (h t)")

    def gates_pe(pe):
        pe.wait_ge(n_["xl"], KB * 5)
        chunk_ready(pe, ph["gates"], 4, 0)
        for t in range(NT):
            for b in range(KB):
                last = mm3(pe, W[0][:, t * 16:(t + 1) * 16], (xh[:, b, t * P:(t + 1) * P], xl[:, b, t * P:(t + 1) * P]),
                           wslot(4, b * 16, (b + 1) * 16), b == 0, b == KB - 1)
        last.then_inc(used[4], 1)
        pe.wait_ge(z_["dve"], 5)
        pe.matmul(W[1][:, 0:16], cst("upper"), flat(gate["g"]), start=True, stop=True)
        pe.matmul(W[1][:, 16:32], cst("ones"), flat(gate["g"]), start=True, stop=True).then_inc(z_["pe"], 1)
        for c in range(2 * HEADS):
            last = pe.matmul(acc[:, c // 4, (c % 4) * P:(c % 4 + 1) * P], flat(gate["g"])[:, c:c + 1].to_broadcast([P, P]),
                             cst("upper"), start=True, stop=True)
        last.then_inc(z_["pe"], 1)

    def gates_act(act):
        act.wait_ge(z_["dve"], 1)
        act.activation(gate["th"][:], W[0][:, 0:32].rearrange("p (t x) -> p x t", t=NT)[:, 0:8, :], ACT.Tanh,
                       scale=0.5).then_inc(z_["act"], 1)
        act.wait_ge(z_["dve"], 3)
        act.activation(gate["e"][:], gate["abs"][:], ACT.Exp, scale=-1.0).then_inc(z_["act"], 1)
        act.activation(flat(gate["ea"]), vcol("a_log"), ACT.Exp).then_inc(z_["act"], 1)
        act.wait_ge(z_["act"], 2)
        act.activation(gate["ln"][:], gate["e"][:], ACT.Ln, bias=1.0).then_inc(z_["act"], 1)
        act.wait_ge(z_["dve"], 10)
        act.activation(gate["eg"][:], gate["cum"][:], ACT.Exp).then_inc(z_["act"], 1)
        act.activation(gate["kd"][:], gate["kdx"][:], ACT.Exp).then_inc(z_["act"], 1)
        act.wait_ge(z_["pe"], 2)
        act.activation(cum_all[:], acc[:].rearrange("p a (c k) -> p (a c) k", c=4), ACT.Copy).then_inc(z_["act"], 1)

    def gates_dve(dve):
        dve.wait_ge(used[4], ph["gates"].base[4] + 1)
        dec = W[0][:, 0:32].rearrange("p (t x) -> p x t", t=NT)[:, 8:16, :]
        dve.tensor_tensor(gate["z"][:], dec, vcol("dt").rearrange("p (h t) -> p h t", t=NT), ALU.add).then_inc(z_["dve"], 1)
        dve.wait_ge(z_["dve"], 1)
        dve.tensor_scalar(gate["neg"][:], gate["z"][:], -1.0, None, ALU.mult).then_inc(z_["dve"], 1)
        dve.wait_ge(z_["dve"], 2)
        dve.tensor_tensor(gate["abs"][:], gate["z"][:], gate["neg"][:], ALU.max).then_inc(z_["dve"], 1)
        dve.wait_ge(z_["act"], 4)
        dve.scalar_tensor_tensor(gate["sp"][:], gate["z"][:], 0.0, gate["ln"][:], ALU.max, ALU.add).then_inc(z_["dve"], 1)
        dve.wait_ge(z_["dve"], 4)
        dve.scalar_tensor_tensor(gate["g"][:], gate["sp"][:], -1.0, gate["ea"][:], ALU.mult, ALU.mult).then_inc(z_["dve"], 1)
        dve.tensor_scalar(gate["beta"][:], gate["th"][:], 1.0, 0.5, ALU.add, ALU.mult).then_inc(z_["dve"], 1)
        dve.wait_ge(z_["dve"], 6)
        dve.tensor_scalar(gate["vbeta"][:], gate["beta"][:], 0.5, None, ALU.mult).then_inc(z_["dve"], 1)
        dve.tensor_scalar(gdn_gain[:], vcol("gdn_gain"), 0.5, None, ALU.mult).then_inc(z_["dve"], 1)
        dve.wait_ge(z_["pe"], 1)
        dve.tensor_copy(flat(gate["cum"]), W[1][:, 0:16]).then_inc(z_["dve"], 1)
        dve.wait_ge(z_["dve"], 9)
        dve.tensor_tensor(flat(gate["kdx"]), W[1][:, 16:32], flat(gate["cum"]), ALU.subtract).then_inc(z_["dve"], 1)
        dve.wait_ge(z_["act"], 5)
        dve.tensor_tensor(gate["bg"][:], gate["eg"][:], gate["beta"][:], ALU.mult).then_inc(z_["dve"], 1)
        dve.wait_ge(z_["act"], 6)
        dve.wait_ge(z_["dve"], 11)

    taps = [sems(f"c{x}", "mid tap th silu" if x < 3 else "tap th") for x in range(4)]
    e_ = sems("e", "turned sq mean root tk back backev dd exp lu be kk mk mt mtev init_g bm init_v "
              "xm tt x t f1 f1ev f2 f2ev f3 f3ev f4 osq oss om oroot on ot o32 oh ol chain")
    tanh_ = [sb(f"tanh{x}", [P, TOK]) for x in range(4)]
    open_scope()
    conv = [sb(f"conv{x}", [P, TOK]) for x in range(3)]
    silu2 = sb("silu2", [P, 6, TOK])
    z2 = hn[:].rearrange("p t (h k) -> p (t h) k", k=TOK)
    ssq = sb("ssq", [P, 8])
    ssq4, mean4, root4 = sb("ssq4", [P, 4]), sb("mean4", [P, 4]), sb("root4", [P, 4])
    mean8, root8, fac8 = sb("mean8", [P, 8]), sb("root8", [P, 8]), sb("fac8", [P, 8])
    sq = sb("sq", [P, 8, P])
    qk_tok = sb("qk_tok", [P, 2, 4, P])
    kdec, kbg, qdec = sb("kdec", [P, 2, P]), sb("kbg", [P, 2, P]), sb("qdec", [P, 2, P])
    vbeta = sb("vbeta", [P, 4, P])
    qk_t = silu2[:, 0:4, :].rearrange("p (e x) (c k) -> p e (x c) k", e=2, c=2)
    qdec_t = sb("qdec_t", [P, 2, P])
    dec_l, dec_u = sb("dec_l", [P, 4, P]), sb("dec_u", [P, 4, P])
    mask_e = sb("mask_e", [P, 2, 2, 2, P])
    mk = sb("mk", [P, 2, 2, 2, P])
    mt = sb("mt", [P, 4, P])
    inv = sb("inv", [P, 2, 4, P])
    bm = sb("bm", [P, 2, 4, P])
    dcum = bm[:, 0, :, :]
    xm = sb("xm", [P, 4, P])
    vnew = sb("vnew", [P, 2, 2, P])
    nwt = sb("nwt", [P, 2, P])
    state = sb("state", [P, 2, P])
    ogn = sb("ogn", [P, 4, P])
    og32 = sb("og32", [P, 2, TOK])

    def quad(bank):
        return bank[:].rearrange("p (a k) -> p a k", a=4)

    A = [acc[:, k, :] for k in range(4)]
    level_of = cst("levels", "p (l k) -> p l k", l=LEVELS)
    BLOCKS = [(x, e) for e in range(2) for x in range(4)]

    def gdn_block(pe, x, e, j, part):
        b_ = 2 * j + e
        if part == 0:
            chunk_ready(pe, ph["gdn"], x, b_)
            if not (isinstance(b_, int) and b_ == 0):
                pe.wait_ge(taps[x]["tap"], 3 * b_ if x < 3 else b_)
        for s in range(8 * part, 8 * part + 8):
            b, term = divmod(s, 3)
            l, r = ((high, xh), (high, xl), (low, xh))[term]
            last = pe.matmul(W[x][:, 0:TOK], l[x][:, b * P:(b + 1) * P], r[:, b, :], start=(s == 0), stop=(s == 23))
        if part == 2:
            last.then_inc(used[x], 1)

    def block_act(act, split, x, e, j):
        b_ = 2 * j + e
        act.wait_ge(used[x], ph["gdn"].base[x] + b_ + 1)
        if x < 3:
            if not (isinstance(b_, int) and b_ == 0):
                act.wait_ge(taps[x]["silu"], b_)
            act.activation(conv[x][:], W[x][:, 0:TOK], ACT.Copy, scale=conv_tap(b_, x, 3)).then_inc(taps[x]["mid"], 1)
            refill(split, ph["gdn"], x, b_)
            act.wait_ge(taps[x]["tap"], 3 * b_ + 3)
            act.activation(tanh_[x][:], conv[x][:], ACT.Tanh, scale=0.5).then_inc(taps[x]["th"], 1)
        else:
            if not (isinstance(b_, int) and b_ == 0):
                act.wait_ge(taps[x]["tap"], b_)
            act.activation(tanh_[x][:], W[x][:, 0:TOK], ACT.Tanh, scale=0.5).then_inc(taps[x]["th"], 1)
            refill(split, ph["gdn"], x, b_)

    def conv_tap(b_, x, tap):
        return vcol("conv", b_ * 12 + (x * 4 + tap), 1)

    def block_dve(dve, split, x, e, j):
        b_ = 2 * j + e
        if x < 3:
            dve.wait_ge(taps[x]["mid"], b_ + 1)
            for n, back in enumerate((1, 2, 3)):
                dve.scalar_tensor_tensor(conv[x][:, back:TOK], W[x][:, 0:TOK - back], conv_tap(b_, x, 3 - back),
                                         conv[x][:, back:TOK], ALU.mult, ALU.add).then_inc(taps[x]["tap"], 1)
                if n < 2:
                    dve.wait_ge(taps[x]["tap"], 3 * b_ + n + 1)
            refill(split, ph["gdn"], x, b_)
            dve.wait_ge(taps[x]["th"], b_ + 1)
            dve.scalar_tensor_tensor(silu2[:, 3 * e + x, :], tanh_[x][:], 1.0, conv[x][:], ALU.add, ALU.mult).then_inc(taps[x]["silu"], 1)
        else:
            dve.wait_ge(taps[x]["th"], b_ + 1)
            at = b_ if isinstance(b_, int) else None
            dst = z2[:, at, :] if at is not None else z2[:, bass.ds(b_, 1), :].rearrange("p a k -> p (a k)")
            dve.scalar_tensor_tensor(dst, tanh_[x][:], 1.0, W[x][:, 0:TOK], ALU.add, ALU.mult).then_inc(taps[x]["tap"], 1)
            refill(split, ph["gdn"], x, b_)

    def is0(j):
        return isinstance(j, int) and j == 0

    def turn_pe(pe, j):
        for x in range(3):
            pe.wait_ge(taps[x]["silu"], 2 * j + 2)
        for e in range(2):
            for x in range(2):
                for t in range(NT):
                    pe.transpose(W[e][:, (2 * x + t) * P:(2 * x + t + 1) * P], silu2[:, 3 * e + x, t * P:(t + 1) * P], ident)
        for e in range(2):
            for t in range(NT):
                last = pe.transpose(W[2][:, (2 * e + t) * P:(2 * e + t + 1) * P], silu2[:, 3 * e + 2, t * P:(t + 1) * P], ident)
        last.then_inc(e_["turned"], 1)

    def back_pe(pe, j):
        pe.wait_ge(e_["tk"], j + 1)
        pe.wait_ge(taps[3]["tap"], 2 * j + 2)
        for e in range(2):
            for c in range(4):
                pe.transpose(W[e][:, c * P:(c + 1) * P], qk_tok[:, e, c, :], ident)
        for e in range(2):
            last = pe.transpose(W[3][:, e * P:(e + 1) * P], qdec[:, e, :], ident)
        last.then_inc(e_["back"], 1)

    def products_pe(pe, j):
        pe.wait_ge(e_["backev"], j + 1)
        if is0(j):
            pe.wait_ge(z_["act"], 7)
        for e in range(2):
            for which in range(2):
                for t in range(NT):
                    c = 2 * which + t
                    last = pe.matmul(A[2 + e][:, c * P:(c + 1) * P], qk_t[:, e, 2 + t, :],
                                     qk_t[:, e, 2 + t if which == 0 else t, :], start=True, stop=True)
        last.then_inc(e_["kk"], 1)
        pe.wait_ge(e_["mk"], j + 1)
        for e in range(2):
            for t in range(NT):
                last = pe.transpose(W[2][:, (2 * e + t) * P:(2 * e + t + 1) * P], mk[:, e, 0, t, :], ident)
        last.then_inc(e_["mt"], 1)

    def squares_act(act, j, e):
        if e == 0:
            act.wait_ge(e_["turned"], j + 1)
        act.activation(sq[:, 4 * e:4 * e + 4, :], quad(W[e]), ACT.Square).then_inc(e_["sq"], 1)

    def decay_act(act, j):
        act.wait_ge(e_["dd"], j + 1)
        if not is0(j):
            act.wait_ge(e_["be"], j)
        act.activation(dec_l[:], dec_l[:], ACT.Exp, scale=-1.0)
        act.activation(dec_u[:], dec_u[:], ACT.Exp).then_inc(e_["exp"], 1)

    def back_act(act, j):
        act.wait_ge(e_["back"], j + 1)
        for e in range(2):
            act.activation(qk_t[:, e, :, :], quad(W[e]), ACT.Copy)
        act.activation(qdec_t[:], W[3][:, 0:TOK].rearrange("p (e k) -> p e k", e=2), ACT.Copy).then_inc(e_["backev"], 1)

    def mt_act(act, j):
        act.wait_ge(e_["mt"], j + 1)
        act.activation(mt[:], quad(W[2]), ACT.Copy).then_inc(e_["mtev"], 1)

    def gate_at(name, j, step=1, chunk=None):
        v = flat(gate[name])
        if isinstance(j, int):
            v = v[:, 4 * j:4 * j + 4]
        else:
            v = v[:, bass.ds(j * 4, 4)]
        return v if chunk is None else v.rearrange("p (h t) -> p h t", t=NT)[:, :, chunk]

    def prepare_dve(dve, j):
        dve.wait_ge(e_["sq"], 2 * j + 2)
        chain = Chain(dve, e_["chain"], 4, j)
        chain(dve.tensor_reduce(ssq[:], sq[:], AX.X, ALU.add))
        dve.tensor_scalar(mean8[:], ssq[:], 0.25, EPS, ALU.mult, ALU.add).then_inc(e_["mean"], 1)
        if is0(j):
            dve.wait_ge(z_["act"], 7)
        c = cum_all[:, 4 * j:4 * j + 4, :] if isinstance(j, int) else cum_all[:, bass.ds(j * 4, 4), :]
        chain(dve.tensor_tensor(dcum, c, spread(gate_at("cum", j), P), ALU.subtract))
        if not is0(j):
            dve.wait_ge(e_["be"], j)
        dve.tensor_scalar(dec_l[:], dcum, 0.0, None, ALU.max)
        dve.tensor_scalar(dec_u[:], dcum, 0.0, None, ALU.min).then_inc(e_["dd"], 1)
        dve.wait_ge(e_["root"], j + 1)
        chain(dve.tensor_tensor(fac8[:], root8[:], vcol("l2_factor"), ALU.mult))
        for e in range(2):
            last = dve.tensor_tensor(qk_tok[:, e, :, :], quad(W[e]), spread(fac8[:, 4 * e:4 * e + 4], P), ALU.mult)
        chain(last)
        if not is0(j):
            dve.wait_ge(e_["f4"], j)
        dve.tensor_tensor(kdec[:], qk_tok[:, :, 2, :], spread(gate_at("kd", j, chunk=0), P), ALU.mult)
        dve.tensor_tensor(kbg[:], qk_tok[:, :, 3, :], spread(gate_at("bg", j, chunk=1), P), ALU.mult)
        dve.tensor_tensor(qdec[:], qk_tok[:, :, 1, :], spread(gate_at("eg", j, chunk=1), P), ALU.mult)
        dve.tensor_tensor(vbeta[:], quad(W[2]), spread(gate_at("vbeta", j), P), ALU.mult).then_inc(e_["tk"], 1)

    def masked_dve(dve, j):
        dve.wait_ge(e_["kk"], j + 1)
        dve.wait_ge(e_["be"], j + 1)
        for e in range(2):
            last = dve.tensor_tensor(mk[:, e, :, :, :].rearrange("p a t k -> p (a t) k"), quad(A[2 + e]),
                                     mask_e[:, e, :, :, :].rearrange("p a t k -> p (a t) k"), ALU.mult)
        last.then_inc(e_["mk"], 1)
        dve.wait_ge(e_["mtev"], j + 1)
        chain = Chain(dve, e_["init_v"], 2, j)
        chain(dve.tensor_tensor(bm[:, 1, :, :], mt[:], repeat(cst("level1_t"), 4), ALU.mult))
        chain(dve.tensor_tensor(inv[:, 1, :, :], repeat(ident, 4), bm[:, 1, :, :], ALU.subtract))

    def prepare_pool(pool, j):
        pool.wait_ge(e_["mean"], j + 1)
        pool.tensor_tensor(root8[:], mean8[:], power[:], ALU.pow).then_inc(e_["root"], 1)
        pool.wait_ge(e_["exp"], j + 1)
        if not is0(j):
            pool.wait_ge(e_["mk"], j)
        for e in range(2):
            pool.tensor_tensor(mask_e[:, e, 1, :, :], dec_u[:, 2 * e:2 * e + 2, :], repeat(cst("upper"), NT), ALU.mult)
        last = pool.tensor_tensor(dec_l[:], dec_l[:], repeat(cst("strict_lower"), 4), ALU.mult)
        last.then_inc(e_["lu"], 1)
        pool.wait_ge(e_["lu"], j + 1)
        for e in range(2):
            last = pool.tensor_tensor(mask_e[:, e, 0, :, :], dec_l[:, 2 * e:2 * e + 2, :],
                                      spread(gate_at("beta", j)[:, 2 * e:2 * e + 2], P), ALU.mult)
        last.then_inc(e_["be"], 1)

    def init_pool(pool, j):
        pool.wait_ge(e_["mk"], j + 1)
        if not is0(j):
            pool.wait_ge(e_["f3"], j)
        for e in range(2):
            last = pool.tensor_tensor(bm[:, 0, 2 * e:2 * e + 2, :], mk[:, e, 0, :, :], repeat(cst("level1"), NT), ALU.mult)
        last.then_inc(e_["bm"], 1)
        pool.wait_ge(e_["bm"], j + 1)
        pool.tensor_tensor(inv[:, 0, :, :], repeat(ident, 4), bm[:, 0, :, :], ALU.subtract).then_inc(e_["init_g"], 1)

    def level_x(pe, l, j):
        if l == 0:
            pe.wait_ge(e_["init_g"], j + 1)
            pe.wait_ge(e_["init_v"], 2 * j + 2)
        else:
            pe.wait_ge(e_["tt"], LEVELS * j + l)
        for c in range(4):
            last = pe.matmul(A[0][:, c * P:(c + 1) * P], mt[:, c, :], inv[:, 0, c, :], start=True, stop=True)
        last.then_inc(e_["x"], 1)

    def level_t(pe, l, j):
        pe.wait_ge(e_["xm"], LEVELS * j + l + 1)
        for c in range(4):
            if l < LEVELS - 1:
                pe.matmul(A[2][:, c * P:(c + 1) * P], inv[:, 1, c, :], xm[:, c, :], start=True, stop=True)
            last = pe.matmul(A[3][:, c * P:(c + 1) * P], xm[:, c, :], inv[:, 1, c, :], start=True, stop=True)
        last.then_inc(e_["t"], 1)

    def level_xm(dve, l, j):
        dve.wait_ge(e_["x"], LEVELS * j + l + 1)
        dve.tensor_tensor(xm[:], quad(A[0]), repeat(level_of[:, l, :], 4), ALU.mult).then_inc(e_["xm"], 1)

    def level_tt(dve, l, j):
        dve.wait_ge(e_["t"], LEVELS * j + l + 1)
        if l < LEVELS - 1:
            dve.tensor_tensor(inv[:].rearrange("p a c k -> p (a c k)"), inv[:].rearrange("p a c k -> p (a c k)"),
                              acc[:, 2:4, :].rearrange("p a b -> p (a b)"), ALU.subtract).then_inc(e_["tt"], 1)
        else:
            dve.tensor_tensor(inv[:, 1, :, :], inv[:, 1, :, :], quad(A[3]), ALU.subtract).then_inc(e_["tt"], 1)

    GAP_BLOCKS = {1: 0, 2: 1, 4: 2, 5: 3, 7: 4, 8: 5, 10: 6, 11: 7}

    def pair_pe(pe, i):
        more = not (isinstance(i, int) and i == PAIRS - 1)
        for l in range(LEVELS):
            for half in range(2):
                (level_x, level_t)[half](pe, l, i)
                if more:
                    for piece in (4 * l + 2 * half, 4 * l + 2 * half + 1):
                        x, e = BLOCKS[piece // 3]
                        gdn_block(pe, x, e, i + 1, piece % 3)
        pe.wait_ge(e_["tt"], LEVELS * (i + 1))
        for e in range(2):
            pe.matmul(A[0][:, e * P:(e + 1) * P], inv[:, 1, 2 * e, :], vbeta[:, 2 * e, :], start=True, stop=True)
        for e in range(2):
            last = pe.matmul(A[0][:, (2 + e) * P:(3 + e) * P], kbg[:, e, :], inv[:, 1, 2 * e + 1, :], start=True, stop=True)
        last.then_inc(e_["f1"], 1)
        if more:
            turn_pe(pe, i + 1)
        pe.wait_ge(e_["f1ev"], i + 1)
        for e in range(2):
            last = pe.matmul(A[1][:, e * P:(e + 1) * P], kdec[:, e, :], vnew[:, 0, e, :], start=True, stop=True)
        last.then_inc(e_["f2"], 1)
        pe.wait_ge(e_["f2ev"], i + 1)
        for e in range(2):
            pe.matmul(A[0][:, e * P:(e + 1) * P], inv[:, 1, 2 * e + 1, :], vbeta[:, 2 * e + 1, :], start=True, stop=False)
            last = pe.matmul(A[0][:, e * P:(e + 1) * P], nwt[:, e, :], state[:, e, :], start=False, stop=True)
        last.then_inc(e_["f3"], 1)
        pe.wait_ge(e_["f3ev"], i + 1)
        for e in range(2):
            pe.matmul(A[1][:, 2 * e * P:(2 * e + 1) * P], mk[:, e, 1, 0, :], vnew[:, 0, e, :], start=True, stop=True)
            o = A[1][:, (2 * e + 1) * P:(2 * e + 2) * P]
            pe.matmul(o, mk[:, e, 1, 1, :], vnew[:, 1, e, :], start=True, stop=False)
            last = pe.matmul(o, qdec_t[:, e, :], state[:, e, :], start=False, stop=True)
        last.then_inc(e_["f4"], 1)
        if more:
            back_pe(pe, i + 1)
        pe.wait_ge(e_["on"], i + 1)
        for c in range(4):
            last = pe.transpose(A[0][:, c * P:(c + 1) * P], ogn[:, c, :], ident)
        last.then_inc(e_["ot"], 1)
        if more:
            products_pe(pe, i + 1)

    def gdn_pe(pe):
        pe.wait_ge(z_["act"], 1)
        pe.wait_ge(z_["dve"], 10)
        for x, e in BLOCKS:
            for part in range(3):
                gdn_block(pe, x, e, 0, part)
        turn_pe(pe, 0)
        back_pe(pe, 0)
        products_pe(pe, 0)
        over(pe, PAIRS, lambda i: pair_pe(pe, i))

    def pair_act(act, i):
        split = hi_of(act)
        more = not (isinstance(i, int) and i == PAIRS - 1)
        if more:
            for x, e in BLOCKS:
                block_act(act, split, x, e, i + 1)
        else:
            first_of_next(split, ph["gdn"])
        act.wait_ge(e_["f1"], i + 1)
        act.activation(vnew[:, 0, :, :], A[0][:, 0:2 * P].rearrange("p (e k) -> p e k", e=2), ACT.Copy)
        act.activation(nwt[:], A[0][:, 2 * P:4 * P].rearrange("p (e k) -> p e k", e=2), ACT.Copy, scale=-1.0).then_inc(e_["f1ev"], 1)
        if more:
            squares_act(act, i + 1, 0)
        act.wait_ge(e_["f2"], i + 1)
        act.activation(state[:], A[1][:, 0:2 * P].rearrange("p (e k) -> p e k", e=2), ACT.Copy).then_inc(e_["f2ev"], 1)
        if more:
            squares_act(act, i + 1, 1)
        act.wait_ge(e_["f3"], i + 1)
        act.activation(vnew[:, 1, :, :], A[0][:, 0:2 * P].rearrange("p (e k) -> p e k", e=2), ACT.Copy).then_inc(e_["f3ev"], 1)
        if more:
            decay_act(act, i + 1)
        act.wait_ge(e_["f4"], i + 1)
        act.activation(junk[:, 0:512], A[1], ACT.Square).then_inc(e_["osq"], 1)
        if more:
            back_act(act, i + 1)
        act.wait_ge(e_["o32"], i + 1)
        pair = slice(2 * i, 2 * i + 2) if isinstance(i, int) else bass.ds(i * 2, 2)
        act.activation(obh[:, pair, :], og32[:], ACT.Copy).then_inc(e_["oh"], 1)
        if more:
            mt_act(act, i + 1)

    def gdn_act(act):
        split = hi_of(act)
        for x, e in BLOCKS:
            block_act(act, split, x, e, 0)
        squares_act(act, 0, 0)
        squares_act(act, 0, 1)
        decay_act(act, 0)
        back_act(act, 0)
        mt_act(act, 0)
        over(act, PAIRS, lambda i: pair_act(act, i), 2)

    def pair_dve(dve, i):
        split = lo_of(dve)
        more = not (isinstance(i, int) and i == PAIRS - 1)
        for l in range(LEVELS):
            for half in range(2):
                (level_xm, level_tt)[half](dve, l, i)
                gap = 2 * l + half - 1
                if more and gap in GAP_BLOCKS:
                    x, e = BLOCKS[GAP_BLOCKS[gap]]
                    block_dve(dve, split, x, e, i + 1)
        if more:
            x, e = BLOCKS[7]
            block_dve(dve, split, x, e, i + 1)
            prepare_dve(dve, i + 1)
        else:
            first_of_next(split, ph["gdn"])
        dve.wait_ge(e_["osq"], i + 1)
        chain = Chain(dve, e_["oss"], 1, i)
        chain(dve.tensor_reduce(ssq4[:], junk[:, 0:512].rearrange("p (a k) -> p a k", a=4), AX.X, ALU.add))
        dve.tensor_scalar(mean4[:], ssq4[:], 1.0 / P, EPS, ALU.mult, ALU.add).then_inc(e_["om"], 1)
        dve.wait_ge(e_["oroot"], i + 1)
        dve.tensor_tensor(ogn[:], quad(A[1]), spread(root4[:], P), ALU.mult).then_inc(e_["on"], 1)
        dve.wait_ge(e_["ot"], i + 1)
        if not is0(i):
            dve.wait_ge(e_["oh"], i)
            dve.wait_ge(e_["ol"], i)
        pair = slice(2 * i, 2 * i + 2) if isinstance(i, int) else bass.ds(i * 2, 2)
        dve.scalar_tensor_tensor(og32[:].rearrange("p e k -> p (e k)"), A[0], gdn_gain[:],
                                 z2[:, pair, :].rearrange("p e k -> p (e k)"), ALU.mult, ALU.mult).then_inc(e_["o32"], 1)
        if more:
            masked_dve(dve, i + 1)

    def gdn_dve(dve):
        split = lo_of(dve)
        for x, e in BLOCKS:
            block_dve(dve, split, x, e, 0)
        prepare_dve(dve, 0)
        masked_dve(dve, 0)
        over(dve, PAIRS, lambda i: pair_dve(dve, i), 2)

    def pair_pool(pool, i):
        split = lo_of(pool, True)
        more = not (isinstance(i, int) and i == PAIRS - 1)
        if more:
            for x, e in BLOCKS:
                refill(split, ph["gdn"], x, 2 * (i + 1) + e)
            prepare_pool(pool, i + 1)
        else:
            first_of_next(split, ph["gdn"])
        pool.wait_ge(e_["om"], i + 1)
        pool.tensor_tensor(root4[:], mean4[:], power[:, 0:4], ALU.pow).then_inc(e_["oroot"], 1)
        pool.wait_ge(e_["oh"], i + 1)
        pair = slice(2 * i, 2 * i + 2) if isinstance(i, int) else bass.ds(i * 2, 2)
        pool.tensor_tensor(obl[:, pair, :], og32[:], obh[:, pair, :], ALU.subtract).then_inc(e_["ol"], 1)
        if more:
            init_pool(pool, i + 1)

    def gdn_pool(pool):
        split = lo_of(pool, True)
        for x, e in BLOCKS:
            refill(split, ph["gdn"], x, e)
        prepare_pool(pool, 0)
        init_pool(pool, 0)
        over(pool, PAIRS, lambda i: pair_pool(pool, i), 2)

    close_scope()
    open_scope()

    t_ = sems("t", "zth zs o")
    oah, oal = sb("oah", [P, HEADS, TOK], F32R), sb("oal", [P, HEADS, TOK], F32R)
    qk_row = sb("qk_row", [P, 4, P])
    att_a, att_b = sb("att_a", [P, 4, ROT]), sb("att_b", [P, 4, ROT])
    qk_col = sb("qk_col", [P, 2, TOK])
    causal_prob = sb("causal_prob", [P, 3 * P])
    causal_t = sb("causal_t", [P, 3 * P])
    zsilu = sb("zsilu", [P, TOK])
    KEYS = ((0, P), (P, 3 * P))
    B4, B5 = acc[:, 0, :], acc[:, 1, :]

    def att_pe(pe):
        def queries_keys(j):
            if not is0(j):
                pe.wait_ge(h["qkev"], j + ATT_SEEN)
            for t in range(NT):
                for b in range(KB):
                    k = b // 4
                    if t == 0 and b % 4 == 0:
                        chunk_ready(pe, ph["att"], k, j)
                    o = (b % 4) * TOK
                    last = mm3(pe, W[0][:, t * TOK:(t + 1) * TOK], (xh[:, b, t * P:(t + 1) * P], xl[:, b, t * P:(t + 1) * P]),
                               wslot(k, o, o + TOK), b == 0, b == KB - 1)
                    if t == NT - 1 and b % 4 == 3:
                        last.then_inc(used[k], 1)

        def values(j):
            chunk_ready(pe, ph["att"], 2, j)
            if not is0(j):
                pe.wait_ge(h["vev"], j + ATT_SEEN)
            for t in range(NT):
                for b in range(KB):
                    last = mm3(pe, W[1][:, t * P:(t + 1) * P], (xh[:, b, t * P:(t + 1) * P], xl[:, b, t * P:(t + 1) * P]),
                               wslot(2, b * P, (b + 1) * P), b == 0, b == KB - 1)
            last.then_inc(used[2], 1)

        def turn(j):
            pe.wait_ge(h["roped"], j + 1 + HEADS)
            if not is0(j):
                pe.wait_ge(h["turned_ev"], j + HEADS)
            for x in range(2):
                for t in range(NT):
                    last = pe.transpose(B4[:, x * TOK + t * P:x * TOK + (t + 1) * P], qk_row[:, 2 * t + x, :], ident)
            last.then_inc(h["turned"], 1)

        def gates(j):
            chunk_ready(pe, ph["att"], 3, j)
            if not is0(j):
                pe.wait_ge(t_["zs"], j)
            project_t(pe, B5[:, 0:TOK], 3).then_inc(used[3], 1)

        def head(i):
            more = not (isinstance(i, int) and i == HEADS - 1)
            pe.wait_ge(h["turned_ev"], i + 1 + HEADS)
            if not is0(i):
                pe.wait_ge(t_["o"], i)
            for t in range(NT):
                a, b = KEYS[t]
                last = pe.matmul(W[2][:, a:b], qk_col[:, 0, t * P:(t + 1) * P], qk_col[:, 1, 0:b - a], start=True, stop=True)
            last.then_inc(h["s"], 1)
            if more:
                queries_keys(i + 1)
            pe.wait_ge(h["p"], i + 1 + ATT_SEEN)
            for c in range(3):
                last = pe.transpose(W[3][:, c * P:(c + 1) * P], causal_prob[:, c * P:(c + 1) * P], ident)
            last.then_inc(h["pt"], 1)
            if more:
                values(i + 1)
                turn(i + 1)
            pe.wait_ge(h["ptev"], i + 1 + ATT_SEEN)
            pe.wait_ge(h["vev"], i + 1 + ATT_SEEN)
            pe.matmul(W[2][:, 0:TOK], v_sb[:, 0, :], causal_t[:, 0:TOK], start=True, stop=False)
            pe.matmul(W[2][:, P:TOK], v_sb[:, 1, :], causal_t[:, TOK:3 * P], start=False, stop=True).then_inc(h["pv"], 1)
            if more:
                gates(i + 1)

        queries_keys(0)
        values(0)
        turn(0)
        gates(0)
        over(pe, HEADS, head)

    def att_act(act):
        split = hi_of(act)

        def take_qk(j):
            act.wait_ge(used[1], ph["att"].base[1] + j + 1)
            act.activation(qk_row[:].rearrange("p a k -> p (a k)"), W[0][:], ACT.Copy).then_inc(h["qkev"], 1)

        def take_turned(j):
            act.wait_ge(h["turned"], j + 1 + HEADS)
            act.activation(qk_col[:].rearrange("p a k -> p (a k)"), B4, ACT.Copy).then_inc(h["turned_ev"], 1)

        def gate_tanh(j):
            act.wait_ge(used[3], ph["att"].base[3] + j + 1)
            if not is0(j):
                act.wait_ge(t_["zs"], j)
            act.activation(tanh_[3][:], B5[:, 0:TOK], ACT.Tanh, scale=0.5).then_inc(t_["zth"], 1)

        def head(i):
            more = not (isinstance(i, int) and i == HEADS - 1)
            if not more:
                first_of_next(split, ph["att"])
            act.wait_ge(h["mx"], i + 1 + ATT_SEEN)
            for t in range(NT):
                a, b = KEYS[t]
                last = act.activation(causal_prob[:, a:b], causal_prob[:, a:b], ACT.Exp, bias=soft[:, 4 + t:5 + t],
                                      scale=ATT_SCALE, accum_out=soft[:, 8 + t:9 + t])
            last.then_inc(h["e"], 1)
            if more:
                take_qk(i + 1)
                refill(split, ph["att"], 0, i + 1)
            act.wait_ge(h["pt"], i + 1 + ATT_SEEN)
            act.activation(causal_t[:], W[3][:, 0:3 * P], ACT.Copy).then_inc(h["ptev"], 1)
            if more:
                refill(split, ph["att"], 1, i + 1)
                take_turned(i + 1)
                refill(split, ph["att"], 2, i + 1)
            act.wait_ge(t_["o"], i + 1)
            at = slice(i, i + 1) if isinstance(i, int) else bass.ds(i, 1)
            act.activation(oah[:, at, :].rearrange("p a k -> p (a k)"), o32[:], ACT.Copy).then_inc(h["oh"], 1)
            if more:
                gate_tanh(i + 1)
                refill(split, ph["att"], 3, i + 1)

        take_qk(0)
        refill(split, ph["att"], 0, 0)
        refill(split, ph["att"], 1, 0)
        refill(split, ph["att"], 2, 0)
        take_turned(0)
        gate_tanh(0)
        refill(split, ph["att"], 3, 0)
        over(act, HEADS, head, 2)

    def att_dve(dve):
        split = lo_of(dve)
        cos = cst("att_cos", "p (a r) -> p a r", a=4)
        sin = cst("att_sin", "p (a r) -> p a r", a=4)

        def rotate_rows(j):
            dve.wait_ge(h["qkev"], j + 1 + ATT_SEEN)
            rotate(dve, Chain(dve, h["rope"], 1, j, HEADS), qk_row[:, :, 0:ROT], qk_row[:, :, 0:ROT], cos, sin, ROT // 2,
                   att_a, att_b).then_inc(h["roped"], 1)

        def take_values(j):
            dve.wait_ge(used[2], ph["att"].base[2] + j + 1)
            if not is0(j):
                dve.wait_ge(h["pv"], j + ATT_SEEN)
            dve.tensor_copy(v_sb[:], W[1][:, 0:TOK].rearrange("p (t c) -> p t c", t=NT)).then_inc(h["vev"], 1)

        def gate_silu(j):
            dve.wait_ge(t_["zth"], j + 1)
            dve.scalar_tensor_tensor(zsilu[:], tanh_[3][:], 1.0, B5[:, 0:TOK], ALU.add, ALU.mult).then_inc(t_["zs"], 1)

        def head(i):
            more = not (isinstance(i, int) and i == HEADS - 1)
            if not more:
                first_of_next(split, ph["att"])
            chain = Chain(dve, h["sm"], 3, i, 7 * HEADS)
            dve.wait_ge(h["s"], i + 1 + ATT_SEEN)
            chain(dve.tensor_tensor(causal_prob[:], W[2][:, 0:3 * P], cst("causal"), ALU.add))
            for t in range(NT):
                a, b = KEYS[t]
                last = dve.tensor_reduce(soft[:, t:t + 1], causal_prob[:, a:b], AX.X, ALU.max)
            chain(last)
            dve.tensor_scalar(soft[:, 4:6], soft[:, 0:2], -ATT_SCALE, None, ALU.mult).then_inc(h["mx"], 1)
            dve.wait_ge(h["e"], i + 1 + ATT_SEEN)
            chain(dve.reciprocal(soft[:, 12:14], soft[:, 8:10]))
            for t in range(NT):
                a, b = KEYS[t]
                last = dve.tensor_scalar(causal_prob[:, a:b], causal_prob[:, a:b], soft[:, 12 + t:13 + t], None, ALU.mult)
            last.then_inc(h["p"], 1)
            if more:
                rotate_rows(i + 1)
                refill(split, ph["att"], 0, i + 1)
                refill(split, ph["att"], 1, i + 1)
                take_values(i + 1)
                refill(split, ph["att"], 2, i + 1)
            dve.wait_ge(h["pv"], i + 1 + ATT_SEEN)
            dve.wait_ge(t_["zs"], i + 1)
            if not is0(i):
                dve.wait_ge(h["oh"], i + ATT_SEEN)
                dve.wait_ge(h["ol"], i + ATT_SEEN)
            dve.scalar_tensor_tensor(o32[:], W[2][:, 0:TOK], 0.5, zsilu[:], ALU.mult, ALU.mult).then_inc(t_["o"], 1)
            if more:
                gate_silu(i + 1)
                refill(split, ph["att"], 3, i + 1)

        rotate_rows(0)
        for k in range(2):
            refill(split, ph["att"], k, 0)
        take_values(0)
        refill(split, ph["att"], 2, 0)
        gate_silu(0)
        refill(split, ph["att"], 3, 0)
        over(dve, HEADS, head, 2)

    def att_pool(pool):
        split = lo_of(pool, True)

        def head(i):
            more = not (isinstance(i, int) and i == HEADS - 1)
            if more:
                for k in range(3):
                    refill(split, ph["att"], k, i + 1)
            else:
                first_of_next(split, ph["att"])
            pool.wait_ge(h["oh"], i + 1 + ATT_SEEN)
            at = slice(i, i + 1) if isinstance(i, int) else bass.ds(i, 1)
            pool.tensor_tensor(oal[:, at, :].rearrange("p a k -> p (a k)"), o32[:],
                               oah[:, at, :].rearrange("p a k -> p (a k)"), ALU.subtract).then_inc(h["ol"], 1)
            if more:
                refill(split, ph["att"], 3, i + 1)

        for k in range(4):
            refill(split, ph["att"], k, 0)
        over(pool, HEADS, head, 2)

    r_ = sems("r", "tha thb ma mb sum mh ml")
    tha, thb = sb("tha", [P, TOK]), sb("thb", [P, TOK])
    mga, mgb = sb("mga", [P, TOK]), sb("mgb", [P, TOK])
    mg = sb("mg", [P, TOK])
    mgh, mgl = sb("mgh", [P, TOK], F32R), sb("mgl", [P, TOK], F32R)

    def out_pe(pe):
        def add_output(i, start=False, stop=False):
            chunk_ready(pe, ph["out"], 4, i)
            pe.wait_ge(r_["ml"], i + 1)
            rows_out(pe, 4, mgh, mgl, start, stop).then_inc(used[4], 1)

        def group(i):
            for k, x, freed in ((0, (xh, xl), r_["tha"]), (1, (xh, xl), r_["thb"]), (2, (oah, oal), r_["ma"]), (3, (obh, obl), r_["mb"])):
                chunk_ready(pe, ph["out"], k, i)
                if not is0(i):
                    pe.wait_ge(freed, i)
                project_t(pe, W[k][:, 0:TOK], k, x=x).then_inc(used[k], 1)
                if k == 1 and not is0(i):
                    add_output(i - 1, start=isinstance(i, int) and i == 1)

        pe.wait_ge(h["ol"], HEADS + ATT_SEEN)
        pe.wait_ge(t_["zs"], HEADS)
        pe.wait_ge(e_["ol"], PAIRS)
        group(0)
        group(1)
        with pe.Fori(2, HEADS) as r:
            group(pe.snap(r))
        add_output(HEADS - 1, stop=True)

    def out_act(act):
        split = hi_of(act)

        def group(i):
            for k, (s, th) in enumerate(((r_["tha"], tha), (r_["thb"], thb))):
                act.wait_ge(used[k], ph["out"].base[k] + i + 1)
                if not is0(i):
                    act.wait_ge((r_["ma"], r_["mb"])[k], i)
                act.activation(th[:], W[k][:, 0:TOK], ACT.Tanh, scale=0.5).then_inc(s, 1)
                refill(split, ph["out"], k, i)
            if not is0(i):
                refill(split, ph["out"], 4, i - 1)
            refill(split, ph["out"], 2, i)
            act.wait_ge(r_["sum"], i + 1)
            if not is0(i):
                act.wait_ge(used[4], ph["out"].base[4] + i)
            act.activation(mgh[:], mg[:], ACT.Copy, scale=0.5).then_inc(r_["mh"], 1)
            refill(split, ph["out"], 3, i)

        over(act, HEADS, group)

    def out_dve(dve):
        split = lo_of(dve)

        def group(i):
            refill(split, ph["out"], 0, i)
            refill(split, ph["out"], 1, i)
            if not is0(i):
                refill(split, ph["out"], 4, i - 1)
            for k, (s, th, out, ready) in enumerate(((r_["ma"], tha, mga, r_["tha"]), (r_["mb"], thb, mgb, r_["thb"]))):
                dve.wait_ge(ready, i + 1)
                dve.wait_ge(used[2 + k], ph["out"].base[2 + k] + i + 1)
                dve.scalar_tensor_tensor(out[:], th[:], 1.0, W[2 + k][:, 0:TOK], ALU.add, ALU.mult).then_inc(s, 1)
            dve.wait_ge(r_["mb"], i + 1)
            if not is0(i):
                dve.wait_ge(r_["mh"], i)
            dve.tensor_tensor(mg[:], mga[:], mgb[:], ALU.add).then_inc(r_["sum"], 1)
            dve.wait_ge(r_["mh"], i + 1)
            dve.scalar_tensor_tensor(mgl[:], mg[:], 0.5, mgh[:], ALU.mult, ALU.subtract).then_inc(r_["ml"], 1)
            refill(split, ph["out"], 2, i)
            refill(split, ph["out"], 3, i)

        over(dve, HEADS, group)

    def out_pool(pool):
        split = lo_of(pool, True)

        def group(i):
            refill(split, ph["out"], 0, i)
            refill(split, ph["out"], 1, i)
            if not is0(i):
                refill(split, ph["out"], 4, i - 1)
            refill(split, ph["out"], 2, i)
            refill(split, ph["out"], 3, i)

        over(pool, HEADS, group)

    stored = sem("stored")
    ready = sems("s", "power")
    block = ctx.enter_context(nc.Block())

    @block.sync
    def _(sp):
        start_sp(sp)
        early = set()
        for p in ph.values():
            for k in p.widths:
                if (p.name, k) not in early:
                    load(sp, p, k, 0)
            for q in p.after:
                for k in q.widths:
                    if k not in p.widths:
                        load(sp, q, k, 0)
                        early.add((q.name, k))
            if p.count == 1:
                continue
            prompt = [k for k in p.widths if k not in p.lagging]
            for k in prompt:
                load(sp, p, k, 1)
            with sp.Fori(2, p.count) as r:
                i = sp.snap(r)
                for k in prompt:
                    load(sp, p, k, i)
                for k in p.lagging:
                    load(sp, p, k, i - 1)
            for q in p.after if p.lagging else []:
                for k in q.widths:
                    if k in prompt:
                        load(sp, q, k, 0)
                        early.add((q.name, k))
            for k in p.lagging:
                load(sp, p, k, p.count - 1)
        for t in range(NT):
            sp.wait_ge(n_["hid"], 8 + t + 1)
            sp.dma_start(y_out[t * P:(t + 1) * P, :], hid[:, t, :]).then_inc(stored, 16)
        sp.wait_ge(stored, 16 * NT)

    @block.tensor
    def _(pe):
        pe.wait_ge(g["tables"], 32)
        pre_pe(pe, 0)
        down_pe(pe)
        mla_pe(pe)
        pre_pe(pe, 1)
        ffn_pe(pe, 0)
        pre_pe(pe, 2)
        diff_pe(pe)
        pre_pe(pe, 3)
        ffn_pe(pe, 1)
        pre_pe(pe, 4)
        gates_pe(pe)
        gdn_pe(pe)
        att_pe(pe)
        out_pe(pe)

    @block.scalar
    def _(act):
        for k in range(6):
            split_high(act, ph["down_a"], k, 0)
        act.wait_ge(g["tables"], 32)
        pre_act(act, 0)
        down_act(act)
        mla_act(act)
        post_act(act, 0, ph["mla"], 2)
        pre_act(act, 1)
        ffn_act(act, 0)
        post_act(act, 1, ph["ffn0"], 5)
        pre_act(act, 2)
        diff_setup_act(act)
        diff_act(act)
        post_act(act, 2, ph["diff"], 3)
        pre_act(act, 3)
        ffn_act(act, 1)
        post_act(act, 3, ph["ffn1"], 5)
        pre_act(act, 4)
        gates_act(act)
        gdn_act(act)
        att_act(act)
        out_act(act)
        post_act(act, 4, ph["out"], 4)

    @block.vector
    def _(dve):
        dve.memset(power[:], -0.5).then_inc(ready["power"], 1)
        dve.wait_ge(g["tables"], 32)
        dve.wait_ge(g["x"], 16)
        for k in range(6):
            split_low(dve, False, ph["down_a"], k, 0)
        pre_dve(dve, 0)
        down_dve(dve)
        mla_dve(dve)
        post_dve(dve, 0)
        pre_dve(dve, 1)
        ffn_dve(dve, 0)
        post_dve(dve, 1)
        pre_dve(dve, 2)
        diff_setup_dve(dve)
        diff_dve(dve)
        post_dve(dve, 2)
        pre_dve(dve, 3)
        ffn_dve(dve, 1)
        post_dve(dve, 3)
        pre_dve(dve, 4)
        gates_dve(dve)
        gdn_dve(dve)
        att_dve(dve)
        out_dve(dve)
        post_dve(dve, 4)

    @block.gpsimd
    def _(pool):
        start_pool(pool)
        pool.wait_ge(ready["power"], 1)
        pool.wait_ge(g["tables"], 32)
        pre_pool(pool, 0)
        down_pool(pool)
        first_of_next(lo_of(pool, True), ph["mla"])
        post_pool(pool, 0)
        pre_pool(pool, 1)
        ffn_pool(pool, 0)
        post_pool(pool, 1)
        pre_pool(pool, 2)
        diff_pool(pool)
        post_pool(pool, 2)
        pre_pool(pool, 3)
        ffn_pool(pool, 1)
        post_pool(pool, 3)
        pre_pool(pool, 4)
        gdn_pool(pool)
        att_pool(pool)
        out_pool(pool)
        post_pool(pool, 4)

    close_scope()
    ctx.close()


def kernel(**inputs):
    import concourse.bacc as bacc
    from concourse.bass_utils import run_bass_kernel_spmd

    arrays = {f"in_{n}": a for n, a in lay_out(inputs).items()}
    nc = bacc.Bacc("TRN2", target_bir_lowering=False, num_devices=1)
    dram = {n[3:]: nc.dram_tensor(n, a.shape, F32, kind="ExternalInput").ap() for n, a in arrays.items()}
    out = nc.dram_tensor("out", (TOK, D), F32, kind="ExternalOutput").ap()
    build(nc, dram, out)
    result = run_bass_kernel_spmd(nc, [arrays], core_ids=[0])
    return result.results[0]["out"].reshape(1, TOK, D)
```

```python
from contextlib import ExitStack
import math

import numpy as np

import concourse.bass as bass
from concourse import mybir

F32 = mybir.dt.float32
F32R = mybir.dt.float32r
ALU = mybir.AluOpType
ACT = mybir.ActivationFunctionType
AX = mybir.AxisListType

P = 128
TOK = 256
NT = TOK // P
D = 1024
KB = D // P
EPS = 1e-6
HEADS = 8
FFN = 2816
FFN_STEPS = FFN // (2 * P)
PAIRS = HEADS // 2

MLA_QL, MLA_KVL, MLA_ROPE, MLA_NOPE = 384, 256, 64, 128
MLA_QB, MLA_KVB = MLA_QL // P, MLA_KVL // P
MLA_SCALE = (MLA_NOPE + MLA_ROPE) ** -0.5
MLA_DOWN = MLA_QL + MLA_KVL + MLA_ROPE
DIFF_SCALE = 64 ** -0.5
LAM_INIT = 0.8 - 0.6 * math.exp(-0.3)
ATT_SCALE = P ** -0.5
ROT = 32
LEVELS = 6


class Phase:

    def __init__(self, name, widths, count, gpsimd_low=(), lagging=()):
        self.name, self.widths, self.count, self.gpsimd_low, self.lagging = name, widths, count, gpsimd_low, lagging
        self.base = {}


def phases():
    every = {k: 1024 for k in range(6)}
    four = {k: 1024 for k in range(4)}
    ph = dict(
        down_a=Phase("down_a", {k: MLA_DOWN for k in range(6)}, 1),
        down_b=Phase("down_b", {k: MLA_DOWN for k in range(2)}, 1),
        mla=Phase("mla", {0: MLA_QB * 256, 1: MLA_KVB * 256, 2: 1024}, HEADS, lagging=(2,)),
        ffn0=Phase("ffn0", every, FFN_STEPS, (3,), (5,)),
        diff=Phase("diff", {k: 1024 for k in (2, 0, 1, 3)}, HEADS, (1, 3), (3,)),
        ffn1=Phase("ffn1", every, FFN_STEPS, (3,), (5,)),
        gates=Phase("gates", {4: KB * 16}, 1),
        gdn=Phase("gdn", {k: 1024 for k in range(3)}, HEADS, (0, 1, 2)),
        gdnz=Phase("gdnz", {3: 1024, 4: 1024}, PAIRS, (3, 4)),
        att=Phase("att", four, HEADS, (0, 2, 3)),
        out=Phase("out", {k: 1024 for k in range(5)}, HEADS, (1, 3), (4,)),
    )
    used = dict.fromkeys(range(6), 0)
    for p in ph.values():
        for k in p.widths:
            p.base[k] = used[k]
            used[k] += p.count
    ph["down_a"].after, ph["down_b"].after, ph["mla"].after = [ph["down_b"]], [ph["mla"]], [ph["ffn0"]]
    ph["ffn0"].after, ph["diff"].after, ph["ffn1"].after = [ph["diff"]], [ph["ffn1"]], [ph["gates"], ph["gdn"], ph["gdnz"]]
    ph["gates"].after, ph["gdn"].after, ph["gdnz"].after = [ph["gdnz"]], [ph["att"]], [ph["att"]]
    ph["att"].after, ph["out"].after = [ph["out"]], []
    return ph


VEC = {}


def _vec(name, width):
    VEC[name] = (sum(w for _, w in VEC.values()), width)


for _n, _w in (("pre_gain", 5 * KB), ("q_gain", MLA_QB), ("kv_gain", MLA_KVB), ("sub_gain", 1),
               ("gdn_gain", 1), ("norm_scale", 8), ("conv", HEADS * 12), ("ffn_conv", 2 * FFN_STEPS * 16),
               ("slope", HEADS), ("dt", 2 * HEADS), ("a_log", 2 * HEADS), ("lam", 256),
               ("l2_factor", 8)):
    _vec(_n, _w)
NVEC = sum(w for _, w in VEC.values())
FIRST_VEC = VEC["conv"][0]

CONST = {}


def _const(name, width):
    CONST[name] = (sum(w for _, w in CONST.values()), width)


for _n, _w in (("ident", P), ("upper", P), ("strict_lower", P), ("level1", P), ("level1_t", P),
               ("levels", LEVELS * P), ("ones", P), ("causal", 3 * P), ("dist", NT * TOK),
               ("mla_cos", NT * MLA_ROPE), ("mla_sin", NT * MLA_ROPE), ("mla_rot", TOK),
               ("att_cos", NT * 2 * ROT), ("att_sin", NT * 2 * ROT)):
    _const(_n, _w)
NCONST = sum(w for _, w in CONST.values())


def constants():
    c = np.zeros((P, NCONST), np.float32)

    def put(name, a):
        o, w = CONST[name]
        c[:, o:o + w] = np.asarray(a, np.float32).reshape(P, w)

    r, k = np.arange(P)[:, None], np.arange(P)[None, :]
    put("ident", r == k)
    put("upper", r <= k)
    put("strict_lower", k < r)

    def level(s):
        return (r // (2 * s) == k // (2 * s)) & (r % (2 * s) >= s) & (k % (2 * s) < s)

    put("level1", level(1))
    put("level1_t", level(1).T)
    put("levels", np.stack([level(2 << n) for n in range(LEVELS)], 1))
    put("ones", np.ones((P, P)))
    tri = np.where(k <= r, 0.0, -1e30)
    put("causal", np.stack([tri, np.zeros((P, P)), tri], 1))
    pos = np.arange(TOK).reshape(NT, P).T
    put("dist", np.abs(pos[:, :, None] - np.arange(TOK)[None, None, :]))

    def rope(inv, repeat):
        ang = (np.arange(TOK, dtype=np.float32)[:, None] * inv[None, :]).astype(np.float32)
        co, si = np.cos(ang), np.sin(ang)
        both = np.concatenate([co, co], 1), np.concatenate([-si, si], 1)
        return [np.repeat(x.reshape(NT, P, -1).transpose(1, 0, 2)[:, :, None], repeat, 2) for x in both]

    inv = np.float32(10000.0) ** (-np.arange(0, MLA_ROPE, 2, dtype=np.float32) / np.float32(MLA_ROPE))
    co, si = rope(inv, 1)
    put("mla_rot", np.concatenate([x[:, :, 0].transpose(2, 1, 0).reshape(MLA_ROPE, TOK) for x in (co, si)]))
    put("mla_cos", co)
    put("mla_sin", si)
    inv = np.power(np.float32(500000.0), -np.arange(ROT // 2, dtype=np.float32) * np.float32(2.0 / ROT))
    co, si = rope(inv, 2)
    put("att_cos", co)
    put("att_sin", si)
    return c


def lay_out(a):
    f = {k: np.asarray(v) for k, v in a.items()}
    out = {"x": f["x"][0], "const": constants()}

    v = np.zeros((P, NVEC), np.float32)

    def put(name, x):
        o, w = VEC[name]
        v[:, o:o + w] = np.asarray(x).reshape(P, w)

    def channels(x):
        return x.reshape(-1, P).T

    ng = f["norm_g"]
    put("pre_gain", np.concatenate([channels(g) for g in (ng[0, 0], ng[0, 2], ng[1, 0], ng[1, 2],
                                                          f["pre_norm_w_2"][0])], 1))
    put("q_gain", channels(f["mla_q_norm_g"][0]))
    put("kv_gain", channels(f["mla_kv_norm_g"][0]))
    put("sub_gain", channels(f["diff_subln_g"][0]))
    put("gdn_gain", channels(f["gdn_norm_w_2"][0]))
    put("conv", f["conv_w_2"][0].reshape(4, 3, HEADS, P).transpose(3, 2, 1, 0))
    taps = np.concatenate([f["ffn_conv_w"], f["ffn_conv_b"][:, None]], 1)
    put("ffn_conv", taps.reshape(2, 4, 2, FFN_STEPS, 2, P).transpose(5, 0, 3, 4, 2, 1))
    slopes = 2.0 ** (-8.0 * np.arange(1, HEADS + 1) / HEADS)
    put("slope", np.broadcast_to(-slopes / DIFF_SCALE, (P, HEADS)))
    put("dt", np.broadcast_to(np.repeat(f["dt_bias_2"][0], 2), (P, 16)))
    put("a_log", np.broadcast_to(np.repeat(f["a_log_2"][0], 2), (P, 16)))
    put("lam", np.broadcast_to(f["diff_lambda"][0].reshape(-1), (P, 256)))
    put("norm_scale", np.broadcast_to(np.array([1 / MLA_QL, 1 / MLA_QL, 1 / MLA_KVL, 1 / MLA_KVL, 0, 0, 0, 0]), (P, 8)))
    fac = np.array([0.5 * P ** -0.5, 0.5 * P ** -0.5, 0.5, 0.5] * 2)
    put("l2_factor", np.broadcast_to(fac, (P, 8)))
    out["vec"] = v
    out["post_gain"] = np.ascontiguousarray(np.broadcast_to(
        np.stack([ng[0, 1], ng[0, 3], ng[1, 1], ng[1, 3], f["post_norm_w_2"][0]])[:, None], (5, P, D)))

    def chunks(name, parts):
        for slot, x in parts.items():
            out[f"w_{name}_{slot}"] = np.ascontiguousarray(x).reshape(x.shape[0] * P, -1)

    down = np.concatenate([f["mla_w_dq"][0], f["mla_w_dkv"][0]], 1).reshape(KB, P, MLA_DOWN)
    chunks("down_a", {k: down[k:k + 1] for k in range(6)})
    chunks("down_b", {k: down[6 + k:7 + k] for k in range(2)})

    def rows(w):
        return w.reshape(-1, P, D)

    def heads(w, width):
        return w.reshape(-1, P, w.shape[1] // width, width).transpose(2, 1, 0, 3)

    uq = heads(f["mla_w_uq"][0], 192)
    uq = np.concatenate([uq, uq[..., 160:192], uq[..., 128:160]], 3)
    chunks("mla", {0: uq, 1: heads(f["mla_w_ukv"][0], 256),
                   2: rows(f["mla_w_o"][0])})
    for layer in range(2):
        up = f["ffn_w_up"][layer].reshape(KB, P, 2, FFN_STEPS, 2, P)
        dn = f["ffn_w_down"][layer].reshape(FFN_STEPS, 2, P, D)
        parts = {2 * j + g: up[:, :, g, :, j].transpose(2, 1, 0, 3) for j in range(2) for g in range(2)}
        parts.update({4 + j: dn[:, j] for j in range(2)})
        chunks(f"ffn{layer}", parts)
    qkv = f["diff_w_qkv"][0]
    chunks("diff", {**{n: heads(qkv[:, n * D:n * D + D], P) for n in range(3)}, 3: rows(f["diff_w_o"][0])})
    w_in = f["w_in_2"][0]

    def part(n):
        return w_in[:, n * D:n * D + D]

    qk = np.stack([heads(part(0), P), heads(part(1), P)], 3)
    chunks("att", {0: qk[:, :, 0:4], 1: qk[:, :, 4:8], 2: heads(part(2), P), 3: heads(part(3), P)})
    chunks("gdn", {n: heads(part(4 + n), P) for n in range(3)})
    chunks("gdnz", {3 + n: heads(part(7), P)[n::2] for n in range(2)})
    o = 8 * D
    chunks("gates", {4: w_in[:, o:o + 16].reshape(KB, P, 16).transpose(1, 0, 2)[None]})
    o += 16
    chunks("out", {0: heads(w_in[:, o:o + D], P), 1: heads(w_in[:, o + D:o + 2 * D], P),
                   2: heads(f["w_branch_a_2"][0], P), 3: heads(f["w_branch_b_2"][0], P),
                   4: rows(f["w_out_2"][0])})
    return out


def build(nc, dram, y_out):
    ph = phases()
    ctx = ExitStack()

    scope = [ctx]

    def sb(name, shape, dt=F32):
        return scope[-1].enter_context(nc.sbuf_tensor(name, shape, dt))

    def open_scope():
        scope.append(ExitStack())

    def close_scope():
        scope.pop().close()

    def sem(name):
        return ctx.enter_context(nc.semaphore(name))

    def sems(prefix, names):
        return {n: sem(f"{prefix}_{n}") for n in names.split()}

    raw = [sb(f"raw{k}", [P, 1024]) for k in range(5)]
    high = [sb(f"high{k}", [P, 1024], F32R) for k in range(5)]
    low = [sb(f"low{k}", [P, 1024], F32R) for k in range(5)]

    const = sb("const", [P, NCONST])
    vec = sb("vec", [P, NVEC])
    post_gain = sb("post_gain_sb", [P, D])
    hid = sb("hid", [P, NT, D])
    hn = sb("hn", [P, NT, D])
    junk = sb("junk", [P, 512])
    xh = sb("xh", [P, KB, TOK], F32R)
    xl = sb("xl", [P, KB, TOK], F32R)
    stat = sb("stat", [P, 16])
    mean = sb("mean", [P, 16])
    power = sb("power", [P, 8])

    v_sb = sb("v_sb", [P, NT, P])
    soft = sb("soft", [P, 16])
    o32 = sb("o32", [P, TOK])
    open_scope()
    raw.append(sb("raw5", [P, 1024]))
    high.append(sb("high5", [P, 1024], F32R))
    low.append(sb("low5", [P, 1024], F32R))

    acc = ctx.enter_context(nc.psum_tensor("acc", [P, 4, 512], F32))
    W = [ctx.enter_context(nc.psum_tensor(f"work{k}", [P, 512], F32)) for k in range(4)]

    def cst(name, shape=None, **dims):
        o, w = CONST[name]
        return const[:, o:o + w] if shape is None else const[:, o:o + w].rearrange(shape, **dims)

    def vcol(name, at=0, width=None):
        o, w = VEC[name]
        if isinstance(at, int):
            return vec[:, o + at:o + at + (width or w)]
        return vec[:, bass.ds(at + o, width)]

    ident = cst("ident")

    def spread(ap, n):
        return ap.unsqueeze(2).to_broadcast([P, ap.shape[1], n])

    def repeat(ap, n):
        return ap.unsqueeze(1).to_broadcast([P, n, ap.shape[1]])

    landed = [sem(f"landed{k}") for k in range(6)]
    high_done = [sem(f"high_done{k}") for k in range(6)]
    low_done = [sem(f"low_done{k}") for k in range(6)]
    used = [sem(f"used{k}") for k in range(6)]

    def load(sp, p, k, i):
        n, w = p.base[k] + i, p.widths[k]
        src = dram[f"w_{p.name}_{k}"]
        if not (isinstance(n, int) and n == 0):
            sp.wait_ge(low_done[k], n)
        at = slice(i * P, (i + 1) * P) if isinstance(i, int) else bass.ds(i * P, P)
        sp.dma_start(raw[k][:, 0:w], src[at, :]).then_inc(landed[k], 16)

    def split_high(act, p, k, i):
        n, w = p.base[k] + i, p.widths[k]
        if not (isinstance(n, int) and n == 0):
            act.wait_ge(used[k], n)
        act.wait_ge(landed[k], n * 16 + 16)
        act.activation(high[k][:, 0:w], raw[k][:, 0:w], ACT.Copy).then_inc(high_done[k], 1)

    def split_low(eng, is_gpsimd, p, k, i):
        n, w = p.base[k] + i, p.widths[k]
        if (k in p.gpsimd_low) != is_gpsimd:
            return
        eng.wait_ge(high_done[k], n + 1)
        eng.tensor_tensor(low[k][:, 0:w], raw[k][:, 0:w], high[k][:, 0:w], ALU.subtract).then_inc(low_done[k], 1)

    def refill(split, p, k, i):
        if not (isinstance(i, int) and i == p.count - 1):
            return split(p, k, i + 1)
        for q in p.after:
            if k in q.widths:
                return split(q, k, 0)

    def first_of_next(split, p):
        for q in p.after:
            for k in q.widths:
                if k not in p.widths:
                    split(q, k, 0)

    def hi_of(act):
        return lambda p, k, i: split_high(act, p, k, i)

    def lo_of(eng, is_gpsimd=False):
        return lambda p, k, i: split_low(eng, is_gpsimd, p, k, i)

    def chunk_ready(pe, p, k, i):
        pe.wait_ge(low_done[k], p.base[k] + i + 1)

    def mm3(pe, out, lhs, rhs, start, stop):
        pe.matmul(out, lhs[0], rhs[0], start=start, stop=False)
        pe.matmul(out, lhs[0], rhs[1], start=False, stop=False)
        return pe.matmul(out, lhs[1], rhs[0], start=False, stop=stop)

    def both(h, l, *at):
        return h[at], l[at]

    def wslot(k, a, b):
        return high[k][:, a:b], low[k][:, a:b]

    SPLIT_ORDER = [0, 2, 4, 6, 1, 3, 5, 7]

    def project_t(pe, out, k, width=P, offset=0, x=None, blocks=KB, arriving=None):
        x = x or (xh, xl)
        order = range(blocks) if arriving is None else SPLIT_ORDER
        for n, b in enumerate(order):
            if arriving is not None:
                pe.wait_ge(n_["xl"], KB * arriving + max(n + 1, 5))
            o = b * width + offset
            last = mm3(pe, out, wslot(k, o, o + P), (x[0][:, b, :], x[1][:, b, :]), n == 0, n == blocks - 1)
        return last

    def rows_out(pe, k, oh, ol, start, stop):
        for t in range(NT):
            for half in range(2):
                c = half * 512
                last = mm3(pe, acc[:, 2 * t + half, :], (oh[:, t * P:(t + 1) * P], ol[:, t * P:(t + 1) * P]),
                           wslot(k, c, c + 512), start, stop)
        return last

    class Chain:

        def __init__(self, eng, s, per, i, seen=0):
            self.eng, self.s, self.per, self.at, self.k = eng, s, per, i * per + seen, 0

        def __call__(self, ins):
            ins.then_inc(self.s, 1)
            self.k += 1
            assert self.k <= self.per
            self.eng.wait_ge(self.s, self.at + self.k)

    def over(eng, count, body, peel_end=1):
        body(0)
        with eng.Fori(1, count - peel_end) as i:
            body(eng.snap(i))
        for i in range(count - peel_end, count):
            body(i)

    g = sems("g", "x tables const")
    n_ = sems("n", "hid sq mean root hn turned xh xl")
    h = sems("h", "qkev s mx sm e p pt ptev vev pv oh ol rope roped turned turned_ev")
    DIFF_SEEN, ATT_SEEN = HEADS, 2 * HEADS
    q_ = sems("q", "sq mean root upd gain")

    def evac_split_act(act, items, banks, base, s, turned=None):
        for p, (src, gain, h, l, bank) in enumerate(items):
            if turned:
                act.wait_ge(*turned(bank))
            if p >= banks:
                act.wait_ge(s["xl"], base + p - banks + 1)
            act.activation(h, src, ACT.Copy, scale=gain).then_inc(s["xh"], 1)

    def evac_split_dve(dve, items, base, s):
        for p, (src, gain, h, l, bank) in enumerate(items):
            dve.wait_ge(s["xh"], base + p + 1)
            dve.scalar_tensor_tensor(l, src, gain, h, ALU.mult, ALU.subtract).then_inc(s["xl"], 1)

    def x_items(n):
        out = []
        for p in range(KB):
            b = SPLIT_ORDER[p]
            out.append((W[b // 2][:, (b % 2) * TOK:(b % 2 + 1) * TOK], vcol("pre_gain", n * KB + b, 1),
                        xh[:, b, :], xl[:, b, :], b // 2))
        return out

    def pre_pe(pe, n):
        for t in range(NT):
            pe.wait_ge(n_["hn"], 2 * n + t + 1)
            for b in range(KB):
                last = pe.transpose(W[b // 2][:, (b % 2) * TOK + t * P:(b % 2) * TOK + (t + 1) * P],
                                    hn[:, t, b * P:(b + 1) * P], ident)
                if b % 2 and t == NT - 1:
                    last.then_inc(n_["turned"], 1)

    def pre_act(act, n):
        for t in range(NT):
            if n:
                act.wait_ge(n_["hid"], 2 * (n - 1) + t + 1)
            elif t == 0:
                act.wait_ge(g["x"], 16)
            act.activation(hn[:, t, :], hid[:, t, :], ACT.Square, accum_out=stat[:, t:t + 1]).then_inc(n_["sq"], 1)

    def pre_act_split(act, n):
        evac_split_act(act, x_items(n), 4, KB * n, n_, lambda bank: (n_["turned"], 4 * n + bank + 1))

    def pre_dve(dve, n):
        for t in range(NT):
            dve.wait_ge(n_["sq"], 2 * n + t + 1)
            dve.tensor_scalar(mean[:, t:t + 1], stat[:, t:t + 1], 1.0 / D, EPS, ALU.mult, ALU.add).then_inc(n_["mean"], 1)
            dve.wait_ge(n_["root"], 2 * n + t + 1)
            dve.tensor_scalar(hn[:, t, :], hid[:, t, :], stat[:, 8 + t:9 + t], None, ALU.mult).then_inc(n_["hn"], 1)

    def pre_dve_split(dve, n):
        evac_split_dve(dve, x_items(n), KB * n, n_)

    def pre_pool(pool, n):
        for t in range(NT):
            pool.wait_ge(n_["mean"], 2 * n + t + 1)
            pool.tensor_tensor(stat[:, 8 + t:9 + t], mean[:, t:t + 1], power[:, 0:1], ALU.pow).then_inc(n_["root"], 1)

    def post_act(act, n, p, k):
        act.wait_ge(used[k], p.base[k] + p.count)
        for t in range(NT):
            if t:
                act.wait_ge(q_["upd"], 2 * n + 1)
            act.activation(xh[:, 4 * t:4 * t + 4, :].rearrange("p b k -> p (b k)"),
                           acc[:, 2 * t:2 * t + 2, :].rearrange("p a b -> p (a b)"), ACT.Square,
                           accum_out=stat[:, 2 + t:3 + t]).then_inc(q_["sq"], 1)

    def post_dve(dve, n, p, k):
        dve.wait_ge(q_["gain"], 16 * (n + 1))
        dve.wait_ge(used[k], p.base[k] + p.count)
        for t in (1, 0):
            if t == 0:
                dve.wait_ge(q_["sq"], 2 * n + 1)
                dve.tensor_scalar(mean[:, 2:3], stat[:, 2:3], 1.0 / D, EPS, ALU.mult, ALU.add).then_inc(q_["mean"], 1)
            dve.tensor_tensor(hn[:, t, :], acc[:, 2 * t:2 * t + 2, :].rearrange("p a b -> p (a b)"), post_gain[:],
                              ALU.mult).then_inc(q_["upd"], 1)
        dve.wait_ge(q_["sq"], 2 * n + 2)
        dve.tensor_scalar(mean[:, 3:4], stat[:, 3:4], 1.0 / D, EPS, ALU.mult, ALU.add).then_inc(q_["mean"], 1)
        dve.wait_ge(q_["upd"], 2 * n + 2)
        for t in range(NT):
            dve.wait_ge(q_["root"], 2 * n + t + 1)
            dve.scalar_tensor_tensor(hid[:, t, :], hn[:, t, :], stat[:, 10 + t:11 + t], hid[:, t, :], ALU.mult,
                                     ALU.add).then_inc(n_["hid"], 1)

    def post_pool(pool, n):
        for t in range(NT):
            pool.wait_ge(q_["mean"], 2 * n + t + 1)
            pool.tensor_tensor(stat[:, 10 + t:11 + t], mean[:, 2 + t:3 + t], power[:, 0:1], ALU.pow).then_inc(q_["root"], 1)
        if n < 4:
            pool.wait_ge(q_["upd"], 2 * n + 2)
            pool.dma_start(post_gain[:], dram["post_gain"][n + 1]).then_inc(q_["gain"], 16)

    def start_sp(sp):
        sp.dma_start(hid[:], dram["x"].rearrange("(t p) d -> p t d", p=P)).then_inc(g["x"], 16)
        sp.dma_start(const[:, 0:P], dram["const"][:, 0:P]).then_inc(g["tables"], 16)
        sp.dma_start(vec[:, 0:FIRST_VEC], dram["vec"][:, 0:FIRST_VEC]).then_inc(g["tables"], 16)

    def start_later_sp(sp):
        sp.dma_start(const[:, P:NCONST], dram["const"][:, P:NCONST]).then_inc(g["const"], 16)
        sp.dma_start(vec[:, FIRST_VEC:NVEC], dram["vec"][:, FIRST_VEC:NVEC]).then_inc(g["const"], 16)

    def start_pool(pool):
        pool.dma_start(post_gain[:], dram["post_gain"][0]).then_inc(q_["gain"], 16)

    m = sems("m", "sq mean root cn turned xh xl krev rope_k qk")
    cqh, cql = sb("cqh", [P, MLA_QB, TOK], F32R), sb("cql", [P, MLA_QB, TOK], F32R)
    ckh, ckl = sb("ckh", [P, MLA_KVB, TOK], F32R), sb("ckl", [P, MLA_KVB, TOK], F32R)
    rope_pad = sb("rope_pad", [P, NT, P])
    rope_a, rope_b = sb("rope_a", [P, NT, MLA_ROPE]), sb("rope_b", [P, NT, MLA_ROPE])
    kr_t = sb("kr_t", [P, TOK])
    qr_t = sb("qr_t", [P, TOK])
    q_sb, k_sb = sb("q_sb", [P, TOK]), sb("k_sb", [P, TOK])
    prob = sb("prob", [P, 4, TOK])
    prob_t = sb("prob_t", [P, NT, TOK])
    oh, ol = sb("oh", [P, TOK], F32R), sb("ol", [P, TOK], F32R)

    def down_pe(pe):
        for b in range(KB):
            p, k = (ph["down_a"], b) if b < 6 else (ph["down_b"], b - 6)
            chunk_ready(pe, p, k, 0)
            if b == 0:
                pe.wait_ge(n_["xl"], KB)
            for t in range(NT):
                x = (xh[:, b, t * P:(t + 1) * P], xl[:, b, t * P:(t + 1) * P])
                mm3(pe, acc[:, t, 0:MLA_QL], x, wslot(k, 0, MLA_QL), b == 0, b == KB - 1)
                last = mm3(pe, acc[:, 2 + t, 0:320], x, wslot(k, MLA_QL, MLA_DOWN), b == 0, b == KB - 1)
            last.then_inc(used[k], 1)
        pe.wait_ge(m["cn"], 4)
        pe.wait_ge(m["rope_k"], 3)
        for src, bank, half in ((0, 0, 0), (1, 0, 1), (2, 1, 0), (3, 1, 1), (4, 2, 0), (5, 2, 1)):
            for t in range(NT):
                a = latent[:, t, src * P:(src + 1) * P] if src < 5 else rope_pad[:, t, :]
                last = pe.transpose(W[bank][:, half * TOK + t * P:half * TOK + (t + 1) * P], a, ident)
            if half:
                last.then_inc(m["turned"], 1)

    latent = sb("latent", [P, NT, 5 * P])

    def latent_items():
        def item(src, bank, half):
            h, l, gain = ((cqh, cql, vcol("q_gain", src, 1)) if src < 3 else (ckh, ckl, vcol("kv_gain", src - 3, 1)))
            b = src if src < 3 else src - 3
            return W[bank][:, half * TOK:(half + 1) * TOK], gain, h[:, b, :], l[:, b, :], bank
        return [item(0, 0, 0), item(2, 1, 0), item(4, 2, 0), item(1, 0, 1), item(3, 1, 1)]

    def down_act(act):
        split = hi_of(act)
        for k in range(2):
            refill(split, ph["down_a"], k, 0)
        act.wait_ge(used[1], 2)
        for t in range(NT):
            act.activation(hn[:, t, 0:MLA_QL], acc[:, t, 0:MLA_QL], ACT.Square, accum_out=stat[:, 4 + t:5 + t]).then_inc(m["sq"], 1)
        for t in range(NT):
            act.activation(hn[:, t, MLA_QL:MLA_QL + MLA_KVL], acc[:, 2 + t, 0:MLA_KVL], ACT.Square,
                           accum_out=stat[:, 6 + t:7 + t]).then_inc(m["sq"], 1)
        for k in range(2):
            refill(split, ph["down_b"], k, 0)
        first_of_next(split, ph["down_b"])
        evac_split_act(act, latent_items(), 3, 0, m, lambda bank: (m["turned"], bank + 1))
        act.wait_ge(m["xl"], 3)
        act.activation(kr_t[:], W[2][:, TOK:2 * TOK], ACT.Copy).then_inc(m["krev"], 1)

    def rotate(dve, chain, out, src, cos, sin, half, a, b):
        dve.tensor_tensor(a[:], src, cos, ALU.mult)
        dve.tensor_tensor(b[:, :, 0:half], src[:, :, half:2 * half], sin[:, :, 0:half], ALU.mult)
        chain(dve.tensor_tensor(b[:, :, half:2 * half], src[:, :, 0:half], sin[:, :, half:2 * half], ALU.mult))
        return dve.tensor_tensor(out, a[:], b[:], ALU.add)

    mla_cos = cst("mla_cos", "p (t r) -> p t r", t=NT)
    mla_sin = cst("mla_sin", "p (t r) -> p t r", t=NT)

    def down_dve(dve):
        split = lo_of(dve)
        for k in range(2):
            refill(split, ph["down_a"], k, 0)
        dve.wait_ge(m["sq"], 4)
        dve.tensor_tensor(mean[:, 4:8], stat[:, 4:8], vcol("norm_scale", 0, 4), ALU.mult).then_inc(m["mean"], 1)
        dve.wait_ge(m["mean"], 1)
        dve.tensor_scalar(mean[:, 4:8], mean[:, 4:8], EPS, None, ALU.add).then_inc(m["mean"], 1)
        kr = acc[:, 2:4, MLA_KVL:MLA_KVL + MLA_ROPE]

        def chain(ins):
            ins.then_inc(m["rope_k"], 1)
            dve.wait_ge(m["rope_k"], 1)

        rotate(dve, chain, rope_pad[:, :, 0:MLA_ROPE], kr, mla_cos, mla_sin, 32, rope_a, rope_b).then_inc(m["rope_k"], 1)
        dve.tensor_tensor(rope_pad[:, :, MLA_ROPE:P], rope_a[:], rope_b[:], ALU.add).then_inc(m["rope_k"], 1)
        dve.wait_ge(m["root"], 1)
        for t in range(NT):
            dve.tensor_scalar(latent[:, t, 0:MLA_QL], acc[:, t, 0:MLA_QL], stat[:, 12 + t:13 + t], None, ALU.mult).then_inc(m["cn"], 1)
            dve.tensor_scalar(latent[:, t, MLA_QL:5 * P], acc[:, 2 + t, 0:MLA_KVL], stat[:, 14 + t:15 + t], None,
                              ALU.mult).then_inc(m["cn"], 1)
        for k in range(2):
            refill(split, ph["down_b"], k, 0)
        evac_split_dve(dve, latent_items(), 0, m)
        first_of_next(split, ph["down_b"])

    def down_pool(pool):
        pool.wait_ge(m["mean"], 2)
        pool.tensor_tensor(stat[:, 12:16], mean[:, 4:8], power[:, 0:4], ALU.pow).then_inc(m["root"], 1)

    def mla_pe(pe):
        def queries_keys(j):
            chunk_ready(pe, ph["mla"], 0, j)
            chunk_ready(pe, ph["mla"], 1, j)
            if isinstance(j, int) and j == 0:
                pe.wait_ge(m["xl"], 5)
                pe.wait_ge(m["krev"], 1)
            else:
                pe.wait_ge(h["qkev"], j)
            project_t(pe, W[0][:, 0:TOK], 0, 256, 0, (cqh, cql), MLA_QB)
            project_t(pe, W[0][:, TOK:2 * TOK], 1, 256, 0, (ckh, ckl), MLA_KVB).then_inc(m["qk"], 1)

        def rotated_values(j):
            if not (isinstance(j, int) and j == 0):
                pe.wait_ge(h["vev"], j)
            project_t(pe, W[1][:, 0:TOK], 0, 256, P, (cqh, cql), MLA_QB).then_inc(used[0], 1)
            for t in range(NT):
                for b in range(MLA_KVB):
                    last = mm3(pe, W[1][:, TOK + t * P:TOK + (t + 1) * P],
                               (ckh[:, b, t * P:(t + 1) * P], ckl[:, b, t * P:(t + 1) * P]),
                               wslot(1, b * 256 + P, b * 256 + 256), b == 0, b == MLA_KVB - 1)
            last.then_inc(used[1], 1)

        def head(i):
            pe.wait_ge(h["qkev"], i + 1)
            pe.wait_ge(h["roped"], i + 1)
            first = isinstance(i, int) and i == 0
            more = not (isinstance(i, int) and i == HEADS - 1)
            for t in range(NT):
                out = W[2][:, t * TOK:(t + 1) * TOK]
                pe.matmul(out, q_sb[:, t * P:(t + 1) * P], k_sb[:], start=True, stop=False)
                last = pe.matmul(out, qr_t[:, t * P:(t + 1) * P], kr_t[:], start=False, stop=True)
            last.then_inc(h["s"], 1)
            if not first:
                chunk_ready(pe, ph["mla"], 2, i - 1)
                pe.wait_ge(h["ol"], i)
                if isinstance(i, int) and i == 1:
                    rows_out(pe, 2, oh, ol, True, False).then_inc(used[2], 1)
                else:
                    rows_out(pe, 2, oh, ol, False, False).then_inc(used[2], 1)
            if more:
                queries_keys(i + 1)
            pe.wait_ge(h["p"], i + 1)
            for t in range(NT):
                for b in range(NT):
                    last = pe.transpose(W[3][:, b * TOK + t * P:b * TOK + (t + 1) * P], prob[:, t, b * P:(b + 1) * P], ident)
            last.then_inc(h["pt"], 1)
            if more:
                rotated_values(i + 1)
            pe.wait_ge(h["ptev"], i + 1)
            pe.wait_ge(h["vev"], i + 1)
            for b in range(NT):
                last = pe.matmul(W[3][:, 0:TOK], v_sb[:, b, :], prob_t[:, b, :], start=(b == 0), stop=(b == NT - 1))
            last.then_inc(h["pv"], 1)

        queries_keys(0)
        rotated_values(0)
        head(0)
        head(1)
        with pe.Fori(2, HEADS - 1) as r:
            head(pe.snap(r))
        head(HEADS - 1)
        chunk_ready(pe, ph["mla"], 2, HEADS - 1)
        pe.wait_ge(h["ol"], HEADS)
        rows_out(pe, 2, oh, ol, False, True).then_inc(used[2], 1)

    def mla_act(act):
        split = hi_of(act)

        def take_qk(j):
            act.wait_ge(m["qk"], j + 1)
            act.activation(q_sb[:], W[0][:, 0:TOK], ACT.Copy)
            act.activation(k_sb[:], W[0][:, TOK:2 * TOK], ACT.Copy).then_inc(h["qkev"], 1)

        def head(i):
            first = isinstance(i, int) and i == 0
            more = not (isinstance(i, int) and i == HEADS - 1)
            act.wait_ge(h["mx"], i + 1)
            for t in range(NT):
                last = act.activation(prob[:, t, :], W[2][:, t * TOK:(t + 1) * TOK], ACT.Exp, bias=soft[:, 4 + t:5 + t],
                                      scale=MLA_SCALE, accum_out=soft[:, 8 + t:9 + t])
            last.then_inc(h["e"], 1)
            if more:
                take_qk(i + 1)
            if not first:
                refill(split, ph["mla"], 2, i - 1)
            act.wait_ge(h["pt"], i + 1)
            act.activation(prob_t[:], W[3][:].rearrange("p (b q) -> p b q", b=NT), ACT.Copy).then_inc(h["ptev"], 1)
            if more:
                refill(split, ph["mla"], 0, i + 1)
                refill(split, ph["mla"], 1, i + 1)
            act.wait_ge(h["pv"], i + 1)
            act.activation(oh[:], W[3][:, 0:TOK], ACT.Copy).then_inc(h["oh"], 1)

        take_qk(0)
        refill(split, ph["mla"], 0, 0)
        refill(split, ph["mla"], 1, 0)
        over(act, HEADS, head, 2)

    def mla_dve(dve):
        split = lo_of(dve)

        def rotate_queries(j):
            dve.wait_ge(used[1], ph["mla"].base[1] + j + 1)
            dve.tensor_tensor(qr_t[:], W[1][:, 0:TOK], cst("mla_rot"), ALU.mult).then_inc(h["roped"], 1)

        def take_values(j):
            if not (isinstance(j, int) and j == 0):
                dve.wait_ge(h["pv"], j)
            dve.tensor_copy(v_sb[:], W[1][:, TOK:2 * TOK].rearrange("p (t c) -> p t c", t=NT)).then_inc(h["vev"], 1)

        def head(i):
            first = isinstance(i, int) and i == 0
            more = not (isinstance(i, int) and i == HEADS - 1)
            chain = Chain(dve, h["sm"], 2, i)
            dve.wait_ge(h["s"], i + 1)
            chain(dve.tensor_reduce(soft[:, 0:2], W[2][:].rearrange("p (t k) -> p t k", t=NT), AX.X, ALU.max))
            dve.tensor_scalar(soft[:, 4:6], soft[:, 0:2], -MLA_SCALE, None, ALU.mult).then_inc(h["mx"], 1)
            for k in range(2):
                refill(split, ph["mla"], k, i)
            dve.wait_ge(h["e"], i + 1)
            chain(dve.reciprocal(soft[:, 12:14], soft[:, 8:10]))
            for t in range(NT):
                last = dve.tensor_scalar(prob[:, t, :], prob[:, t, :], soft[:, 12 + t:13 + t], None, ALU.mult)
            last.then_inc(h["p"], 1)
            if not first:
                refill(split, ph["mla"], 2, i - 1)
            if more:
                rotate_queries(i + 1)
                take_values(i + 1)
            dve.wait_ge(h["oh"], i + 1)
            dve.tensor_tensor(ol[:], W[3][:, 0:TOK], oh[:], ALU.subtract).then_inc(h["ol"], 1)

        rotate_queries(0)
        take_values(0)
        over(dve, HEADS, head, 2)

    f = [sems(f"f{j}", "g_mid v_mid g_tap v_tap gelu h32 hh hl") for j in range(2)]
    cg = [sb(f"cg{j}", [P, TOK]) for j in range(2)]
    cv = [sb(f"cv{j}", [P, TOK]) for j in range(2)]
    gelu = [sb(f"gelu{j}", [P, TOK]) for j in range(2)]
    h32 = [sb(f"h32_{j}", [P, TOK]) for j in range(2)]
    hh = [sb(f"hh{j}", [P, TOK], F32R) for j in range(2)]
    hl = [sb(f"hl{j}", [P, TOK], F32R) for j in range(2)]

    def ffn_pe(pe, layer):
        p = (ph["ffn0"], ph["ffn1"])[layer]
        done = layer * FFN_STEPS

        def up(j, i):
            for gate, bank in ((1, 2 * j), (0, 2 * j + 1)):
                chunk_ready(pe, p, bank, i)
                if not (isinstance(i, int) and i + done == 0):
                    pe.wait_ge(f[j]["g_tap"] if gate else f[j]["v_tap"], 2 * (i + done))
                first = isinstance(i, int) and i == 0 and j == 0 and gate
                project_t(pe, W[bank][:, 0:TOK], bank, arriving=2 * layer + 1 if first else None).then_inc(used[bank], 1)

        def down(j, i, start=False, stop=False):
            chunk_ready(pe, p, 4 + j, i)
            pe.wait_ge(f[j]["hl"], i + done + 1)
            rows_out(pe, 4 + j, hh[j], hl[j], start, stop).then_inc(used[4 + j], 1)

        def step(i):
            up(0, i)
            if not (isinstance(i, int) and i == 0):
                down(1, i - 1)
            up(1, i)
            down(0, i, start=isinstance(i, int) and i == 0)

        over(pe, FFN_STEPS, step)
        down(1, FFN_STEPS - 1, stop=True)

    def ffn_taps(layer, i, j, value, tap, lo_, hi_=None):
        at = layer * FFN_STEPS * 16 + (2 * j + value) * 4 + tap
        return vcol("ffn_conv", i * 16 + at, 1)

    def ffn_act(act, layer):
        p = (ph["ffn0"], ph["ffn1"])[layer]
        done = layer * FFN_STEPS
        split = hi_of(act)

        def block(j, i, between):
            late = j == 1 and isinstance(i, int) and i == FFN_STEPS - 1
            for value in range(2):
                bank, s = 2 * j + value, f[j]
                act.wait_ge(used[bank], p.base[bank] + i + 1)
                if value and not (isinstance(i, int) and i + done == 0):
                    act.wait_ge(s["h32"], i + done)
                act.activation((cg, cv)[value][j][:], W[bank][:, 0:TOK], ACT.Identity,
                               scale=ffn_taps(layer, i, j, value, 1, 0),
                               bias=ffn_taps(layer, i, j, value, 3, 0)).then_inc((s["g_mid"], s["v_mid"])[value], 1)
                if not late:
                    refill(split, p, bank, i)
            act.wait_ge(f[j]["g_tap"], 2 * (i + done) + 2)
            act.activation(gelu[j][:], cg[j][:], ACT.Gelu_apprx_tanh).then_inc(f[j]["gelu"], 1)
            act.wait_ge(f[j]["h32"], i + done + 1)
            if not (isinstance(i, int) and i + done == 0):
                act.wait_ge(used[4 + j], used_before(i, j))
            act.activation(hh[j][:], h32[j][:], ACT.Copy).then_inc(f[j]["hh"], 1)
            if late:
                for bank in (2 * j, 2 * j + 1):
                    refill(split, p, bank, i)
            between()

        def used_before(i, j):
            return p.base[4 + j] + i

        def step(i):
            if isinstance(i, int) and i == FFN_STEPS - 1:
                first_of_next(split, p)
            block(0, i, lambda: None if isinstance(i, int) and i == 0 else refill(split, p, 5, i - 1))
            block(1, i, lambda: refill(split, p, 4, i))

        over(act, FFN_STEPS, step)
        refill(split, p, 5, FFN_STEPS - 1)

    def ffn_dve(dve, layer):
        p = (ph["ffn0"], ph["ffn1"])[layer]
        done = layer * FFN_STEPS
        split = lo_of(dve)

        def block(j, i):
            last_step = isinstance(i, int) and i == FFN_STEPS - 1
            for value in range(2):
                bank, s = 2 * j + value, f[j]
                mid, tap, c = (s["g_mid"], s["v_mid"])[value], (s["g_tap"], s["v_tap"])[value], (cg, cv)[value][j]
                dve.wait_ge(mid, i + done + 1)
                dve.scalar_tensor_tensor(c[:, 1:TOK], W[bank][:, 0:TOK - 1], ffn_taps(layer, i, j, value, 0, 0),
                                         c[:, 1:TOK], ALU.mult, ALU.add).then_inc(tap, 1)
                dve.wait_ge(tap, 2 * (i + done) + 1)
                dve.scalar_tensor_tensor(c[:, 0:TOK - 1], W[bank][:, 1:TOK], ffn_taps(layer, i, j, value, 2, 0),
                                         c[:, 0:TOK - 1], ALU.mult, ALU.add).then_inc(tap, 1)
                if not (j and last_step):
                    refill(split, p, bank, i)

        def step(i):
            last_step = isinstance(i, int) and i == FFN_STEPS - 1
            block(0, i)
            if not (isinstance(i, int) and i == 0):
                refill(split, p, 5, i - 1)
            block(1, i)
            if last_step:
                for bank in (2, 3):
                    refill(split, p, bank, i)
                first_of_next(split, p)
            refill(split, p, 4, i)

        over(dve, FFN_STEPS, step)
        refill(split, p, 5, FFN_STEPS - 1)

    def ffn_pool(pool, layer):
        p = (ph["ffn0"], ph["ffn1"])[layer]
        done = layer * FFN_STEPS
        split = lo_of(pool, True)

        def hidden(j, i):
            s = f[j]
            pool.wait_ge(s["gelu"], i + done + 1)
            pool.wait_ge(s["v_tap"], 2 * (i + done) + 2)
            if not (isinstance(i, int) and i + done == 0):
                pool.wait_ge(s["hh"], i + done)
            pool.tensor_tensor(h32[j][:], gelu[j][:], cv[j][:], ALU.mult).then_inc(s["h32"], 1)
            pool.wait_ge(s["hh"], i + done + 1)
            pool.tensor_tensor(hl[j][:], h32[j][:], hh[j][:], ALU.subtract).then_inc(s["hl"], 1)

        def step(i):
            hidden(0, i)
            if not (isinstance(i, int) and i == 0):
                refill(split, p, 5, i - 1)
            refill(split, p, 0, i)
            refill(split, p, 1, i)
            hidden(1, i)
            refill(split, p, 2, i)
            refill(split, p, 3, i)
            refill(split, p, 4, i)
            if isinstance(i, int) and i == FFN_STEPS - 1:
                first_of_next(split, p)

        over(pool, FFN_STEPS, step)
        refill(split, p, 5, FFN_STEPS - 1)

    d = sems("d", "lam sq ms root on ot vtev vt")
    qz = [sb(f"qz{j}", [P, TOK]) for j in range(2)]
    lam = sb("lam", [P, 8])
    lam_prod = sb("lam_prod", [P, 2, 64])
    sub = sb("sub", [P, 1])
    onorm = sb("onorm", [P, NT, P])
    vt_sb = sb("vt_sb", [P, TOK])

    def diff_setup_dve(dve):
        for j in range(2):
            dve.memset(qz[j][:], 0.0)
        dve.tensor_scalar(sub[:], vcol("sub_gain"), 1.0 - LAM_INIT, None, ALU.mult)
        lp = vcol("lam").rearrange("p (a b c) -> p a b c", a=2, b=2)
        dve.tensor_tensor(lam_prod[:], lp[:, :, 0, :], lp[:, :, 1, :], ALU.mult).then_inc(d["lam"], 1)
        dve.wait_ge(d["lam"], 1)
        dve.tensor_reduce(lam[:, 0:2], lam_prod[:], AX.X, ALU.add).then_inc(d["lam"], 1)
        dve.wait_ge(d["lam"], 3)
        dve.tensor_tensor(lam[:, 4:5], lam[:, 3:4], lam[:, 2:3], ALU.subtract).then_inc(d["lam"], 1)
        dve.wait_ge(d["lam"], 4)
        dve.tensor_scalar(lam[:, 5:6], lam[:, 4:5], -LAM_INIT, None, ALU.add).then_inc(d["lam"], 1)

    def diff_setup_act(act):
        act.wait_ge(d["lam"], 2)
        act.activation(lam[:, 2:4], lam[:, 0:2], ACT.Exp).then_inc(d["lam"], 1)

    def diff_pe(pe):

        def queries_keys(j, k):
            chunk_ready(pe, ph["diff"], k, j)
            first = isinstance(j, int) and j == 0 and k == 0
            project_t(pe, W[0][:, k * TOK:(k + 1) * TOK], k, arriving=2 if first else None).then_inc(used[k], 1)

        def values(j):
            chunk_ready(pe, ph["diff"], 2, j)
            if not (isinstance(j, int) and j == 0):
                pe.wait_ge(h["vev"], j + DIFF_SEEN)
            project_t(pe, W[1][:, 0:TOK], 2).then_inc(used[2], 1)

        def turn_values(j):
            pe.wait_ge(d["vtev"], j + 1)
            for t in range(NT):
                last = pe.transpose(W[1][:, t * P:(t + 1) * P], vt_sb[:, t * P:(t + 1) * P], ident)
            last.then_inc(d["vt"], 1)

        def turn_result(i):
            pe.wait_ge(d["on"], i + 1)
            for t in range(NT):
                last = pe.transpose(W[3][:, t * P:(t + 1) * P], onorm[:, t, :], ident)
            last.then_inc(d["ot"], 1)

        def add_output(i):
            chunk_ready(pe, ph["diff"], 3, i)
            pe.wait_ge(h["ol"], i + 1 + DIFF_SEEN)
            int_ = isinstance(i, int)
            rows_out(pe, 3, oh, ol, int_ and i == 0, int_ and i == HEADS - 1).then_inc(used[3], 1)

        def head(i):
            first = isinstance(i, int) and i == 0
            more = not (isinstance(i, int) and i == HEADS - 1)
            pe.wait_ge(h["qkev"], i + 1 + DIFF_SEEN)
            if not first:
                pe.wait_ge(h["ptev"], i + DIFF_SEEN)
            for j in range(2):
                for t in range(NT):
                    last = pe.matmul(W[2 + j][:, t * TOK:(t + 1) * TOK], qz[j][:, t * P:(t + 1) * P], k_sb[:],
                                     start=True, stop=True)
            last.then_inc(h["s"], 1)
            if more:
                values(i + 1)
            if not first:
                turn_result(i - 1)
            if more:
                for k in range(2):
                    queries_keys(i + 1, k)
            pe.wait_ge(h["p"], i + 1 + DIFF_SEEN)
            for t in range(NT):
                for b in range(NT):
                    last = pe.transpose(W[2][:, b * TOK + t * P:b * TOK + (t + 1) * P], prob[:, t, b * P:(b + 1) * P], ident)
            last.then_inc(h["pt"], 1)
            if not first:
                add_output(i - 1)
            if more:
                turn_values(i + 1)
                pe.wait_ge(h["qkev"], i + 2 + DIFF_SEEN)
            pe.wait_ge(h["ptev"], i + 1 + DIFF_SEEN)
            pe.wait_ge(h["vev"], i + 1 + DIFF_SEEN)
            for t in range(NT):
                for b in range(NT):
                    last = pe.matmul(W[0][:, t * P:(t + 1) * P], prob_t[:, b, t * P:(t + 1) * P], v_sb[:, b, :],
                                     start=(b == 0), stop=(b == NT - 1))
            last.then_inc(h["pv"], 1)

        for k in range(2):
            queries_keys(0, k)
        values(0)
        turn_values(0)
        head(0)
        head(1)
        with pe.Fori(2, HEADS - 1) as r:
            head(pe.snap(r))
        head(HEADS - 1)
        turn_result(HEADS - 1)
        add_output(HEADS - 1)

    def diff_act(act):
        split = hi_of(act)

        def take_qk(j):
            act.wait_ge(used[1], ph["diff"].base[1] + j + 1)
            act.activation(qz[0][0:64, :], W[0][0:64, 0:TOK], ACT.Copy)
            act.activation(qz[1][64:P, :], W[0][64:P, 0:TOK], ACT.Copy)
            act.activation(k_sb[:], W[0][:, TOK:2 * TOK], ACT.Copy).then_inc(h["qkev"], 1)

        def take_values(j):
            act.wait_ge(used[2], ph["diff"].base[2] + j + 1)
            act.activation(vt_sb[:], W[1][:, 0:TOK], ACT.Copy).then_inc(d["vtev"], 1)

        def result_high(i):
            act.wait_ge(d["ot"], i + 1)
            act.activation(oh[:], W[3][:, 0:TOK], ACT.Copy, scale=sub[:]).then_inc(h["oh"], 1)

        def head(i):
            first = isinstance(i, int) and i == 0
            more = not (isinstance(i, int) and i == HEADS - 1)
            act.wait_ge(h["mx"], i + 1 + DIFF_SEEN)
            for k in range(4):
                last = act.activation(prob[:, k, :], prob[:, k, :], ACT.Exp, bias=soft[:, 4 + k:5 + k],
                                      scale=DIFF_SCALE, accum_out=soft[:, 8 + k:9 + k])
            last.then_inc(h["e"], 1)
            if not first:
                result_high(i - 1)
            if more:
                take_values(i + 1)
                refill(split, ph["diff"], 2, i + 1)
                refill(split, ph["diff"], 0, i + 1)
                take_qk(i + 1)
            act.wait_ge(h["pt"], i + 1 + DIFF_SEEN)
            act.activation(prob_t[:], W[2][:].rearrange("p (b q) -> p b q", b=NT), ACT.Copy).then_inc(h["ptev"], 1)
            if more:
                refill(split, ph["diff"], 1, i + 1)
            else:
                first_of_next(split, ph["diff"])
            if not first:
                refill(split, ph["diff"], 3, i - 1)
            act.wait_ge(h["pv"], i + 1 + DIFF_SEEN)
            for t in range(NT):
                last = act.activation(junk[:, t * P:(t + 1) * P], W[0][:, t * P:(t + 1) * P], ACT.Square,
                                      accum_out=stat[:, 4 + t:5 + t])
            last.then_inc(d["sq"], 1)

        act.wait_ge(d["lam"], 1)
        refill(split, ph["diff"], 0, 0)
        take_qk(0)
        refill(split, ph["diff"], 1, 0)
        take_values(0)
        refill(split, ph["diff"], 2, 0)
        over(act, HEADS, head, 2)
        result_high(HEADS - 1)

    def diff_dve(dve):
        split = lo_of(dve)
        dist = cst("dist")

        def take_values(j):
            dve.wait_ge(d["vt"], j + 1)
            if not (isinstance(j, int) and j == 0):
                dve.wait_ge(h["pv"], j + DIFF_SEEN)
            dve.tensor_copy(v_sb[:], W[1][:, 0:TOK].rearrange("p (t c) -> p t c", t=NT)).then_inc(h["vev"], 1)

        def result_mean(i):
            dve.wait_ge(d["sq"], i + 1)
            dve.tensor_scalar(mean[:, 4:6], stat[:, 4:6], 1.0 / P, EPS, ALU.mult, ALU.add).then_inc(d["ms"], 1)

        def result_norm(i):
            dve.wait_ge(d["root"], i + 1)
            for t in range(NT):
                last = dve.tensor_scalar(onorm[:, t, :], W[0][:, t * P:(t + 1) * P], stat[:, 12 + t:13 + t],
                                         None, ALU.mult)
            last.then_inc(d["on"], 1)

        def result_low(i):
            dve.wait_ge(h["oh"], i + 1 + DIFF_SEEN)
            dve.scalar_tensor_tensor(ol[:], W[3][:, 0:TOK], sub[:], oh[:], ALU.mult, ALU.subtract).then_inc(h["ol"], 1)

        def head(i):
            first = isinstance(i, int) and i == 0
            more = not (isinstance(i, int) and i == HEADS - 1)
            if not first:
                result_mean(i - 1)
            chain = Chain(dve, h["sm"], 5, i, 2 * HEADS)
            dve.wait_ge(h["s"], i + 1 + DIFF_SEEN)
            for j in range(2):
                last = dve.scalar_tensor_tensor(prob[:, 2 * j:2 * j + 2, :].rearrange("p t k -> p (t k)"), dist,
                                                vcol("slope", i, 1), W[2 + j][:], ALU.mult, ALU.add)
            chain(last)
            if not first:
                result_norm(i - 1)
            chain(dve.tensor_reduce(soft[:, 0:4], prob[:], AX.X, ALU.max))
            dve.tensor_scalar(soft[:, 4:8], soft[:, 0:4], -DIFF_SCALE, None, ALU.mult).then_inc(h["mx"], 1)
            dve.wait_ge(h["e"], i + 1 + DIFF_SEEN)
            chain(dve.reciprocal(soft[:, 12:16], soft[:, 8:12]))
            chain(dve.tensor_scalar(soft[:, 14:16], soft[:, 14:16], lam[:, 5:6], None, ALU.mult))
            for t in range(NT):
                last = dve.tensor_scalar(prob[:, t, :], prob[:, t, :], soft[:, 12 + t:13 + t], None, ALU.mult)
            chain(last)
            for t in range(NT):
                last = dve.scalar_tensor_tensor(prob[:, t, :], prob[:, 2 + t, :], soft[:, 14 + t:15 + t], prob[:, t, :],
                                                ALU.mult, ALU.add)
            last.then_inc(h["p"], 1)
            if not first:
                result_low(i - 1)
            if more:
                refill(split, ph["diff"], 2, i + 1)
                refill(split, ph["diff"], 0, i + 1)
                refill(split, ph["diff"], 1, i + 1)
            else:
                first_of_next(split, ph["diff"])
            if not first:
                refill(split, ph["diff"], 3, i - 1)
            if more:
                take_values(i + 1)

        dve.wait_ge(d["lam"], 5)
        for k in (0, 1):
            refill(split, ph["diff"], k, 0)
        take_values(0)
        refill(split, ph["diff"], 2, 0)
        over(dve, HEADS, head, 2)
        result_mean(HEADS - 1)
        result_norm(HEADS - 1)
        result_low(HEADS - 1)

    def diff_pool(pool):
        split = lo_of(pool, True)

        def result_root(i):
            pool.wait_ge(d["ms"], i + 1)
            pool.tensor_tensor(stat[:, 12:14], mean[:, 4:6], power[:, 0:2], ALU.pow).then_inc(d["root"], 1)

        def head(i):
            first = isinstance(i, int) and i == 0
            more = not (isinstance(i, int) and i == HEADS - 1)
            if not first:
                result_root(i - 1)
            if not more:
                first_of_next(split, ph["diff"])
            if more:
                refill(split, ph["diff"], 2, i + 1)
                refill(split, ph["diff"], 0, i + 1)
                refill(split, ph["diff"], 1, i + 1)
            if not first:
                refill(split, ph["diff"], 3, i - 1)

        for k in (0, 1, 2):
            refill(split, ph["diff"], k, 0)
        over(pool, HEADS, head, 2)
        result_root(HEADS - 1)

    close_scope()

    z_ = sems("z", "pe act dve")
    gate = {n: sb(f"gate_{n}", [P, HEADS, NT]) for n in
            "z neg abs e ln sp ea g cum eg th beta vbeta tot bg kdx kd".split()}
    grown_all = sb("grown_all", [P, HEADS, P])
    cum_all = sb("cum_all", [P, 2 * HEADS, P])
    gdn_gain = sb("gdn_gain", [P, 1])
    obh, obl = sb("obh", [P, HEADS, TOK], F32R), sb("obl", [P, HEADS, TOK], F32R)

    def flat(t):
        return t[:].rearrange("p h t -> p (h t)")

    def gates_pe(pe):
        pe.wait_ge(n_["xl"], KB * 5)
        chunk_ready(pe, ph["gates"], 4, 0)
        for t in range(NT):
            for b in range(KB):
                last = mm3(pe, W[0][:, t * 16:(t + 1) * 16], (xh[:, b, t * P:(t + 1) * P], xl[:, b, t * P:(t + 1) * P]),
                           wslot(4, b * 16, (b + 1) * 16), b == 0, b == KB - 1)
        last.then_inc(used[4], 1)
        pe.wait_ge(z_["dve"], 5)
        pe.matmul(W[1][:, 0:16], cst("upper"), flat(gate["g"]), start=True, stop=True)
        pe.matmul(W[1][:, 16:32], cst("ones"), flat(gate["g"]), start=True, stop=True).then_inc(z_["pe"], 1)
        for c in range(2 * HEADS):
            last = pe.matmul(acc[:, c // 4, (c % 4) * P:(c % 4 + 1) * P], flat(gate["g"])[:, c:c + 1].to_broadcast([P, P]),
                             cst("upper"), start=True, stop=True)
        last.then_inc(z_["pe"], 1)

    def gates_act(act):
        act.wait_ge(z_["dve"], 1)
        act.activation(gate["th"][:], W[0][:, 0:32].rearrange("p (t x) -> p x t", t=NT)[:, 0:8, :], ACT.Tanh,
                       scale=0.5).then_inc(z_["act"], 1)
        act.wait_ge(z_["dve"], 3)
        act.activation(gate["e"][:], gate["abs"][:], ACT.Exp, scale=-1.0).then_inc(z_["act"], 1)
        act.activation(flat(gate["ea"]), vcol("a_log"), ACT.Exp).then_inc(z_["act"], 1)
        act.wait_ge(z_["act"], 2)
        act.activation(gate["ln"][:], gate["e"][:], ACT.Ln, bias=1.0).then_inc(z_["act"], 1)
        act.wait_ge(z_["dve"], 10)
        act.activation(gate["eg"][:], gate["cum"][:], ACT.Exp).then_inc(z_["act"], 1)
        act.activation(gate["kd"][:], gate["kdx"][:], ACT.Exp).then_inc(z_["act"], 1)
        act.wait_ge(z_["pe"], 2)
        act.activation(cum_all[:], acc[:].rearrange("p a (c k) -> p (a c) k", c=4), ACT.Copy).then_inc(z_["act"], 1)
        act.activation(grown_all[:], acc[:].rearrange("p a (h t k) -> p (a h) t k", h=2, t=NT)[:, :, 1, :],
                       ACT.Exp).then_inc(z_["act"], 1)
        refill(hi_of(act), ph["gates"], 4, 0)

    def gates_dve(dve):
        dve.wait_ge(used[4], ph["gates"].base[4] + 1)
        dec = W[0][:, 0:32].rearrange("p (t x) -> p x t", t=NT)[:, 8:16, :]
        dve.tensor_tensor(gate["z"][:], dec, vcol("dt").rearrange("p (h t) -> p h t", t=NT), ALU.add).then_inc(z_["dve"], 1)
        dve.wait_ge(z_["dve"], 1)
        dve.tensor_scalar(gate["neg"][:], gate["z"][:], -1.0, None, ALU.mult).then_inc(z_["dve"], 1)
        dve.wait_ge(z_["dve"], 2)
        dve.tensor_tensor(gate["abs"][:], gate["z"][:], gate["neg"][:], ALU.max).then_inc(z_["dve"], 1)
        dve.wait_ge(z_["act"], 4)
        dve.scalar_tensor_tensor(gate["sp"][:], gate["z"][:], 0.0, gate["ln"][:], ALU.max, ALU.add).then_inc(z_["dve"], 1)
        dve.wait_ge(z_["dve"], 4)
        dve.scalar_tensor_tensor(gate["g"][:], gate["sp"][:], -1.0, gate["ea"][:], ALU.mult, ALU.mult).then_inc(z_["dve"], 1)
        dve.tensor_scalar(gate["beta"][:], gate["th"][:], 1.0, 0.5, ALU.add, ALU.mult).then_inc(z_["dve"], 1)
        dve.wait_ge(z_["dve"], 6)
        dve.tensor_scalar(gate["vbeta"][:], gate["beta"][:], 0.5, None, ALU.mult).then_inc(z_["dve"], 1)
        dve.tensor_scalar(gdn_gain[:], vcol("gdn_gain"), 0.5, None, ALU.mult).then_inc(z_["dve"], 1)
        dve.wait_ge(z_["pe"], 1)
        dve.tensor_copy(flat(gate["cum"]), W[1][:, 0:16]).then_inc(z_["dve"], 1)
        dve.wait_ge(z_["dve"], 9)
        dve.tensor_tensor(flat(gate["kdx"]), W[1][:, 16:32], flat(gate["cum"]), ALU.subtract).then_inc(z_["dve"], 1)
        dve.wait_ge(z_["act"], 5)
        dve.tensor_tensor(gate["bg"][:], gate["eg"][:], gate["beta"][:], ALU.mult).then_inc(z_["dve"], 1)
        dve.wait_ge(z_["act"], 6)
        dve.wait_ge(z_["dve"], 11)

    taps = [sems(f"c{x}", "mid tap th silu" if x < 3 else "tap th") for x in range(4)]
    e_ = sems("e", "turned turned_v sums cums tv grown sq mean root tk back backev dd exp lu be kk mk mt mtev init_g bm init_v "
              "xm tt x t f1 f1ev f2 f2ev f3 f3ev f4 osq oss om oroot on ot o32 oh ol chain")
    tanh_ = [sb(f"tanh{x}", [P, TOK]) for x in range(4)]
    open_scope()
    conv = [sb(f"conv{x}", [P, TOK]) for x in range(3)]
    silu2 = sb("silu2", [P, 6, TOK])
    z2 = hn[:].rearrange("p t (h k) -> p (t h) k", k=TOK)
    ssq = sb("ssq", [P, 8])
    ssq4, mean4, root4 = sb("ssq4", [P, 4]), sb("mean4", [P, 4]), sb("root4", [P, 4])
    mean8, root8, fac8 = sb("mean8", [P, 8]), sb("root8", [P, 8]), sb("fac8", [P, 8])
    sq = sb("sq", [P, 8, P])
    qk_tok = sb("qk_tok", [P, 2, 4, P])
    kdec, kbg = sb("kdec", [P, 2, P]), sb("kbg", [P, 2, P])
    vbeta = sb("vbeta", [P, 4, P])
    qk_t = silu2[:, 0:4, :].rearrange("p (e x) (c k) -> p e (x c) k", e=2, c=2)
    qdec_t = sb("qdec_t", [P, 2, P])
    dec_l, dec_u = sb("dec_l", [P, 4, P]), sb("dec_u", [P, 4, P])
    mask_e = sb("mask_e", [P, 2, 2, 2, P])
    mk = sb("mk", [P, 2, 2, 2, P])
    mt = sb("mt", [P, 4, P])
    inv = sb("inv", [P, 2, 4, P])
    bm = sb("bm", [P, 2, 4, P])
    dcum = bm[:, 0, :, :]
    xm = sb("xm", [P, 4, P])
    vnew = sb("vnew", [P, 2, 2, P])
    nwt = sb("nwt", [P, 2, P])
    state = sb("state", [P, 2, P])
    ogn = sb("ogn", [P, 4, P])
    og32 = sb("og32", [P, 2, TOK])

    def quad(bank):
        return bank[:].rearrange("p (a k) -> p a k", a=4)

    A = [acc[:, k, :] for k in range(4)]
    level_of = cst("levels", "p (l k) -> p l k", l=LEVELS)
    BLOCKS = [(0, 0), (1, 0), (2, 0), (0, 1), (1, 1), (2, 1)]

    def source(x, e, j):
        return (ph["gdn"], x, 2 * j + e) if x < 3 else (ph["gdnz"], 3 + e, j)

    def gdn_block(pe, x, e, j, part):
        b_ = 2 * j + e
        p, slot, c = source(x, e, j)
        if part == 0:
            chunk_ready(pe, p, slot, c)
            if not (isinstance(b_, int) and b_ == 0):
                pe.wait_ge(taps[x]["tap"], 3 * b_ if x < 3 else b_)
        for s in range(12 * part, 12 * part + 12):
            b, term = divmod(s, 3)
            l, r = ((high, xh), (high, xl), (low, xh))[term]
            last = pe.matmul(W[x][:, 0:TOK], l[slot][:, b * P:(b + 1) * P], r[:, b, :], start=(s == 0), stop=(s == 23))
        if part == 1:
            last.then_inc(used[slot], 1)

    def block_act(act, split, x, e, j):
        block_mid_act(act, split, x, e, j)
        block_end_act(act, x, e, j)

    def block_mid_act(act, split, x, e, j):
        b_ = 2 * j + e
        p, slot, c = source(x, e, j)
        act.wait_ge(used[slot], p.base[slot] + c + 1)
        if x < 3:
            if not (isinstance(b_, int) and b_ == 0):
                act.wait_ge(taps[x]["silu"], b_)
            act.activation(conv[x][:], W[x][:, 0:TOK], ACT.Copy, scale=conv_tap(b_, x, 3)).then_inc(taps[x]["mid"], 1)
            refill(split, p, slot, c)
        else:
            if not (isinstance(b_, int) and b_ == 0):
                act.wait_ge(taps[x]["tap"], b_)
            act.activation(tanh_[x][:], W[x][:, 0:TOK], ACT.Tanh, scale=0.5).then_inc(taps[x]["th"], 1)
            refill(split, p, slot, c)

    def block_end_act(act, x, e, j):
        if x < 3:
            act.wait_ge(taps[x]["tap"], 3 * (2 * j + e) + 3)
            act.activation(tanh_[x][:], conv[x][:], ACT.Tanh, scale=0.5).then_inc(taps[x]["th"], 1)

    def conv_tap(b_, x, tap):
        return vcol("conv", b_ * 12 + (x * 4 + tap), 1)

    def block_dve(dve, x, e, j):
        b_ = 2 * j + e
        if x < 3:
            dve.wait_ge(taps[x]["mid"], b_ + 1)
            for n, back in enumerate((1, 2, 3)):
                dve.scalar_tensor_tensor(conv[x][:, back:TOK], W[x][:, 0:TOK - back], conv_tap(b_, x, 3 - back),
                                         conv[x][:, back:TOK], ALU.mult, ALU.add).then_inc(taps[x]["tap"], 1)
                if n < 2:
                    dve.wait_ge(taps[x]["tap"], 3 * b_ + n + 1)
            dve.wait_ge(taps[x]["th"], b_ + 1)
            if (x, e) == BLOCKS[0] and not is0(j):
                dve.wait_ge(e_["grown"], j)
            dve.scalar_tensor_tensor(silu2[:, 3 * e + x, :], tanh_[x][:], 1.0, conv[x][:], ALU.add, ALU.mult).then_inc(taps[x]["silu"], 1)
        else:
            dve.wait_ge(taps[x]["th"], b_ + 1)
            dst = z2[:, b_, :] if isinstance(b_, int) else z2[:, bass.ds(b_, 1), :].rearrange("p a k -> p (a k)")
            dve.scalar_tensor_tensor(dst, tanh_[x][:], 1.0, W[x][:, 0:TOK], ALU.add, ALU.mult).then_inc(taps[x]["tap"], 1)

    def is0(j):
        return isinstance(j, int) and j == 0

    def turn_pe(pe, j):
        for x in range(2):
            pe.wait_ge(taps[x]["silu"], 2 * j + 2)
        for e in range(2):
            for x in range(2):
                for t in range(NT):
                    last = pe.transpose(W[e][:, (2 * x + t) * P:(2 * x + t + 1) * P], silu2[:, 3 * e + x, t * P:(t + 1) * P], ident)
        last.then_inc(e_["turned"], 1)

    def turn_values_pe(pe, j):
        pe.wait_ge(taps[2]["silu"], 2 * j + 2)
        for e in range(2):
            for t in range(NT):
                last = pe.transpose(W[2][:, (2 * e + t) * P:(2 * e + t + 1) * P], silu2[:, 3 * e + 2, t * P:(t + 1) * P], ident)
        last.then_inc(e_["turned_v"], 1)

    def back_pe(pe, j):
        pe.wait_ge(e_["tk"], j + 1)
        for e in range(2):
            for c in range(4):
                last = pe.transpose(W[e][:, c * P:(c + 1) * P], qk_tok[:, e, c, :], ident)
        last.then_inc(e_["back"], 1)

    def products_pe(pe, j):
        pe.wait_ge(e_["backev"], j + 1)
        if is0(j):
            pe.wait_ge(z_["act"], 8)
        for e in range(2):
            for which in range(2):
                for t in range(NT):
                    c = 2 * which + t
                    last = pe.matmul(A[2 + e][:, c * P:(c + 1) * P], qk_t[:, e, 2 + t, :],
                                     qk_t[:, e, 2 + t if which == 0 else t, :], start=True, stop=True)
        last.then_inc(e_["kk"], 1)

    def turn_m_pe(pe, j):
        pe.wait_ge(e_["mk"], j + 1)
        pe.wait_ge(e_["tv"], j + 1)
        for e in range(2):
            for t in range(NT):
                last = pe.transpose(W[2][:, (2 * e + t) * P:(2 * e + t + 1) * P], mk[:, e, 0, t, :], ident)
        last.then_inc(e_["mt"], 1)

    def squares_act(act, j, e):
        if e == 0:
            act.wait_ge(e_["turned"], j + 1)
        act.activation(sq[:, 4 * e:4 * e + 4, :], quad(W[e]), ACT.Square).then_inc(e_["sq"], 1)

    def decay_act(act, j):
        act.wait_ge(e_["dd"], j + 1)
        if not is0(j):
            act.wait_ge(e_["be"], j)
        act.activation(dec_l[:], dec_l[:], ACT.Exp, scale=-1.0)
        act.activation(dec_u[:], dec_u[:], ACT.Exp).then_inc(e_["exp"], 1)

    def back_act(act, j):
        act.wait_ge(e_["back"], j + 1)
        for e in range(2):
            last = act.activation(qk_t[:, e, :, :], quad(W[e]), ACT.Copy)
        last.then_inc(e_["backev"], 1)

    def mt_act(act, j):
        act.wait_ge(e_["mt"], j + 1)
        act.activation(mt[:], quad(W[2]), ACT.Copy).then_inc(e_["mtev"], 1)

    def gate_at(name, j, step=1, chunk=None):
        v = flat(gate[name])
        if isinstance(j, int):
            v = v[:, 4 * j:4 * j + 4]
        else:
            v = v[:, bass.ds(j * 4, 4)]
        return v if chunk is None else v.rearrange("p (h t) -> p h t", t=NT)[:, :, chunk]

    def squares_dve(dve, j):
        dve.wait_ge(e_["sq"], 2 * j + 2)
        chain = Chain(dve, e_["sums"], 1, j)
        chain(dve.tensor_reduce(ssq[:], sq[:], AX.X, ALU.add))
        dve.tensor_scalar(mean8[:], ssq[:], 0.25, EPS, ALU.mult, ALU.add).then_inc(e_["mean"], 1)

    def decay_dve(dve, j):
        chain = Chain(dve, e_["cums"], 1, j)
        if is0(j):
            dve.wait_ge(z_["act"], 8)
        c = cum_all[:, 4 * j:4 * j + 4, :] if isinstance(j, int) else cum_all[:, bass.ds(j * 4, 4), :]
        chain(dve.tensor_tensor(dcum, c, spread(gate_at("cum", j), P), ALU.subtract))
        if not is0(j):
            dve.wait_ge(e_["be"], j)
        dve.tensor_scalar(dec_l[:], dcum, 0.0, None, ALU.max)
        dve.tensor_scalar(dec_u[:], dcum, 0.0, None, ALU.min).then_inc(e_["dd"], 1)

    def norm_dve(dve, j):
        chain = Chain(dve, e_["chain"], 1, j)
        dve.wait_ge(e_["root"], j + 1)
        chain(dve.tensor_tensor(fac8[:], root8[:], vcol("l2_factor"), ALU.mult))
        for e in range(2):
            last = dve.tensor_tensor(qk_tok[:, e, :, :], quad(W[e]), spread(fac8[:, 4 * e:4 * e + 4], P), ALU.mult)
        last.then_inc(e_["tk"], 1)

    def scaled_dve(dve, j):
        if not is0(j):
            dve.wait_ge(e_["f3"], j)
        dve.wait_ge(e_["tk"], j + 1)
        dve.tensor_tensor(kdec[:], qk_tok[:, :, 2, :], spread(gate_at("kd", j, chunk=0), P), ALU.mult)
        dve.tensor_tensor(kbg[:], qk_tok[:, :, 3, :], spread(gate_at("bg", j, chunk=1), P), ALU.mult)
        dve.wait_ge(e_["turned_v"], j + 1)
        dve.tensor_tensor(vbeta[:], quad(W[2]), spread(gate_at("vbeta", j), P), ALU.mult).then_inc(e_["tv"], 1)

    def masked_dve(dve, j):
        dve.wait_ge(e_["kk"], j + 1)
        dve.wait_ge(e_["be"], j + 1)
        for e in range(2):
            last = dve.tensor_tensor(mk[:, e, :, :, :].rearrange("p a t k -> p (a t) k"), quad(A[2 + e]),
                                     mask_e[:, e, :, :, :].rearrange("p a t k -> p (a t) k"), ALU.mult)
        last.then_inc(e_["mk"], 1)

    def init_dve(dve, j):
        dve.wait_ge(e_["mtev"], j + 1)
        chain = Chain(dve, e_["init_v"], 2, j)
        chain(dve.tensor_tensor(bm[:, 1, :, :], mt[:], repeat(cst("level1_t"), 4), ALU.mult))
        chain(dve.tensor_tensor(inv[:, 1, :, :], repeat(ident, 4), bm[:, 1, :, :], ALU.subtract))

    def root_pool(pool, j):
        pool.wait_ge(e_["mean"], j + 1)
        pool.tensor_tensor(root8[:], mean8[:], power[:], ALU.pow).then_inc(e_["root"], 1)

    def mask_pool(pool, j):
        pool.wait_ge(e_["exp"], j + 1)
        if not is0(j):
            pool.wait_ge(e_["mk"], j)
        for e in range(2):
            pool.tensor_tensor(mask_e[:, e, 1, :, :], dec_u[:, 2 * e:2 * e + 2, :], repeat(cst("upper"), NT), ALU.mult)
        last = pool.tensor_tensor(dec_l[:], dec_l[:], repeat(cst("strict_lower"), 4), ALU.mult)
        last.then_inc(e_["lu"], 1)
        pool.wait_ge(e_["lu"], j + 1)
        for e in range(2):
            last = pool.tensor_tensor(mask_e[:, e, 0, :, :], dec_l[:, 2 * e:2 * e + 2, :],
                                      spread(gate_at("beta", j)[:, 2 * e:2 * e + 2], P), ALU.mult)
        last.then_inc(e_["be"], 1)

    def grow_pool(pool, j):
        pool.wait_ge(e_["backev"], j + 1)
        if not is0(j):
            pool.wait_ge(e_["f4"], j)
        g2 = grown_all[:, 2 * j:2 * j + 2, :] if isinstance(j, int) else grown_all[:, bass.ds(j * 2, 2), :]
        pool.tensor_tensor(qdec_t[:], qk_t[:, :, 1, :], g2, ALU.mult).then_inc(e_["grown"], 1)

    def init_pool(pool, j):
        pool.wait_ge(e_["mk"], j + 1)
        if not is0(j):
            pool.wait_ge(e_["f3"], j)
        for e in range(2):
            last = pool.tensor_tensor(bm[:, 0, 2 * e:2 * e + 2, :], mk[:, e, 0, :, :], repeat(cst("level1"), NT), ALU.mult)
        last.then_inc(e_["bm"], 1)
        pool.wait_ge(e_["bm"], j + 1)
        pool.tensor_tensor(inv[:, 0, :, :], repeat(ident, 4), bm[:, 0, :, :], ALU.subtract).then_inc(e_["init_g"], 1)

    def level_x(pe, l, j):
        if l == 0:
            pe.wait_ge(e_["init_g"], j + 1)
            pe.wait_ge(e_["init_v"], 2 * j + 2)
        else:
            pe.wait_ge(e_["tt"], LEVELS * j + l)
        for c in range(4):
            last = pe.matmul(A[0][:, c * P:(c + 1) * P], mt[:, c, :], inv[:, 0, c, :], start=True, stop=True)
        last.then_inc(e_["x"], 1)

    def level_t(pe, l, j):
        pe.wait_ge(e_["xm"], LEVELS * j + l + 1)
        for c in range(4):
            if l < LEVELS - 1:
                pe.matmul(A[2][:, c * P:(c + 1) * P], inv[:, 1, c, :], xm[:, c, :], start=True, stop=True)
            last = pe.matmul(A[3][:, c * P:(c + 1) * P], xm[:, c, :], inv[:, 1, c, :], start=True, stop=True)
        last.then_inc(e_["t"], 1)

    def level_xm(dve, l, j):
        dve.wait_ge(e_["x"], LEVELS * j + l + 1)
        dve.tensor_tensor(xm[:], quad(A[0]), repeat(level_of[:, l, :], 4), ALU.mult).then_inc(e_["xm"], 1)

    def level_tt(dve, l, j):
        dve.wait_ge(e_["t"], LEVELS * j + l + 1)
        if l < LEVELS - 1:
            dve.tensor_tensor(inv[:].rearrange("p a c k -> p (a c k)"), inv[:].rearrange("p a c k -> p (a c k)"),
                              acc[:, 2:4, :].rearrange("p a b -> p (a b)"), ALU.subtract).then_inc(e_["tt"], 1)
        else:
            dve.tensor_tensor(inv[:, 1, :, :], inv[:, 1, :, :], quad(A[3]), ALU.subtract).then_inc(e_["tt"], 1)

    def att_start_pe(pe, part):
        for s in range(6 * part, 6 * part + 6):
            b, term = s // 3 % 8, s % 3
            if s < 48:
                t, k, o = s // 24, b // 4, b % 4 * TOK
                x, w = ((xh, high), (xh, low), (xl, high))[term]
                ops = x[:, b, t * P:(t + 1) * P], w[k][:, o:o + TOK]
                out, first, ended = W[0][:, t * TOK:(t + 1) * TOK], t == 0 and b in (0, 4), t == 1 and b in (3, 7)
            else:
                k, o = 2, b * P
                w, x = ((high, xh), (high, xl), (low, xh))[term]
                ops = w[k][:, o:o + P], x[:, b, :]
                out, first, ended = W[1][:, 0:TOK], b == 0, b == 7
            if first and term == 0:
                chunk_ready(pe, ph["att"], k, 0)
            last = pe.matmul(out, *ops, start=(b == 0 and term == 0), stop=(b == 7 and term == 2))
            if ended and term == 2:
                last.then_inc(used[k], 1)

    def pair_pe(pe, i):
        more = not (isinstance(i, int) and i == PAIRS - 1)
        for l in range(LEVELS):
            for half in range(2):
                (level_x, level_t)[half](pe, l, i)
                gap = 2 * l + half
                if more:
                    gdn_block(pe, *BLOCKS[gap // 2], i + 1, gap % 2)
                    if gap == 11:
                        turn_pe(pe, i + 1)
                else:
                    att_start_pe(pe, gap)
        pe.wait_ge(e_["tt"], LEVELS * (i + 1))
        for e in range(2):
            pe.matmul(A[0][:, e * P:(e + 1) * P], inv[:, 1, 2 * e, :], vbeta[:, 2 * e, :], start=True, stop=True)
        for e in range(2):
            last = pe.matmul(A[0][:, (2 + e) * P:(3 + e) * P], kbg[:, e, :], inv[:, 1, 2 * e + 1, :], start=True, stop=True)
        last.then_inc(e_["f1"], 1)
        if more:
            gdn_block(pe, 3, 0, i + 1, 0)
        pe.wait_ge(e_["f1ev"], i + 1)
        for e in range(2):
            last = pe.matmul(A[1][:, e * P:(e + 1) * P], kdec[:, e, :], vnew[:, 0, e, :], start=True, stop=True)
        last.then_inc(e_["f2"], 1)
        if more:
            gdn_block(pe, 3, 0, i + 1, 1)
        pe.wait_ge(e_["f2ev"], i + 1)
        for e in range(2):
            pe.matmul(A[0][:, e * P:(e + 1) * P], inv[:, 1, 2 * e + 1, :], vbeta[:, 2 * e + 1, :], start=True, stop=False)
            last = pe.matmul(A[0][:, e * P:(e + 1) * P], nwt[:, e, :], state[:, e, :], start=False, stop=True)
        last.then_inc(e_["f3"], 1)
        if more:
            turn_values_pe(pe, i + 1)
            back_pe(pe, i + 1)
        pe.wait_ge(e_["f3ev"], i + 1)
        pe.wait_ge(e_["grown"], i + 1)
        for e in range(2):
            pe.matmul(A[1][:, 2 * e * P:(2 * e + 1) * P], mk[:, e, 1, 0, :], vnew[:, 0, e, :], start=True, stop=True)
            o = A[1][:, (2 * e + 1) * P:(2 * e + 2) * P]
            pe.matmul(o, mk[:, e, 1, 1, :], vnew[:, 1, e, :], start=True, stop=False)
            last = pe.matmul(o, qdec_t[:, e, :], state[:, e, :], start=False, stop=True)
        last.then_inc(e_["f4"], 1)
        if more:
            gdn_block(pe, 3, 1, i + 1, 0)
            products_pe(pe, i + 1)
            gdn_block(pe, 3, 1, i + 1, 1)
        pe.wait_ge(e_["on"], i + 1)
        for c in range(4):
            last = pe.transpose(A[0][:, c * P:(c + 1) * P], ogn[:, c, :], ident)
        last.then_inc(e_["ot"], 1)
        if more:
            turn_m_pe(pe, i + 1)

    def gdn_pe(pe):
        pe.wait_ge(z_["act"], 1)
        pe.wait_ge(z_["dve"], 10)
        for x, e in BLOCKS:
            for part in range(2):
                gdn_block(pe, x, e, 0, part)
        turn_pe(pe, 0)
        for part in range(2):
            gdn_block(pe, 3, 0, 0, part)
        turn_values_pe(pe, 0)
        back_pe(pe, 0)
        gdn_block(pe, 3, 1, 0, 0)
        products_pe(pe, 0)
        gdn_block(pe, 3, 1, 0, 1)
        turn_m_pe(pe, 0)
        over(pe, PAIRS, lambda i: pair_pe(pe, i))

    def pair_act(act, i):
        split = hi_of(act)
        more = not (isinstance(i, int) and i == PAIRS - 1)
        if more:
            block_act(act, split, *BLOCKS[0], i + 1)
            decay_act(act, i + 1)
            for x, e in BLOCKS[1:5]:
                block_act(act, split, x, e, i + 1)
            for e in range(2):
                squares_act(act, i + 1, e)
        act.wait_ge(e_["f1"], i + 1)
        act.activation(vnew[:, 0, :, :], A[0][:, 0:2 * P].rearrange("p (e k) -> p e k", e=2), ACT.Copy)
        act.activation(nwt[:], A[0][:, 2 * P:4 * P].rearrange("p (e k) -> p e k", e=2), ACT.Copy, scale=-1.0).then_inc(e_["f1ev"], 1)
        if more:
            block_mid_act(act, split, *BLOCKS[5], i + 1)
        act.wait_ge(e_["f2"], i + 1)
        act.activation(state[:], A[1][:, 0:2 * P].rearrange("p (e k) -> p e k", e=2), ACT.Copy).then_inc(e_["f2ev"], 1)
        if more:
            block_end_act(act, *BLOCKS[5], i + 1)
            block_act(act, split, 3, 0, i + 1)
        act.wait_ge(e_["f3"], i + 1)
        act.activation(vnew[:, 1, :, :], A[0][:, 0:2 * P].rearrange("p (e k) -> p e k", e=2), ACT.Copy).then_inc(e_["f3ev"], 1)
        if more:
            back_act(act, i + 1)
        act.wait_ge(e_["f4"], i + 1)
        act.activation(junk[:, 0:512], A[1], ACT.Square).then_inc(e_["osq"], 1)
        if more:
            block_act(act, split, 3, 1, i + 1)
            mt_act(act, i + 1)
        act.wait_ge(e_["o32"], i + 1)
        pair = slice(2 * i, 2 * i + 2) if isinstance(i, int) else bass.ds(i * 2, 2)
        act.activation(obh[:, pair, :], og32[:], ACT.Copy).then_inc(e_["oh"], 1)

    def gdn_act(act):
        split = hi_of(act)
        for x, e in BLOCKS:
            block_act(act, split, x, e, 0)
        for e in range(2):
            squares_act(act, 0, e)
        decay_act(act, 0)
        block_act(act, split, 3, 0, 0)
        back_act(act, 0)
        block_act(act, split, 3, 1, 0)
        mt_act(act, 0)
        over(act, PAIRS, lambda i: pair_act(act, i), 2)

    def pair_dve(dve, i):
        more = not (isinstance(i, int) and i == PAIRS - 1)
        if not more:
            split_low(dve, False, ph["att"], 1, 0)
        for l in range(LEVELS):
            for half in range(2):
                (level_xm, level_tt)[half](dve, l, i)
                gap = 2 * l + half - 1
                if more and gap == 0:
                    decay_dve(dve, i + 1)
                if more and gap % 2 and gap > 0:
                    block_dve(dve, *BLOCKS[gap // 2], i + 1)
        if more:
            squares_dve(dve, i + 1)
            block_dve(dve, *BLOCKS[5], i + 1)
            norm_dve(dve, i + 1)
            block_dve(dve, 3, 0, i + 1)
            scaled_dve(dve, i + 1)
        dve.wait_ge(e_["osq"], i + 1)
        chain = Chain(dve, e_["oss"], 1, i)
        chain(dve.tensor_reduce(ssq4[:], junk[:, 0:512].rearrange("p (a k) -> p a k", a=4), AX.X, ALU.add))
        dve.tensor_scalar(mean4[:], ssq4[:], 1.0 / P, EPS, ALU.mult, ALU.add).then_inc(e_["om"], 1)
        dve.wait_ge(e_["oroot"], i + 1)
        dve.tensor_tensor(ogn[:], quad(A[1]), spread(root4[:], P), ALU.mult).then_inc(e_["on"], 1)
        if more:
            masked_dve(dve, i + 1)
        dve.wait_ge(e_["ot"], i + 1)
        if not is0(i):
            dve.wait_ge(e_["oh"], i)
            dve.wait_ge(e_["ol"], i)
        pair = slice(2 * i, 2 * i + 2) if isinstance(i, int) else bass.ds(i * 2, 2)
        dve.scalar_tensor_tensor(og32[:].rearrange("p e k -> p (e k)"), A[0], gdn_gain[:],
                                 z2[:, pair, :].rearrange("p e k -> p (e k)"), ALU.mult, ALU.mult).then_inc(e_["o32"], 1)
        if more:
            block_dve(dve, 3, 1, i + 1)
            init_dve(dve, i + 1)

    def gdn_dve(dve):
        for x, e in BLOCKS:
            block_dve(dve, x, e, 0)
        squares_dve(dve, 0)
        decay_dve(dve, 0)
        norm_dve(dve, 0)
        block_dve(dve, 3, 0, 0)
        scaled_dve(dve, 0)
        block_dve(dve, 3, 1, 0)
        masked_dve(dve, 0)
        init_dve(dve, 0)
        over(dve, PAIRS, lambda i: pair_dve(dve, i), 2)

    def pair_pool(pool, i):
        split = lo_of(pool, True)
        more = not (isinstance(i, int) and i == PAIRS - 1)
        if more:
            for x, e in BLOCKS[:2]:
                refill(split, *source(x, e, i + 1))
            mask_pool(pool, i + 1)
            for x, e in BLOCKS[2:5]:
                refill(split, *source(x, e, i + 1))
            root_pool(pool, i + 1)
            refill(split, *source(*BLOCKS[5], i + 1))
        pool.wait_ge(e_["om"], i + 1)
        pool.tensor_tensor(root4[:], mean4[:], power[:, 0:4], ALU.pow).then_inc(e_["oroot"], 1)
        if more:
            refill(split, *source(3, 0, i + 1))
            init_pool(pool, i + 1)
            grow_pool(pool, i + 1)
            refill(split, *source(3, 1, i + 1))
        pool.wait_ge(e_["oh"], i + 1)
        pair = slice(2 * i, 2 * i + 2) if isinstance(i, int) else bass.ds(i * 2, 2)
        pool.tensor_tensor(obl[:, pair, :], og32[:], obh[:, pair, :], ALU.subtract).then_inc(e_["ol"], 1)

    def gdn_pool(pool):
        split = lo_of(pool, True)
        refill(split, ph["gates"], 4, 0)
        for x, e in BLOCKS:
            refill(split, *source(x, e, 0))
        root_pool(pool, 0)
        mask_pool(pool, 0)
        refill(split, *source(3, 0, 0))
        init_pool(pool, 0)
        grow_pool(pool, 0)
        refill(split, *source(3, 1, 0))
        over(pool, PAIRS, lambda i: pair_pool(pool, i), 2)


    close_scope()
    open_scope()

    t_ = sems("t", "zth zs o")
    oah, oal = sb("oah", [P, HEADS, TOK], F32R), sb("oal", [P, HEADS, TOK], F32R)
    qk_row = sb("qk_row", [P, 4, P])
    att_a, att_b = sb("att_a", [P, 4, ROT]), sb("att_b", [P, 4, ROT])
    qk_col = sb("qk_col", [P, 2, TOK])
    causal_prob = sb("causal_prob", [P, 3 * P])
    causal_t = sb("causal_t", [P, 3 * P])
    zsilu = sb("zsilu", [P, TOK])
    vt_att = sb("vt_att", [P, TOK])
    KEYS = ((0, P), (P, 3 * P))
    B4, B5 = acc[:, 0, :], acc[:, 1, :]

    def att_pe(pe):
        def queries_keys(j):
            if not is0(j):
                pe.wait_ge(h["qkev"], j + ATT_SEEN)
            for t in range(NT):
                for b in range(KB):
                    k = b // 4
                    if t == 0 and b % 4 == 0:
                        chunk_ready(pe, ph["att"], k, j)
                    o = (b % 4) * TOK
                    last = mm3(pe, W[0][:, t * TOK:(t + 1) * TOK], (xh[:, b, t * P:(t + 1) * P], xl[:, b, t * P:(t + 1) * P]),
                               wslot(k, o, o + TOK), b == 0, b == KB - 1)
                    if t == NT - 1 and b % 4 == 3:
                        last.then_inc(used[k], 1)

        def values(j):
            chunk_ready(pe, ph["att"], 2, j)
            if not is0(j):
                pe.wait_ge(h["vev"], j + ATT_SEEN)
            project_t(pe, W[1][:, 0:TOK], 2).then_inc(used[2], 1)

        def turn_values(j):
            pe.wait_ge(d["vtev"], j + 1 + HEADS)
            for t in range(NT):
                last = pe.transpose(W[1][:, t * P:(t + 1) * P], vt_att[:, t * P:(t + 1) * P], ident)
            last.then_inc(d["vt"], 1)

        def turn(j):
            pe.wait_ge(h["roped"], j + 1 + HEADS)
            if not is0(j):
                pe.wait_ge(h["turned_ev"], j)
            for x in range(2):
                for t in range(NT):
                    last = pe.transpose(B4[:, x * TOK + t * P:x * TOK + (t + 1) * P], qk_row[:, 2 * t + x, :], ident)
            last.then_inc(h["turned"], 1)

        def gates(j):
            chunk_ready(pe, ph["att"], 3, j)
            if not is0(j):
                pe.wait_ge(t_["zs"], j)
            project_t(pe, B5[:, 0:TOK], 3).then_inc(used[3], 1)

        def head(i):
            more = not (isinstance(i, int) and i == HEADS - 1)
            pe.wait_ge(h["turned_ev"], i + 1)
            if not is0(i):
                pe.wait_ge(t_["o"], i)
            for t in range(NT):
                a, b = KEYS[t]
                last = pe.matmul(W[2][:, a:b], qk_col[:, 0, t * P:(t + 1) * P], qk_col[:, 1, 0:b - a], start=True, stop=True)
            last.then_inc(h["s"], 1)
            if more:
                queries_keys(i + 1)
            pe.wait_ge(h["p"], i + 1 + ATT_SEEN)
            for c in range(3):
                last = pe.transpose(W[3][:, c * P:(c + 1) * P], causal_prob[:, c * P:(c + 1) * P], ident)
            last.then_inc(h["pt"], 1)
            if more:
                values(i + 1)
                turn(i + 1)
            pe.wait_ge(h["ptev"], i + 1 + ATT_SEEN)
            pe.wait_ge(h["vev"], i + 1 + ATT_SEEN)
            pe.matmul(W[2][:, 0:TOK], v_sb[:, 0, :], causal_t[:, 0:TOK], start=True, stop=False)
            pe.matmul(W[2][:, P:TOK], v_sb[:, 1, :], causal_t[:, TOK:3 * P], start=False, stop=True).then_inc(h["pv"], 1)
            if more:
                gates(i + 1)
                turn_values(i + 1)

        turn(0)
        turn_values(0)
        gates(0)
        over(pe, HEADS, head)

    def att_act(act):
        split = hi_of(act)

        def take_qk(j):
            act.wait_ge(used[1], ph["att"].base[1] + j + 1)
            act.activation(qk_row[:].rearrange("p a k -> p (a k)"), W[0][:], ACT.Copy).then_inc(h["qkev"], 1)

        def take_turned(j):
            act.wait_ge(h["turned"], j + 1)
            act.activation(qk_col[:].rearrange("p a k -> p (a k)"), B4, ACT.Copy).then_inc(h["turned_ev"], 1)

        def take_values(j):
            act.wait_ge(used[2], ph["att"].base[2] + j + 1)
            act.activation(vt_att[:], W[1][:, 0:TOK], ACT.Copy).then_inc(d["vtev"], 1)

        def gate_tanh(j):
            act.wait_ge(used[3], ph["att"].base[3] + j + 1)
            if not is0(j):
                act.wait_ge(t_["zs"], j)
            act.activation(tanh_[3][:], B5[:, 0:TOK], ACT.Tanh, scale=0.5).then_inc(t_["zth"], 1)

        def head(i):
            more = not (isinstance(i, int) and i == HEADS - 1)
            if not more:
                first_of_next(split, ph["att"])
            act.wait_ge(h["mx"], i + 1 + ATT_SEEN)
            for t in range(NT):
                a, b = KEYS[t]
                last = act.activation(causal_prob[:, a:b], causal_prob[:, a:b], ACT.Exp, bias=soft[:, 4 + t:5 + t],
                                      scale=ATT_SCALE, accum_out=soft[:, 8 + t:9 + t])
            last.then_inc(h["e"], 1)
            if more:
                take_qk(i + 1)
                refill(split, ph["att"], 0, i + 1)
            act.wait_ge(h["pt"], i + 1 + ATT_SEEN)
            act.activation(causal_t[:], W[3][:, 0:3 * P], ACT.Copy).then_inc(h["ptev"], 1)
            if more:
                refill(split, ph["att"], 1, i + 1)
                take_turned(i + 1)
                take_values(i + 1)
                refill(split, ph["att"], 2, i + 1)
            act.wait_ge(t_["o"], i + 1)
            at = slice(i, i + 1) if isinstance(i, int) else bass.ds(i, 1)
            act.activation(oah[:, at, :].rearrange("p a k -> p (a k)"), o32[:], ACT.Copy).then_inc(h["oh"], 1)
            if more:
                gate_tanh(i + 1)
                refill(split, ph["att"], 3, i + 1)

        take_qk(0)
        refill(split, ph["att"], 0, 0)
        refill(split, ph["att"], 1, 0)
        take_values(0)
        refill(split, ph["att"], 2, 0)
        take_turned(0)
        gate_tanh(0)
        refill(split, ph["att"], 3, 0)
        over(act, HEADS, head, 2)

    def att_dve(dve):
        split = lo_of(dve)
        cos = cst("att_cos", "p (a r) -> p a r", a=4)
        sin = cst("att_sin", "p (a r) -> p a r", a=4)

        def rotate_rows(j):
            dve.wait_ge(h["qkev"], j + 1 + ATT_SEEN)
            rotate(dve, Chain(dve, h["rope"], 1, j), qk_row[:, :, 0:ROT], qk_row[:, :, 0:ROT], cos, sin, ROT // 2,
                   att_a, att_b).then_inc(h["roped"], 1)

        def take_values(j):
            dve.wait_ge(d["vt"], j + 1 + HEADS)
            if not is0(j):
                dve.wait_ge(h["pv"], j + ATT_SEEN)
            dve.tensor_copy(v_sb[:], W[1][:, 0:TOK].rearrange("p (t c) -> p t c", t=NT)).then_inc(h["vev"], 1)

        def gate_silu(j):
            dve.wait_ge(t_["zth"], j + 1)
            dve.scalar_tensor_tensor(zsilu[:], tanh_[3][:], 1.0, B5[:, 0:TOK], ALU.add, ALU.mult).then_inc(t_["zs"], 1)

        def head(i):
            more = not (isinstance(i, int) and i == HEADS - 1)
            if not more:
                first_of_next(split, ph["att"])
            chain = Chain(dve, h["sm"], 3, i, 7 * HEADS)
            dve.wait_ge(h["s"], i + 1 + ATT_SEEN)
            chain(dve.tensor_tensor(causal_prob[:], W[2][:, 0:3 * P], cst("causal"), ALU.add))
            for t in range(NT):
                a, b = KEYS[t]
                last = dve.tensor_reduce(soft[:, t:t + 1], causal_prob[:, a:b], AX.X, ALU.max)
            chain(last)
            dve.tensor_scalar(soft[:, 4:6], soft[:, 0:2], -ATT_SCALE, None, ALU.mult).then_inc(h["mx"], 1)
            dve.wait_ge(h["e"], i + 1 + ATT_SEEN)
            chain(dve.reciprocal(soft[:, 12:14], soft[:, 8:10]))
            for t in range(NT):
                a, b = KEYS[t]
                last = dve.tensor_scalar(causal_prob[:, a:b], causal_prob[:, a:b], soft[:, 12 + t:13 + t], None, ALU.mult)
            last.then_inc(h["p"], 1)
            if more:
                rotate_rows(i + 1)
                refill(split, ph["att"], 0, i + 1)
                refill(split, ph["att"], 1, i + 1)
                refill(split, ph["att"], 2, i + 1)
            dve.wait_ge(h["pv"], i + 1 + ATT_SEEN)
            dve.wait_ge(t_["zs"], i + 1)
            if not is0(i):
                dve.wait_ge(h["oh"], i + ATT_SEEN)
                dve.wait_ge(h["ol"], i + ATT_SEEN)
            dve.scalar_tensor_tensor(o32[:], W[2][:, 0:TOK], 0.5, zsilu[:], ALU.mult, ALU.mult).then_inc(t_["o"], 1)
            if more:
                gate_silu(i + 1)
                take_values(i + 1)
                refill(split, ph["att"], 3, i + 1)

        rotate_rows(0)
        for k in range(2):
            refill(split, ph["att"], k, 0)
        take_values(0)
        refill(split, ph["att"], 2, 0)
        gate_silu(0)
        refill(split, ph["att"], 3, 0)
        over(dve, HEADS, head, 2)

    def att_pool(pool):
        split = lo_of(pool, True)

        def head(i):
            more = not (isinstance(i, int) and i == HEADS - 1)
            if more:
                for k in range(3):
                    refill(split, ph["att"], k, i + 1)
            else:
                first_of_next(split, ph["att"])
            pool.wait_ge(h["oh"], i + 1 + ATT_SEEN)
            at = slice(i, i + 1) if isinstance(i, int) else bass.ds(i, 1)
            pool.tensor_tensor(oal[:, at, :].rearrange("p a k -> p (a k)"), o32[:],
                               oah[:, at, :].rearrange("p a k -> p (a k)"), ALU.subtract).then_inc(h["ol"], 1)
            if more:
                refill(split, ph["att"], 3, i + 1)

        for k in range(4):
            refill(split, ph["att"], k, 0)
        over(pool, HEADS, head, 2)

    r_ = dict(tha=f[0]["g_mid"], thb=f[0]["v_mid"], mh=f[0]["hh"], ma=f[0]["g_tap"], mb=f[0]["v_tap"],
              sum=f[1]["g_tap"], ml=f[1]["v_tap"])
    ACT_SEEN, DVE_SEEN = 2 * FFN_STEPS, 4 * FFN_STEPS
    tha, thb = sb("tha", [P, TOK]), sb("thb", [P, TOK])
    mga, mgb = sb("mga", [P, TOK]), sb("mgb", [P, TOK])
    mg = sb("mg", [P, TOK])
    mgh, mgl = sb("mgh", [P, TOK], F32R), sb("mgl", [P, TOK], F32R)

    def out_pe(pe):
        def add_output(i, start=False, stop=False):
            chunk_ready(pe, ph["out"], 4, i)
            pe.wait_ge(r_["ml"], i + 1 + DVE_SEEN)
            rows_out(pe, 4, mgh, mgl, start, stop).then_inc(used[4], 1)

        def group(i):
            for k, x, freed in ((0, (xh, xl), (r_["tha"], ACT_SEEN)), (1, (xh, xl), (r_["thb"], ACT_SEEN)),
                                (2, (oah, oal), (r_["ma"], DVE_SEEN)), (3, (obh, obl), (r_["mb"], DVE_SEEN))):
                chunk_ready(pe, ph["out"], k, i)
                if not is0(i):
                    pe.wait_ge(freed[0], i + freed[1])
                project_t(pe, W[k][:, 0:TOK], k, x=x).then_inc(used[k], 1)
                if k == 1 and not is0(i):
                    add_output(i - 1, start=isinstance(i, int) and i == 1)

        pe.wait_ge(h["ol"], HEADS + ATT_SEEN)
        pe.wait_ge(t_["zs"], HEADS)
        pe.wait_ge(e_["ol"], PAIRS)
        group(0)
        group(1)
        with pe.Fori(2, HEADS) as r:
            group(pe.snap(r))
        add_output(HEADS - 1, stop=True)

    def out_act(act):
        split = hi_of(act)

        def group(i):
            for k, (s, th) in enumerate(((r_["tha"], tha), (r_["thb"], thb))):
                act.wait_ge(used[k], ph["out"].base[k] + i + 1)
                if not is0(i):
                    act.wait_ge((r_["ma"], r_["mb"])[k], i + DVE_SEEN)
                act.activation(th[:], W[k][:, 0:TOK], ACT.Tanh, scale=0.5).then_inc(s, 1)
                refill(split, ph["out"], k, i)
            if not is0(i):
                refill(split, ph["out"], 4, i - 1)
            refill(split, ph["out"], 2, i)
            act.wait_ge(r_["sum"], i + 1 + DVE_SEEN)
            if not is0(i):
                act.wait_ge(used[4], ph["out"].base[4] + i)
            act.activation(mgh[:], mg[:], ACT.Copy, scale=0.5).then_inc(r_["mh"], 1)
            refill(split, ph["out"], 3, i)

        over(act, HEADS, group)

    def out_dve(dve):
        split = lo_of(dve)

        def group(i):
            refill(split, ph["out"], 0, i)
            refill(split, ph["out"], 1, i)
            if not is0(i):
                refill(split, ph["out"], 4, i - 1)
            for k, (s, th, out, ready) in enumerate(((r_["ma"], tha, mga, r_["tha"]), (r_["mb"], thb, mgb, r_["thb"]))):
                dve.wait_ge(ready, i + 1 + ACT_SEEN)
                dve.wait_ge(used[2 + k], ph["out"].base[2 + k] + i + 1)
                dve.scalar_tensor_tensor(out[:], th[:], 1.0, W[2 + k][:, 0:TOK], ALU.add, ALU.mult).then_inc(s, 1)
            dve.wait_ge(r_["mb"], i + 1 + DVE_SEEN)
            if not is0(i):
                dve.wait_ge(r_["mh"], i + ACT_SEEN)
            dve.tensor_tensor(mg[:], mga[:], mgb[:], ALU.add).then_inc(r_["sum"], 1)
            dve.wait_ge(r_["mh"], i + 1 + ACT_SEEN)
            dve.scalar_tensor_tensor(mgl[:], mg[:], 0.5, mgh[:], ALU.mult, ALU.subtract).then_inc(r_["ml"], 1)
            refill(split, ph["out"], 2, i)
            refill(split, ph["out"], 3, i)

        over(dve, HEADS, group)

    def out_pool(pool):
        split = lo_of(pool, True)

        def group(i):
            refill(split, ph["out"], 0, i)
            refill(split, ph["out"], 1, i)
            if not is0(i):
                refill(split, ph["out"], 4, i - 1)
            refill(split, ph["out"], 2, i)
            refill(split, ph["out"], 3, i)

        over(pool, HEADS, group)

    stored = sem("stored")
    ready = sems("s", "power")
    block = ctx.enter_context(nc.Block())

    @block.sync
    def _(sp):
        start_sp(sp)
        loaded = set()

        def load_first(p, k):
            if (p.name, k) not in loaded:
                load(sp, p, k, 0)
                loaded.add((p.name, k))

        def load_next(p, mine):
            for k in range(6):
                for q in [q for q in p.after if k in q.widths][:1]:
                    if (k in p.widths) == mine and k not in p.lagging:
                        load_first(q, k)

        def load_loop(p):
            for k in p.widths:
                load_first(p, k)
            if p.name == "down_a":
                start_later_sp(sp)
            load_next(p, False)
            if p.count == 1:
                return
            late = p.count == HEADS
            prompt = [k for k in p.widths if k not in p.lagging]
            for k in prompt:
                load(sp, p, k, 1)
            with sp.Fori(2, p.count) as r:
                i = sp.snap(r)
                order = [*prompt, *p.lagging] if late else [*prompt[:2], *p.lagging, *prompt[2:]]
                for k in order:
                    load(sp, p, k, i - 1 if k in p.lagging else i)
            if p.lagging and late:
                load_next(p, True)
            for k in p.lagging:
                load(sp, p, k, p.count - 1)
            if p.lagging and not late:
                load_next(p, True)

        def load_pairs(p, pz):
            for q in (p, pz):
                for k in q.widths:
                    load_first(q, k)
            for k in p.widths:
                load(sp, p, k, 1)
            with sp.Fori(1, PAIRS) as r:
                i = sp.snap(r)
                for k in p.widths:
                    load(sp, p, k, i * 2)
                for k in pz.widths:
                    load(sp, pz, k, i)
                for k in p.widths:
                    load(sp, p, k, i * 2 + 1)

        for p in ph.values():
            if p.name == "gdn":
                load_pairs(p, ph["gdnz"])
            elif p.name != "gdnz":
                load_loop(p)
        for t in range(NT):
            sp.wait_ge(n_["hid"], 8 + t + 1)
            sp.dma_start(y_out[t * P:(t + 1) * P, :], hid[:, t, :]).then_inc(stored, 16)
        sp.wait_ge(stored, 16 * NT)

    @block.tensor
    def _(pe):
        pe.wait_ge(g["tables"], 32)
        pre_pe(pe, 0)
        down_pe(pe)
        mla_pe(pe)
        pre_pe(pe, 1)
        ffn_pe(pe, 0)
        pre_pe(pe, 2)
        diff_pe(pe)
        pre_pe(pe, 3)
        ffn_pe(pe, 1)
        pre_pe(pe, 4)
        pe.wait_ge(g["const"], 32)
        gates_pe(pe)
        gdn_pe(pe)
        att_pe(pe)
        out_pe(pe)

    @block.scalar
    def _(act):
        pre_act(act, 0)
        for k in range(2):
            split_high(act, ph["down_a"], k, 0)
        act.wait_ge(g["tables"], 32)
        pre_act_split(act, 0)
        for k in range(2, 6):
            split_high(act, ph["down_a"], k, 0)
        down_act(act)
        mla_act(act)
        post_act(act, 0, ph["mla"], 2)
        pre_act(act, 1)
        pre_act_split(act, 1)
        first_of_next(hi_of(act), ph["mla"])
        refill(hi_of(act), ph["mla"], 2, HEADS - 1)
        act.wait_ge(g["const"], 32)
        ffn_act(act, 0)
        post_act(act, 1, ph["ffn0"], 5)
        pre_act(act, 2)
        pre_act_split(act, 2)
        diff_setup_act(act)
        diff_act(act)
        post_act(act, 2, ph["diff"], 3)
        pre_act(act, 3)
        pre_act_split(act, 3)
        refill(hi_of(act), ph["diff"], 3, HEADS - 1)
        ffn_act(act, 1)
        post_act(act, 3, ph["ffn1"], 5)
        pre_act(act, 4)
        pre_act_split(act, 4)
        gates_act(act)
        gdn_act(act)
        att_act(act)
        out_act(act)
        post_act(act, 4, ph["out"], 4)

    @block.vector
    def _(dve):
        dve.memset(power[:], -0.5).then_inc(ready["power"], 1)
        dve.wait_ge(g["x"], 16)
        pre_dve(dve, 0)
        for k in range(2):
            split_low(dve, False, ph["down_a"], k, 0)
        dve.wait_ge(g["tables"], 32)
        pre_dve_split(dve, 0)
        for k in range(2, 6):
            split_low(dve, False, ph["down_a"], k, 0)
        dve.wait_ge(g["const"], 32)
        down_dve(dve)
        mla_dve(dve)
        post_dve(dve, 0, ph["mla"], 2)
        pre_dve(dve, 1)
        pre_dve_split(dve, 1)
        first_of_next(lo_of(dve), ph["mla"])
        refill(lo_of(dve), ph["mla"], 2, HEADS - 1)
        ffn_dve(dve, 0)
        post_dve(dve, 1, ph["ffn0"], 5)
        pre_dve(dve, 2)
        pre_dve_split(dve, 2)
        diff_setup_dve(dve)
        diff_dve(dve)
        post_dve(dve, 2, ph["diff"], 3)
        pre_dve(dve, 3)
        pre_dve_split(dve, 3)
        refill(lo_of(dve), ph["diff"], 3, HEADS - 1)
        ffn_dve(dve, 1)
        post_dve(dve, 3, ph["ffn1"], 5)
        pre_dve(dve, 4)
        pre_dve_split(dve, 4)
        gates_dve(dve)
        gdn_dve(dve)
        att_dve(dve)
        out_dve(dve)
        post_dve(dve, 4, ph["out"], 4)

    @block.gpsimd
    def _(pool):
        start_pool(pool)
        pool.wait_ge(ready["power"], 1)
        pre_pool(pool, 0)
        down_pool(pool)
        post_pool(pool, 0)
        pre_pool(pool, 1)
        first_of_next(lo_of(pool, True), ph["mla"])
        ffn_pool(pool, 0)
        post_pool(pool, 1)
        pre_pool(pool, 2)
        diff_pool(pool)
        post_pool(pool, 2)
        pre_pool(pool, 3)
        refill(lo_of(pool, True), ph["diff"], 3, HEADS - 1)
        ffn_pool(pool, 1)
        post_pool(pool, 3)
        pre_pool(pool, 4)
        pool.wait_ge(g["const"], 32)
        gdn_pool(pool)
        att_pool(pool)
        out_pool(pool)
        post_pool(pool, 4)

    close_scope()
    ctx.close()


def kernel(**inputs):
    import concourse.bacc as bacc
    from concourse.bass_utils import run_bass_kernel_spmd

    arrays = {f"in_{n}": a for n, a in lay_out(inputs).items()}
    nc = bacc.Bacc("TRN2", target_bir_lowering=False, num_devices=1)
    dram = {n[3:]: nc.dram_tensor(n, a.shape, F32, kind="ExternalInput").ap() for n, a in arrays.items()}
    out = nc.dram_tensor("out", (TOK, D), F32, kind="ExternalOutput").ap()
    build(nc, dram, out)
    result = run_bass_kernel_spmd(nc, [arrays], core_ids=[0])
    return result.results[0]["out"].reshape(1, TOK, D)
```
